# Optimizing a Trainium2 kernel written in Bass

```python
import math
import jax, jax.numpy as jnp
from jax import lax
import numpy as np

D_MODEL = 1024
BATCH = 1
SEQ = 256
DEPTH = 2

SSM_GROUP = 16
SSM_GROUPS = 40
SSM_WIDTH = SSM_GROUP * SSM_GROUPS
SSM_STATE = 64
ATT_HEADS = 6
ATT_HEAD_DIM = 64
ATT_WIDTH = ATT_HEADS * ATT_HEAD_DIM
MIX_IN_EVEN = SSM_WIDTH + 3 * ATT_WIDTH
MIX_OUT_EVEN = SSM_WIDTH + ATT_WIDTH
DILATED_PATTERNS = ((128, 1), (512, 4), (2048, 16))
ATT_BLK = 128
CONV_WIDTH = D_MODEL
CONV_TAPS = 3
N_GROUPS = 4
EXPERTS_PER_GROUP = 8
N_EXPERTS = N_GROUPS * EXPERTS_PER_GROUP
TOP_K_IN_GROUP = 2
D_EXPERT = 512
MOE_BLK = 256

RMS_EPS = 1e-6
NEG_INF = -1e30
N_EVEN = (DEPTH + 1) // 2
N_ODD = DEPTH // 2

kernel_name = 'hybrid_s5_dilated_attn_shortconv_hier_moe'

def rms_norm(x, g):
    x32 = x.astype(jnp.float32)
    y = x32 * lax.rsqrt(jnp.mean(x32 * x32, axis=-1, keepdims=True) + RMS_EPS)
    return (y * g.astype(jnp.float32)).astype(x.dtype)

def alibi_slopes(n_heads):
    return jnp.asarray([2.0 ** (-8.0 * (h + 1) / n_heads) for h in range(n_heads)], jnp.float32)

def _ssm_combine(e1, e2):
    a1, b1 = e1
    a2, b2 = e2
    return a1 * a2, a2 * b1 + b2

def s5_mixer(u, a_re, a_im, b_re, b_im, c_re, c_im, d_skip, log_step, w_glu, b_glu):
    bsz, s_len, _ = u.shape
    f32 = jnp.float32
    u32 = u.astype(f32).reshape(bsz, s_len, SSM_GROUPS, SSM_GROUP)
    lam = lax.complex(a_re.astype(f32), a_im.astype(f32))
    step = jnp.exp(log_step.astype(f32))[:, None]
    lam_bar = jnp.exp(lam * step)
    b_bar = ((lam_bar - 1.0) / lam)[..., None] * lax.complex(b_re.astype(f32), b_im.astype(f32))
    bu = jnp.einsum('bsgh,gph->bsgp', u32.astype(jnp.complex64), b_bar)
    a = jnp.broadcast_to(lam_bar, (1, s_len) + lam_bar.shape)
    _, states = lax.associative_scan(_ssm_combine, (a, bu), axis=1)
    c = lax.complex(c_re.astype(f32), c_im.astype(f32))
    y = jnp.einsum('bsgp,ghp->bsgh', states, c).real + d_skip.astype(f32).reshape(SSM_GROUPS, SSM_GROUP) * u32
    y = jax.nn.gelu(y.reshape(bsz, s_len, SSM_WIDTH))
    y = y * jax.nn.sigmoid(y @ w_glu.astype(f32) + b_glu.astype(f32))
    return y.astype(u.dtype)

def _to_sub(t, s_pad, dil):
    bsz, s_len, nh, e = t.shape
    t = jnp.pad(t, ((0, 0), (0, s_pad - s_len), (0, 0), (0, 0)))
    return t.reshape(bsz, s_pad // dil, dil, nh, e).transpose(0, 2, 3, 1, 4)

def _from_sub(t, s_len):
    bsz, dil, nh = t.shape[:3]
    rest = t.shape[5:]
    t = t.reshape((bsz, dil, nh, -1) + rest)
    perm = (0, 3, 1, 2) + tuple(range(4, 4 + len(rest)))
    t = t.transpose(perm)
    return t.reshape((bsz, -1, nh) + rest)[:, :s_len]

def dilated_branch(q, k, v, slopes, window, dil):
    bsz, s_len, nh, dh = q.shape
    steps = window // dil
    sub_len = -(-s_len // dil)
    sub_pad = -(-sub_len // ATT_BLK) * ATT_BLK
    s_pad = sub_pad * dil
    nb = sub_pad // ATT_BLK
    qb = _to_sub(q, s_pad, dil).reshape(bsz, dil, nh, nb, ATT_BLK, dh)

    def kv_blocks(t):
        t = jnp.pad(_to_sub(t, s_pad, dil), ((0, 0), (0, 0), (0, 0), (ATT_BLK, 0), (0, 0)))
        t = t.reshape(bsz, dil, nh, nb + 1, ATT_BLK, dh)
        return jnp.concatenate([t[:, :, :, :-1], t[:, :, :, 1:]], axis=4)

    kb, vb = kv_blocks(k), kv_blocks(v)
    s = jnp.einsum('bdhnqe,bdhnke->bdhnqk', qb, kb, preferred_element_type=jnp.float32)
    qi = jnp.arange(ATT_BLK)[:, None]
    kj = jnp.arange(2 * ATT_BLK)[None, :]
    diff = qi + ATT_BLK - kj
    blk_start = (jnp.arange(nb) * ATT_BLK)[:, None, None]
    valid = (diff >= 0) & (diff <= steps) & (blk_start + kj - ATT_BLK >= 0)
    dist = (diff * dil).astype(jnp.float32)
    bias = -slopes[:, None, None, None] * dist[None, None]
    s = jnp.where(valid, s + bias, NEG_INF)
    m = jnp.max(s, axis=-1, keepdims=True)
    p = jnp.where(valid, jnp.exp(s - m), 0.0)
    l = jnp.sum(p, axis=-1)
    o = jnp.einsum('bdhnqk,bdhnke->bdhnqe', p, vb.astype(jnp.float32)) / l[..., None]
    return _from_sub(o, s_len), _from_sub(m[..., 0], s_len), _from_sub(l, s_len)

def dilated_attention(q, k, v):
    slopes = alibi_slopes(ATT_HEADS)
    res = [dilated_branch(q, k, v, slopes, w, d) for (w, d) in DILATED_PATTERNS]
    o_all = jnp.stack([r[0] for r in res])
    m_all = jnp.stack([r[1] for r in res])
    l_all = jnp.stack([r[2] for r in res])
    wts = l_all * jnp.exp(m_all - jnp.max(m_all, axis=0, keepdims=True))
    out = jnp.sum(wts[..., None] * o_all, axis=0) / jnp.sum(wts, axis=0)[..., None]
    return out.astype(q.dtype)

def even_mixer(h, w_in, a_re, a_im, b_re, b_im, c_re, c_im, d_skip, log_step, w_glu, b_glu, q_norm, k_norm, w_out):
    bsz, s_len, _ = h.shape
    proj = h @ w_in
    u = proj[..., :SSM_WIDTH]
    q = proj[..., SSM_WIDTH:SSM_WIDTH + ATT_WIDTH].reshape(bsz, s_len, ATT_HEADS, ATT_HEAD_DIM)
    k = proj[..., SSM_WIDTH + ATT_WIDTH:SSM_WIDTH + 2 * ATT_WIDTH].reshape(bsz, s_len, ATT_HEADS, ATT_HEAD_DIM)
    v = proj[..., SSM_WIDTH + 2 * ATT_WIDTH:].reshape(bsz, s_len, ATT_HEADS, ATT_HEAD_DIM)
    q = rms_norm(q, q_norm) * (ATT_HEAD_DIM ** -0.5)
    k = rms_norm(k, k_norm)
    attn = dilated_attention(q, k, v).reshape(bsz, s_len, ATT_WIDTH)
    ssm = s5_mixer(u, a_re, a_im, b_re, b_im, c_re, c_im, d_skip, log_step, w_glu, b_glu)
    return jnp.concatenate([ssm, attn], axis=-1) @ w_out

def conv_mixer(h, w_in, conv_w, w_out):
    proj = h @ w_in
    b_gate = proj[..., :CONV_WIDTH]
    c_gate = proj[..., CONV_WIDTH:2 * CONV_WIDTH]
    z = proj[..., 2 * CONV_WIDTH:]
    zc = c_gate * z
    zc = lax.conv_general_dilated(zc, conv_w.astype(zc.dtype)[:, None, :], window_strides=(1,),
                                  padding=((CONV_TAPS - 1, 0),), dimension_numbers=('NWC', 'WIO', 'NWC'),
                                  feature_group_count=CONV_WIDTH)
    return (b_gate * zc) @ w_out

def hier_moe(h, w_rg, b_rg, w_re, b_re, w_g, w_u, w_d):
    bsz, s_len, d = h.shape
    n_tok = bsz * s_len
    f32 = jnp.float32
    x2 = h.reshape(n_tok, d)
    g_prob = jax.nn.softmax((x2 @ w_rg).astype(f32) + b_rg.astype(f32), axis=-1)
    g_w, grp = lax.top_k(g_prob, 1)
    grp = grp[:, 0]
    e_logits = ((x2 @ w_re).astype(f32) + b_re.astype(f32)).reshape(n_tok, N_GROUPS, EXPERTS_PER_GROUP)
    e_logits = jnp.take_along_axis(e_logits, grp[:, None, None], axis=1)[:, 0]
    top_p, top_i = lax.top_k(jax.nn.softmax(e_logits, axis=-1), TOP_K_IN_GROUP)
    gate = g_w * top_p / jnp.sum(top_p, axis=-1, keepdims=True)
    expert = grp[:, None] * EXPERTS_PER_GROUP + top_i

    n = n_tok * TOP_K_IN_GROUP
    e_flat = expert.reshape(n).astype(jnp.int32)
    t_flat = jnp.repeat(jnp.arange(n_tok, dtype=jnp.int32), TOP_K_IN_GROUP)
    w_flat = gate.reshape(n)
    order = jnp.argsort(e_flat)
    e_s, t_s, w_s = e_flat[order], t_flat[order], w_flat[order]
    counts = jnp.bincount(e_flat, length=N_EXPERTS)
    starts = jnp.cumsum(counts) - counts
    padded = (counts + MOE_BLK - 1) // MOE_BLK * MOE_BLK
    pends = jnp.cumsum(padded)
    pstarts = pends - padded
    dest = pstarts[e_s] + jnp.arange(n, dtype=jnp.int32) - starts[e_s]
    n_rows = (-(-n // MOE_BLK) + N_EXPERTS) * MOE_BLK
    n_blocks = n_rows // MOE_BLK
    row_tok = jnp.full((n_rows,), n_tok, jnp.int32).at[dest].set(t_s)
    row_w = jnp.zeros((n_rows,), f32).at[dest].set(w_s)
    blk_e = jnp.minimum(jnp.searchsorted(pends, jnp.arange(n_blocks, dtype=jnp.int32) * MOE_BLK, side='right'),
                        N_EXPERTS - 1)
    x_pad = jnp.concatenate([x2, jnp.zeros((1, d), x2.dtype)], axis=0)

    def expert_block(args):
        tok, e = args
        xb = x_pad[tok]
        hb = jax.nn.silu(xb @ w_g[e]) * (xb @ w_u[e])
        return hb @ w_d[e]

    y_rows = lax.map(expert_block, (row_tok.reshape(n_blocks, MOE_BLK), blk_e))
    y = jax.ops.segment_sum(y_rows.reshape(n_rows, d).astype(f32) * row_w[:, None], row_tok,
                            num_segments=n_tok + 1)[:n_tok]
    return y.astype(h.dtype).reshape(bsz, s_len, d)

def setup_inputs(seed: int = 0) -> dict:
    key = jax.random.key(seed)
    ks = jax.random.split(key, 32)
    f32 = jnp.float32
    nrm = lambda k, shape, scale: jax.random.normal(k, shape, f32) * scale
    d = D_MODEL
    a_im_base = jnp.pi * jnp.arange(SSM_STATE, dtype=f32)
    return {
        'x': nrm(ks[0], (BATCH, SEQ, d), 1.0),
        'norm_mix': 1.0 + nrm(ks[1], (DEPTH, d), 0.02),
        'norm_ffn': 1.0 + nrm(ks[2], (DEPTH, d), 0.02),
        'w_in_even': nrm(ks[3], (N_EVEN, d, MIX_IN_EVEN), d ** -0.5),
        'ssm_a_re': -0.5 + nrm(ks[4], (N_EVEN, SSM_GROUPS, SSM_STATE), 0.01),
        'ssm_a_im': a_im_base + nrm(ks[5], (N_EVEN, SSM_GROUPS, SSM_STATE), 0.01),
        'ssm_b_re': nrm(ks[6], (N_EVEN, SSM_GROUPS, SSM_STATE, SSM_GROUP), (2 * SSM_GROUP) ** -0.5),
        'ssm_b_im': nrm(ks[7], (N_EVEN, SSM_GROUPS, SSM_STATE, SSM_GROUP), (2 * SSM_GROUP) ** -0.5),
        'ssm_c_re': nrm(ks[8], (N_EVEN, SSM_GROUPS, SSM_GROUP, SSM_STATE), SSM_STATE ** -0.5),
        'ssm_c_im': nrm(ks[9], (N_EVEN, SSM_GROUPS, SSM_GROUP, SSM_STATE), SSM_STATE ** -0.5),
        'ssm_d': nrm(ks[10], (N_EVEN, SSM_WIDTH), 1.0),
        'ssm_log_step': jax.random.uniform(ks[11], (N_EVEN, SSM_GROUPS), f32, math.log(1e-3), math.log(1e-1)),
        'w_glu': nrm(ks[12], (N_EVEN, SSM_WIDTH, SSM_WIDTH), SSM_WIDTH ** -0.5),
        'b_glu': nrm(ks[13], (N_EVEN, SSM_WIDTH), 0.01),
        'q_norm': 1.0 + nrm(ks[14], (N_EVEN, ATT_HEAD_DIM), 0.02),
        'k_norm': 1.0 + nrm(ks[15], (N_EVEN, ATT_HEAD_DIM), 0.02),
        'w_out_even': nrm(ks[16], (N_EVEN, MIX_OUT_EVEN, d), MIX_OUT_EVEN ** -0.5),
        'w_in_conv': nrm(ks[17], (N_ODD, d, 3 * CONV_WIDTH), d ** -0.5),
        'conv_w': nrm(ks[18], (N_ODD, CONV_TAPS, CONV_WIDTH), CONV_TAPS ** -0.5),
        'w_out_conv': nrm(ks[19], (N_ODD, CONV_WIDTH, d), CONV_WIDTH ** -0.5),
        'w_router_group': nrm(ks[20], (DEPTH, d, N_GROUPS), d ** -0.5),
        'b_router_group': nrm(ks[21], (DEPTH, N_GROUPS), 0.01),
        'w_router_expert': nrm(ks[22], (DEPTH, d, N_EXPERTS), d ** -0.5),
        'b_router_expert': nrm(ks[23], (DEPTH, N_EXPERTS), 0.01),
        'w_expert_gate': nrm(ks[24], (DEPTH, N_EXPERTS, d, D_EXPERT), d ** -0.5),
        'w_expert_up': nrm(ks[25], (DEPTH, N_EXPERTS, d, D_EXPERT), d ** -0.5),
        'w_expert_down': nrm(ks[26], (DEPTH, N_EXPERTS, D_EXPERT, d), D_EXPERT ** -0.5),
    }

def reference(x, norm_mix, norm_ffn, w_in_even, ssm_a_re, ssm_a_im, ssm_b_re, ssm_b_im, ssm_c_re, ssm_c_im,
              ssm_d, ssm_log_step, w_glu, b_glu, q_norm, k_norm, w_out_even, w_in_conv, conv_w, w_out_conv,
              w_router_group, b_router_group, w_router_expert, b_router_expert, w_expert_gate, w_expert_up,
              w_expert_down):
    h = x
    for layer in range(DEPTH):
        hn = rms_norm(h, norm_mix[layer])
        i = layer // 2
        if layer % 2 == 0:
            mix = even_mixer(hn, w_in_even[i], ssm_a_re[i], ssm_a_im[i], ssm_b_re[i], ssm_b_im[i], ssm_c_re[i],
                             ssm_c_im[i], ssm_d[i], ssm_log_step[i], w_glu[i], b_glu[i], q_norm[i], k_norm[i],
                             w_out_even[i])
        else:
            mix = conv_mixer(hn, w_in_conv[i], conv_w[i], w_out_conv[i])
        h = h + mix
        h = h + hier_moe(rms_norm(h, norm_ffn[layer]), w_router_group[layer], b_router_group[layer],
                         w_router_expert[layer], b_router_expert[layer], w_expert_gate[layer],
                         w_expert_up[layer], w_expert_down[layer])
    return h


_drawn_inputs = setup_inputs


def setup_inputs(seed=0):
    import zlib

    import numpy as np

    out = dict(_drawn_inputs(seed))
    spreads = {}
    factors = {'ssm_a_re': 64.0,
     'b_glu': 8.0,
     'k_norm': 2.886,
     'b_router_group': 8.0,
     'b_router_expert': 2.707,
     'ssm_b_re': 4.422,
     'ssm_c_im': 3.228}
    for name, (base, spread) in spreads.items():
        noise = np.random.default_rng([zlib.crc32(name.encode()), seed]).standard_normal(out[name].shape)
        drawn = base * np.exp(spread * noise) if base else spread * noise
        out[name] = __import__('jax').numpy.asarray(drawn.astype(out[name].dtype))
    for name, factor in factors.items():
        out[name] = (out[name] * factor).astype(out[name].dtype)
    return out
```

```python
from contextlib import ExitStack
import math

import concourse.bass as bass
from concourse import mybir

F32 = mybir.dt.float32
I32 = mybir.dt.int32
U32 = mybir.dt.uint32
ACT = mybir.ActivationFunctionType
ALU = mybir.AluOpType
AX = mybir.AxisListType

P = 128
SEQ = 256
D = 1024
NT = SEQ // P
KD = D // P
LAYERS = 2
SSM_W, PAIRS, CHW = 640, 20, 5
HEADS, HD, ATT_W = 6, 64, 384
QCH = ATT_W // P
EPS = 1e-6
GROUPS, EPG, NE, DE = 4, 8, 32, 512
CAP = 64
ROUNDS = SEQ // CAP
LAG = 3
SLOTS, SLOT = 9, 4096
FAR = 1.0e5
NEG = -1.0e30
RINT = 12582912.0
TWO_PI_HI = 6.28125
TWO_PI_LO = 2.0 * math.pi - 6.28125
TURN = 6.283185

C_ID, C_LT, C_ONE, C_IOTA = 0, 128, 256, 384
C_E32, C_G32, C_TOK2, C_FAR, C_I16, C_HPI = 512, 544, 576, 578, 579, 595
C_N = 596


def build(nc, A, out):
    with ExitStack() as ctx:
        def sb(name, shape, dt=F32):
            return ctx.enter_context(nc.sbuf_tensor(name, shape, dt))

        def sem(name):
            return ctx.enter_context(nc.semaphore(name))

        ring = sb("ring", [P, SLOTS, SLOT])
        keep = sb("keep", [P, 4 * NT * D])
        h = keep[:, 0:2048].rearrange("p (t d) -> p t d", t=NT)
        hn = keep[:, 2048:4096].rearrange("p (t d) -> p t d", t=NT)
        hT = keep[:, 4096:6144].rearrange("p (k t) -> p k t", k=KD)
        mixT = keep[:, 6144:8192].rearrange("p (k t) -> p k t", k=KD)
        hn_k = keep[:, 2048:4096].rearrange("p (t q k) -> p t k q", t=NT, k=KD)
        combine = keep[:, 4096:8192].rearrange("p (t s d) -> p t s d", t=NT, s=2)
        cst = sb("cst", [P, C_N])
        ident = cst[:, C_ID:C_ID + P]
        earlier = cst[:, C_LT:C_LT + P]
        ones = cst[:, C_ONE:C_ONE + P]
        iota = cst[:, C_IOTA:C_IOTA + P]
        gains = sb("gains", [P, 4, KD])
        w_router = sb("w_router", [P, LAYERS, KD, GROUPS + NE])
        b_router = sb("b_router", [P, LAYERS, GROUPS + NE])
        conv_taps = sb("conv_taps", [P, KD, 3])
        d_bglu = sb("d_bglu", [P, 2, CHW])
        norm_s = sb("norm_s", [P, 4, NT])
        flag = sb("flag", [P, 1], I32)
        stage = sb("stage", [P, 6700])

        att_bias = stage[:, 0:2304].rearrange("p (h k) -> p h k", h=HEADS)
        ssm_b = stage[:, 2304:3584].rearrange("p (c a s) -> p c a s", c=2, a=CHW)
        ssm_c = stage[:, 3584:4864].rearrange("p (c i j) -> p c i j", c=2, i=PAIRS)
        uT = stage[:, 4864:6144].rearrange("p (c t) -> p c t", c=CHW)
        ssm_p = stage[:, 6144:6204].rearrange("p (v i) -> p v i", v=3)
        sml = stage[:, 6204:6684].rearrange("p (v i) -> p v i", v=24)
        scr = ring[:, 4:9, :].rearrange("p s n -> p (s n)")
        cos_t = scr[:, 0:5120].rearrange("p (i t) -> p i t", i=PAIRS)
        sin_t = scr[:, 5120:10240].rearrange("p (i t) -> p i t", i=PAIRS)
        tmp_t = scr[:, 10240:15360]
        qkv = scr[:, 10240:12544].rearrange("p (t w c) -> p t w c", t=NT, w=3)
        qkT = scr[:, 12544:14080].rearrange("p (c t) -> p c t", c=2 * QCH)
        yT = scr[:, 14080:15360].rearrange("p (c t) -> p c t", c=CHW)
        m1 = scr[:, 15360:15872].rearrange("p (c t) -> p c t", c=2)
        m2 = scr[:, 15872:16384].rearrange("p (c t) -> p c t", c=2)
        vv = scr[:, 16384:16896].rearrange("p (c t) -> p c t", c=2)
        zz = [scr[:, 16896 + 512 * b:17408 + 512 * b].rearrange("p (c t) -> p c t", c=2) for b in range(2)]
        qc = [scr[:, 17920 + 512 * b:18432 + 512 * b].rearrange("p (c t) -> p c t", c=2) for b in range(2)]
        qs = [scr[:, 18944 + 512 * b:19456 + 512 * b].rearrange("p (c t) -> p c t", c=2) for b in range(2)]
        ypre = scr[:, 19968:20480].rearrange("p (b t) -> p b t", b=2)
        prob = scr[:, 0:2304].rearrange("p (h k) -> p h k", h=HEADS)
        probT = scr[:, 2304:4608].rearrange("p (h k) -> p h k", h=HEADS)
        sq = scr[:, 5120:6656].rearrange("p (t c) -> p t c", t=NT)
        glu = scr[:, 6656:7936].rearrange("p (c t) -> p c t", c=CHW)
        tail = ring[:, 3, 3072:4096]
        ssm_cb = tail[:, 0:640].rearrange("p (i j) -> p i j", i=PAIRS)
        qk_gain = tail[:, 640:768].rearrange("p (w e) -> p w e", w=2)
        att_s = tail[:, 768:1024]
        z_sb = stage[:, 0:512].rearrange("p (b t) -> p b t", b=2)
        zc = stage[:, 512:1028].rearrange("p (b t) -> p b t", b=2)
        cv = stage[:, 1028:1540].rearrange("p (b t) -> p b t", b=2)
        sel = [stage[:, 256 * b:256 * b + 256].rearrange("p (t j) -> p t j", t=NT) for b in range(LAG)]
        xT = [stage[:, 768 + 512 * b:1280 + 512 * b].rearrange("p (k j) -> p k j", k=KD) for b in range(LAG)]
        hid = [stage[:, 2304 + 256 * b:2560 + 256 * b] for b in range(LAG)]
        hidT = [stage[:, 3072 + 256 * b:3328 + 256 * b].rearrange("p (b j) -> p b j", b=2) for b in range(LAG)]
        yrow = [stage[:, 3840 + 512 * b:4352 + 512 * b] for b in range(LAG)]
        vals = stage[:, 5376:5632].rearrange("p (t e v) -> p t e v", t=NT, v=4)
        rank = stage[:, 5632:5696].rearrange("p (t e) -> p t e", t=NT)
        rowv = [stage[:, 5696 + 4 * b:5700 + 4 * b] for b in range(LAG)]
        dest = sb("dest", [P, LAG], I32)
        row_at = sb("row_at", [P, 2 * LAG], I32)
        rt = keep[:, 6144:8192]
        lg = rt[:, 0:72].rearrange("p (t n) -> p t n", t=NT)
        gl8 = rt[:, 72:88].rearrange("p (t n) -> p t n", t=NT)
        gm8 = rt[:, 88:104].rearrange("p (t n) -> p t n", t=NT)
        gi8 = rt[:, 104:120].bitcast(U32).rearrange("p (t n) -> p t n", t=NT)
        gif = rt[:, 120:122].rearrange("p (t n) -> p t n", t=NT)
        ge = rt[:, 122:130].rearrange("p (t n) -> p t n", t=NT)
        gw = rt[:, 130:132]
        tm8 = rt[:, 132:148].rearrange("p (t n) -> p t n", t=NT)
        ti8 = rt[:, 148:164].bitcast(U32).rearrange("p (t n) -> p t n", t=NT)
        tif = rt[:, 164:168].rearrange("p (t n) -> p t n", t=NT)
        ex = rt[:, 168:170]
        den = rt[:, 170:172]
        wt = rt[:, 172:176].rearrange("p (s t) -> p s t", s=2)
        cmax = rt[:, 176:177]
        mask = rt[:, 192:256].rearrange("p (t n) -> p t n", t=NT)
        el = rt[:, 256:320].rearrange("p (t n) -> p t n", t=NT)
        oh = [rt[:, 320 + 64 * s:384 + 64 * s].rearrange("p (t n) -> p t n", t=NT) for s in range(2)]
        chosen = rt[:, 448:512].rearrange("p (t n) -> p t n", t=NT)
        rtmp = rt[:, 512:576].rearrange("p (t n) -> p t n", t=NT)

        bank = [ctx.enter_context(nc.psum_tensor(f"bank{i}", [P, 512], F32)) for i in range(8)]
        rows_dram = [nc.dram_tensor(f"rows{l}", [SEQ * 2 * 2, D // 2], F32, kind="Internal").ap()
                     for l in range(LAYERS)]

        ld_x = sem("ld_x")
        ld_const = sem("ld_const")
        ld_ssm = sem("ld_ssm")
        ld_att = sem("ld_att")
        ld_mix0 = [sem(f"ld_mix0_{j}") for j in range(7)]
        ld_mix1 = [sem(f"ld_mix1_{j}") for j in range(8)]
        h_ready = sem("h_ready")
        squares, mean, root, hn_ready, tp_done, hT_ready = (
            sem("squares"), sem("mean"), sem("root"), sem("hn_ready"), sem("tp_done"), sem("hT_ready"))
        u_done, u_copied = sem("u_done"), sem("u_copied")
        qkv_done, qkv_copied = sem("qkv_done"), sem("qkv_copied")
        expd, lam_ready, angle_ready, table_ready = sem("expd"), sem("lam_ready"), sem("angle_ready"), sem("table_ready")
        tab_free = sem("tab_free")
        c_ready = sem("c_ready")
        bu_done, bu_used, z_ready, q_ready, y_done = (sem("bu_done"), sem("bu_used"), sem("z_ready"),
                                                      sem("q_ready"), sem("y_done"))
        ypre_ready, gelu_ready = sem("ypre_ready"), sem("gelu_ready")
        qk_mean, qk_root, qk_ready = sem("qk_mean"), sem("qk_root"), sem("qk_ready")
        qkT_done, qkT_copied = sem("qkT_done"), sem("qkT_copied")
        score_done, shifted, exp_done, prob_ready = sem("score_done"), sem("shifted"), sem("exp_done"), sem("prob_ready")
        pT_done, pT_copied, pv_done, att_ready = sem("pT_done"), sem("pT_copied"), sem("pv_done"), sem("att_ready")
        glu_done, gate_ready, ssm_ready = sem("glu_done"), sem("gate_ready"), sem("ssm_ready")
        out0_done = sem("out0_done")
        cz_done, b_done, z_copied, g_ready, out1_done = (sem("cz_done"), sem("b_done"), sem("z_copied"),
                                                         sem("g_ready"), sem("out1_done"))
        names = ("logits", "gshift", "gexp", "eshift", "eexp", "chosen_ready", "rank_done", "route_ready")
        RS = dict((n, sem(n)) for n in names)

        def expert_sems(tag):
            s = dict((n, sem(f"{n}_{tag}")) for n in
                     ("sel_ready", "gather_done", "xT_ready", "dest_ready", "gu_done", "silu_ready", "hid_ready",
                      "turn_done", "hidT_ready", "down_done", "y_ready"))
            return s

        ES = [expert_sems(f"m{l}") for l in range(LAYERS)]
        OS = [expert_sems(f"o{l}") for l in range(LAYERS)]
        ld_gu = [[sem(f"ld_gu{l}_{u}") for u in range(LAG)] for l in range(LAYERS)]
        ld_down = [[sem(f"ld_down{l}_{u}") for u in range(LAG)] for l in range(LAYERS)]
        ld_over = [sem(f"ld_over{l}") for l in range(LAYERS)]
        scattered = [[sem(f"scattered{l}_{b}") for b in range(LAG)] for l in range(LAYERS)]
        over_scattered = [sem(f"over_scattered{l}") for l in range(LAYERS)]
        combine_ld = [sem(f"combine_ld{l}") for l in range(LAYERS)]
        stored = sem("stored")

        FIRST_SLOT = (3, 0)

        def slots(l, u):
            s = FIRST_SLOT[l] + 3 * u
            return s % SLOTS, (s + 1) % SLOTS, (s + 2) % SLOTS

        def before(eng, s, n, lag, per=1):
            if isinstance(n, int) and n < lag:
                return
            eng.wait_ge(s, (n - (lag - 1)) * per)

        def passes(engine, first, steady, last):
            whole = NE // LAG
            for u in range(LAG):
                first(u, u, 0)
            with engine.Fori(1, whole) as i:
                for u in range(LAG):
                    steady(i * LAG + u, u, i)
            for n in range(whole * LAG, NE):
                last(n, n % LAG, whole)

        def overflow(engine, body):
            count = engine.value_load(flag[0:1, 0:1], min_val=0, max_val=SEQ)
            with engine.If(count > CAP):
                for r in range(1, ROUNDS):
                    body(r - 1, 0, r)
                with engine.Fori(1, NE) as e:
                    for r in range(1, ROUNDS):
                        body(e * (ROUNDS - 1) + (r - 1), e, r)

        w_in0 = A["w_in_even"][0].rearrange("(p k) n -> p k n", k=KD)
        TILES0 = ((0, 512), (512, 1024), (1024, 1408), (1408, 1792))
        w_conv = A["w_in_conv"][0].rearrange("(p k) n -> p k n", k=KD)
        w_gate = [A["w_expert_gate"][l].rearrange("e (p k) f -> p e (k f)", k=KD) for l in range(LAYERS)]
        w_up = [A["w_expert_up"][l].rearrange("e (p k) f -> p e (k f)", k=KD) for l in range(LAYERS)]
        w_down = [A["w_expert_down"][l].rearrange("e (h p b) d -> p e h (b d)", h=2, b=2) for l in range(LAYERS)]

        def slot2(s):
            return ring[:, s, :].rearrange("p (h n) -> p h n", h=2)

        block = ctx.enter_context(nc.Block())

        @block.sync
        def _(sp):
            sp.dma_start(h, A["x"][0].rearrange("(t p) d -> p t d", p=P)).then_inc(ld_x, 16)
            for j, (a, b) in enumerate(TILES0):
                sp.dma_start(ring[:, j, 0:KD * (b - a)].rearrange("p (k n) -> p k n", k=KD),
                             w_in0[:, :, a:b]).then_inc(ld_mix0[j], 16)
            sp.wait_ge(u_done, 2)
            sp.dma_start(ring[:, 0, 0:CHW * SSM_W].rearrange("p (c n) -> p c n", c=CHW),
                         A["w_glu"][0].rearrange("(c p) n -> p c n", p=P)).then_inc(ld_mix0[4], 16)
            sp.wait_ge(qkv_done, 4)
            for j in range(2):
                sp.dma_start(ring[:, 1 + j, :].rearrange("p (c n) -> p c n", c=4),
                             A["w_out_even"][0].rearrange("(c p) n -> p c n", p=P)[:, 4 * j:4 * j + 4, :]
                             ).then_inc(ld_mix0[5 + j], 16)

            def load_gu(l, e, g, up, landed):
                sp.dma_start(ring[:, g, :], w_gate[l][:, bass.ds(e, 1), :]).then_inc(landed, 16)
                sp.dma_start(ring[:, up, :], w_up[l][:, bass.ds(e, 1), :]).then_inc(landed, 16)

            def load_dn(l, e, d, landed):
                sp.dma_start(slot2(d), w_down[l][:, bass.ds(e, 1), :, :]).then_inc(landed, 16)

            for l in range(LAYERS):
                if l == 1:
                    for j in range(6):
                        which, half = (1, 2, 0)[j % 3], j // 3
                        if j == 0:
                            sp.wait_ge(ES[0]["down_done"], NE)
                        sp.dma_start(ring[:, j, :].rearrange("p (k n) -> p k n", k=KD),
                                     w_conv[:, :, which * D + half * 512:which * D + half * 512 + 512]
                                     ).then_inc(ld_mix1[j], 16)
                    for j in range(2):
                        sp.dma_start(ring[:, 6 + j, :].rearrange("p (c n) -> p c n", c=4),
                                     A["w_out_conv"][0].rearrange("(c p) n -> p c n", p=P)[:, 4 * j:4 * j + 4, :]
                                     ).then_inc(ld_mix1[6 + j], 16)

                def first(n, u, i, l=l):
                    g, up, d = slots(l, u)
                    if l == 0 and u == 0:
                        sp.wait_ge(qkv_done, 6)
                        sp.wait_ge(att_ready, 2)
                        sp.wait_ge(ssm_ready, CHW)
                    if l == 0 and u == 2:
                        sp.wait_ge(glu_done, CHW)
                        sp.wait_ge(out0_done, 2)
                    if l == 1 and u == 0:
                        sp.wait_ge(b_done, 4)
                    if l == 1 and u == 1:
                        sp.wait_ge(b_done, 8)
                    if l == 1 and u == 2:
                        sp.wait_ge(out1_done, 2)
                    load_gu(l, n, g, up, ld_gu[l][u])
                    load_dn(l, n, d, ld_down[l][u])

                def steady(n, u, i, l=l):
                    g, up, d = slots(l, u)
                    before(sp, ES[l]["gu_done"], n, LAG)
                    load_gu(l, n, g, up, ld_gu[l][u])
                    before(sp, ES[l]["down_done"], n, LAG)
                    load_dn(l, n, d, ld_down[l][u])

                passes(sp, first, steady, steady)

                sp.wait_ge(RS["route_ready"], l + 1)
                sp.wait_ge(ES[l]["down_done"], NE)

                def body(m, e, l=l):
                    g, up, d = slots(l, 0)
                    before(sp, OS[l]["down_done"], m, 1)
                    load_gu(l, e, g, up, ld_over[l])
                    load_dn(l, e, d, ld_over[l])

                count = sp.value_load(flag[0:1, 0:1], min_val=0, max_val=SEQ)
                with sp.If(count > CAP):
                    body(0, 0)
                    with sp.Fori(1, NE) as e:
                        body(e * (ROUNDS - 1), e)
                    sp.wait_ge(OS[l]["down_done"], NE * (ROUNDS - 1))
            sp.wait_ge(h_ready, 8)
            sp.dma_start(out[0].rearrange("(t p) d -> p t d", p=P), h).then_inc(stored, 16)
            sp.wait_ge(stored, 16)

        @block.tensor
        def _(pe):
            def norm_turn(i):
                pe.wait_ge(hn_ready, 2 * i + 2)
                for j in range(4):
                    t, kh = j // 2, j % 2
                    for k in range(4):
                        last = pe.transpose(bank[j][:, k * P:(k + 1) * P], hn_k[:, t, 4 * kh + k, :], ident)
                    last.then_inc(tp_done, 1)

            def route(l):
                s = RS
                pe.wait_ge(hT_ready, 4 * (2 * l + 1) + 4)
                for t in range(NT):
                    for k in range(KD):
                        last = pe.matmul(bank[4][:, 36 * t:36 * t + 36], hT[:, k, t * P:(t + 1) * P],
                                         w_router[:, l, k, :], start=(k == 0), stop=(k == KD - 1))
                last.then_inc(s["logits"], 1)
                pe.wait_ge(s["chosen_ready"], l + 1)
                pe.matmul(bank[5][:, 0:NE], earlier, chosen[:, 0, :], start=True, stop=True)
                pe.matmul(bank[5][:, NE:2 * NE], ones, chosen[:, 0, :], start=True, stop=False)
                pe.matmul(bank[5][:, NE:2 * NE], earlier, chosen[:, 1, :], start=False, stop=True)
                pe.matmul(bank[5][:, 2 * NE:3 * NE], ones, chosen[:, 0, :], start=True, stop=False)
                pe.matmul(bank[5][:, 2 * NE:3 * NE], ones, chosen[:, 1, :], start=False, stop=True
                          ).then_inc(s["rank_done"], 1)

            def gather(S, n, b, e):
                pe.wait_ge(S["sel_ready"], n + 1)
                before(pe, S["dest_ready"], n, 1)
                for k in range(KD):
                    for t in range(NT):
                        pe.matmul(bank[2][:, k * CAP:(k + 1) * CAP], hn_k[:, t, k, :], sel[b][:, t, 0:CAP],
                                  start=(t == 0), stop=(t == NT - 1))
                for t in range(NT):
                    last = pe.matmul(bank[4][:, 0:4], sel[b][:, t, :], vals[:, t, bass.ds(e, 1), :],
                                     start=(t == 0), stop=(t == NT - 1))
                last.then_inc(S["gather_done"], 1)

            def gate_up(S, n, b, g):
                pe.wait_ge(S["xT_ready"], n + 1)
                before(pe, S["hid_ready"], n, 1)
                both = ring[:, g:g + 2, :].rearrange("p s (k n) -> p k s n", k=KD)
                for k in range(KD):
                    for half in range(2):
                        last = pe.matmul(bank[0][half * CAP:(half + 1) * CAP, :], xT[b][:, k, :],
                                         both[:, k, :, half * 256:half * 256 + 256],
                                         start=(k == 0), stop=(k == KD - 1))
                last.then_inc(S["gu_done"], 1)

            def turn(S, n, b):
                pe.wait_ge(S["hid_ready"], n + 1)
                before(pe, S["hidT_ready"], n, 1)
                for j in range(2):
                    last = pe.transpose(bank[3][:, j * P:(j + 1) * P],
                                        hid[b].rearrange("p (q b) -> p b q", b=2)[:, j, :], ident)
                last.then_inc(S["turn_done"], 1)

            def down(S, n, b, d):
                pe.wait_ge(S["hidT_ready"], n + 1)
                before(pe, S["y_ready"], n, 1)
                for c in range(4):
                    for half in range(2):
                        last = pe.matmul(bank[1][half * CAP:(half + 1) * CAP, :],
                                         hidT[b][:, c % 2, (c // 2) * CAP:(c // 2 + 1) * CAP],
                                         slot2(d)[:, c // 2, (c % 2) * D + half * 512:(c % 2) * D + half * 512 + 512],
                                         start=(c == 0), stop=(c == 3))
                last.then_inc(S["down_done"], 1)

            def experts(l):
                S = ES[l]
                pe.wait_ge(RS["route_ready"], l + 1)

                def step(n, u, i, more=True):
                    g, up, d = slots(l, u)
                    pe.wait_ge(ld_gu[l][u], (i + 1) * 32)
                    gate_up(S, n, u, g)
                    if more:
                        gather(S, n + 1, (u + 1) % LAG, n + 1)
                    turn(S, n, u)
                    pe.wait_ge(ld_down[l][u], (i + 1) * 16)
                    down(S, n, u, d)

                gather(S, 0, 0, 0)
                passes(pe, step, step, lambda n, u, i: step(n, u, i, n < NE - 1))

                O = OS[l]

                def body(m, e, r):
                    g, up, d = slots(l, 0)
                    pe.wait_ge(ld_over[l], (e + 1) * 48)
                    gather(O, m, 0, e)
                    gate_up(O, m, 0, g)
                    turn(O, m, 0)
                    down(O, m, 0, d)
                overflow(pe, body)

            pe.wait_ge(ld_const, 16 * 6)
            norm_turn(0)
            pe.wait_ge(hT_ready, 4)

            def project_u(m):
                j, c = (0, m) if m < 4 else (1, 0)
                w = ring[:, j, :].rearrange("p (k n) -> p k n", k=KD)
                for k in range(KD):
                    last = pe.matmul(bank[4 + m // 2][:, (m % 2) * 256:(m % 2) * 256 + 256],
                                     w[:, k, c * P:(c + 1) * P], hT[:, k, :], start=(k == 0), stop=(k == KD - 1))
                return last

            pe.wait_ge(ld_mix0[0], 16)
            for m in range(5):
                if m == 4:
                    pe.wait_ge(ld_mix0[1], 16)
                last = project_u(m)
                if m % 2 or m == 4:
                    last.then_inc(u_done, 1)

            QKV_BANK = ((0, 1, 2), (3, 0, 1))

            def project_qkv(j):
                w3, t = j // 2, j % 2
                src = ((1, 128, 512), (2, 0, 384), (3, 0, 384))[w3]
                n = 512 if w3 == 0 else 384
                w = ring[:, src[0], 0:KD * n].rearrange("p (k n) -> p k n", k=KD)
                pe.wait_ge(ld_mix0[src[0]], 16)
                if j >= 4:
                    pe.wait_ge(qkv_copied, j - 3)
                for k in range(KD):
                    last = pe.matmul(bank[j % 4][:, 0:ATT_W], hT[:, k, t * P:(t + 1) * P],
                                     w[:, k, src[1]:src[2]], start=(k == 0), stop=(k == KD - 1))
                last.then_inc(qkv_done, 1)

            def drive(i):
                r = 32 * (i % 4)
                if i >= 2:
                    pe.wait_ge(bu_used, i - 1)
                for c in range(2):
                    last = pe.matmul(bank[5 + i % 2][:, c * 256:c * 256 + 256], ssm_b[r:r + 32, c, i // 4, :],
                                     uT[r:r + 32, i // 4, :], start=True, stop=True)
                last.then_inc(bu_done, 1)

            def readout(i):
                c, r = i // 4, 32 * (i % 4)
                pe.wait_ge(q_ready, i + 1)
                if c >= 2 and i % 4 == 0:
                    pe.wait_ge(ypre_ready, c - 1)
                o = bank[(7, 4)[c % 2]][r:r + 32, 0:SEQ]
                b = i % 2
                pe.matmul(o, ssm_c[:, 0, i, :], qc[b][:, 0, :], start=True, stop=False)
                pe.matmul(o, ssm_cb[:, i, :], qs[b][:, 1, :], start=False, stop=False)
                pe.matmul(o, ssm_c[:, 1, i, :], qs[b][:, 0, :], start=False, stop=False)
                pe.matmul(o, ssm_c[:, 1, i, :], qc[b][:, 1, :], start=False, stop=True).then_inc(y_done, 1)

            pe.wait_ge(u_copied, 3)
            pe.wait_ge(ld_ssm, 48)
            pe.wait_ge(c_ready, 1)
            drive(0)
            drive(1)
            for i in range(PAIRS):
                if i < 6:
                    project_qkv(i)
                readout(i)
                if i + 2 < PAIRS:
                    drive(i + 2)

            pe.wait_ge(qk_ready, 1)
            for j in range(3):
                for c in range(4):
                    t, ch = (4 * j + c) // 6, (4 * j + c) % 6
                    last = pe.transpose(bank[j][:, c * P:(c + 1) * P],
                                        qkv[:, t, ch // 3, (ch % 3) * P:(ch % 3 + 1) * P], ident)
                last.then_inc(qkT_done, 1)
            pe.wait_ge(qkT_copied, 3)
            pe.wait_ge(bu_used, PAIRS)
            pe.wait_ge(ypre_ready, CHW)
            for hh in range(HEADS):
                r = 64 * (hh % 2)
                q, k = qkT[r:r + 64, hh // 2, :], qkT[r:r + 64, 3 + hh // 2, :]
                pe.matmul(bank[hh][:, 0:P], q[:, 0:P], k[:, 0:P], start=True, stop=True)
                last = pe.matmul(bank[hh][:, P:P + SEQ], q[:, P:SEQ], k, start=True, stop=True)
            last.then_inc(score_done, 1)
            pe.wait_ge(ld_mix0[4], 16)
            pe.wait_ge(gelu_ready, CHW)
            wg = ring[:, 0, 0:CHW * SSM_W].rearrange("p (c n) -> p c n", c=CHW)
            for m in range(CHW):
                if m >= 2:
                    pe.wait_ge(gate_ready, m - 1)
                for c in range(CHW):
                    last = pe.matmul(bank[6 + m % 2][:, 0:SEQ], wg[:, c, m * P:(m + 1) * P], yT[:, c, :],
                                     start=(c == 0), stop=(c == CHW - 1))
                last.then_inc(glu_done, 1)
            pe.wait_ge(prob_ready, 1)
            for hh in range(HEADS):
                for j in range(3):
                    last = pe.transpose(bank[hh][:, j * P:(j + 1) * P], prob[:, hh, j * P:(j + 1) * P], ident)
                last.then_inc(pT_done, 1)
            pe.wait_ge(pT_copied, HEADS)
            pe.wait_ge(gate_ready, CHW)
            for hh in range(HEADS):
                r, c = 64 * (hh % 2), hh // 2
                o = bank[6 + c // 2][r:r + 64, (c % 2) * SEQ:(c % 2) * SEQ + SEQ]
                pe.matmul(o, qkv[:, 0, 2, hh * HD:(hh + 1) * HD], probT[:, hh, 0:SEQ], start=True, stop=False)
                last = pe.matmul(o[:, P:SEQ], qkv[:, 1, 2, hh * HD:(hh + 1) * HD], probT[:, hh, SEQ:SEQ + P],
                                 start=False, stop=True)
            last.then_inc(pv_done, 1)

            def project_out(lds, first_slot, done):
                for t in range(NT):
                    for c in range(KD):
                        j = c // 4
                        if t == 0 and c % 4 == 0:
                            pe.wait_ge(lds[j], 16)
                        w = ring[:, first_slot + j, :].rearrange("p (c n) -> p c n", c=4)
                        for n in range(2):
                            last = pe.matmul(bank[2 * t + n][:, :], mixT[:, c, t * P:(t + 1) * P],
                                             w[:, c % 4, n * 512:(n + 1) * 512], start=(c == 0), stop=(c == KD - 1))
                    last.then_inc(done, 1)

            pe.wait_ge(ssm_ready, CHW)
            pe.wait_ge(att_ready, 2)
            project_out(ld_mix0[5:7], 1, out0_done)
            norm_turn(1)
            route(0)
            experts(0)

            norm_turn(2)
            pe.wait_ge(hT_ready, 12)
            for m in range(KD):
                half, c = m // 4, m % 4
                for part in range(3):
                    pe.wait_ge(ld_mix1[3 * half + part], 16)
                    if part != 1 and m >= 2:
                        pe.wait_ge(g_ready, m - 1)
                    o = bank[4 + m % 2][:, part * 256:part * 256 + 256] if part < 2 else bank[6 + m % 2][:, 0:256]
                    w = ring[:, 3 * half + part, :].rearrange("p (k n) -> p k n", k=KD)
                    for k in range(KD):
                        last = pe.matmul(o, w[:, k, c * P:(c + 1) * P], hT[:, k, :], start=(k == 0), stop=(k == KD - 1))
                    if part > 0:
                        last.then_inc(cz_done if part == 1 else b_done, 1)
            pe.wait_ge(g_ready, KD)
            project_out(ld_mix1[6:8], 6, out1_done)
            norm_turn(3)
            route(1)
            experts(1)

        @block.vector
        def _(dve):
            def norm(i):
                dve.wait_ge(squares, i + 1)
                dve.tensor_scalar(norm_s[:, 1, :], norm_s[:, 0, :], 1.0 / D, EPS, ALU.mult, ALU.add
                                  ).then_inc(mean, 1)
                dve.wait_ge(root, i + 1)
                dve.reciprocal(norm_s[:, 3, :], norm_s[:, 2, :])
                dve.drain()
                for t in range(NT):
                    dve.tensor_scalar(hn[:, t, :], h[:, t, :], norm_s[:, 3, t:t + 1], None, ALU.mult
                                      ).then_inc(hn_ready, 1)

            def norm_turned(i):
                for j in range(4):
                    t, kh = j // 2, j % 2
                    dve.wait_ge(tp_done, 4 * i + j + 1)
                    dve.tensor_tensor(hT[:, 4 * kh:4 * kh + 4, t * P:(t + 1) * P],
                                      bank[j][:, :].rearrange("p (k q) -> p k q", k=4),
                                      gains[:, i, 4 * kh:4 * kh + 4].unsqueeze(2).to_broadcast([P, 4, P]),
                                      ALU.mult).then_inc(hT_ready, 1)

            def residual(done):
                for t in range(NT):
                    dve.wait_ge(done, t + 1)
                    for n in range(2):
                        last = dve.tensor_tensor(h[:, t, n * 512:(n + 1) * 512], h[:, t, n * 512:(n + 1) * 512],
                                                 bank[2 * t + n][:, :], ALU.add)
                    last.then_inc(h_ready, 1)
                dve.drain()

            def route(l):
                s = RS
                dve.memset(gl8, NEG)
                dve.wait_ge(s["logits"], l + 1)
                dve.tensor_tensor(lg, bank[4][:, 0:72].rearrange("p (t n) -> p t n", t=NT),
                                  b_router[:, l, :].unsqueeze(1).to_broadcast([P, NT, GROUPS + NE]), ALU.add)
                dve.drain()
                dve.tensor_copy(gl8[:, :, 0:GROUPS], lg[:, :, 0:GROUPS])
                dve.drain()
                for t in range(NT):
                    dve.max(gm8[:, t, :], gl8[:, t, :])
                dve.drain()
                for t in range(NT):
                    dve.max_index(gi8[:, t, :], gm8[:, t, :], gl8[:, t, :])
                dve.tensor_tensor(ge, gl8[:, :, 0:GROUPS], gm8[:, :, 0:1].to_broadcast([P, NT, GROUPS]),
                                  ALU.subtract).then_inc(s["gshift"], 1)
                dve.drain()
                dve.tensor_copy(gif, gi8[:, :, 0:1])
                dve.drain()
                dve.tensor_tensor(mask, cst[:, C_G32:C_G32 + NE].unsqueeze(1).to_broadcast([P, NT, NE]),
                                  gif.to_broadcast([P, NT, NE]), ALU.is_equal)
                dve.drain()
                dve.tensor_tensor(el, lg[:, :, GROUPS:], mask, ALU.mult)
                dve.tensor_scalar(rtmp, mask, -NEG, NEG, ALU.mult, ALU.add)
                dve.drain()
                dve.tensor_tensor(el, el, rtmp, ALU.add)
                dve.drain()
                for t in range(NT):
                    dve.max(tm8[:, t, :], el[:, t, :])
                dve.drain()
                for t in range(NT):
                    dve.max_index(ti8[:, t, :], tm8[:, t, :], el[:, t, :])
                dve.tensor_tensor(ex.unsqueeze(2), tm8[:, :, 1:2], tm8[:, :, 0:1], ALU.subtract
                                  ).then_inc(s["eshift"], 1)
                dve.drain()
                dve.tensor_copy(tif, ti8[:, :, 0:2])
                dve.drain()
                for k in range(2):
                    dve.tensor_tensor(oh[k], cst[:, C_E32:C_E32 + NE].unsqueeze(1).to_broadcast([P, NT, NE]),
                                      tif[:, :, k:k + 1].to_broadcast([P, NT, NE]), ALU.is_equal)
                dve.drain()
                dve.tensor_tensor(chosen, oh[0], oh[1], ALU.add).then_inc(s["chosen_ready"], 1)
                dve.wait_ge(s["gexp"], l + 1)
                dve.wait_ge(s["eexp"], l + 1)
                dve.tensor_reduce(gw, ge, AX.X, ALU.add)
                dve.tensor_scalar(den, ex, 1.0, None, ALU.add)
                dve.drain()
                dve.tensor_tensor(den, den, gw, ALU.mult)
                dve.drain()
                dve.reciprocal(wt[:, 0, :], den)
                dve.drain()
                dve.tensor_tensor(wt[:, 1, :], wt[:, 0, :], ex, ALU.mult)
                dve.drain()
                dve.tensor_tensor(vals[:, :, :, 0], oh[1],
                                  cst[:, C_TOK2:C_TOK2 + NT].unsqueeze(2).to_broadcast([P, NT, NE]), ALU.add)
                dve.tensor_tensor(oh[0], oh[0], wt[:, 0, :].unsqueeze(2).to_broadcast([P, NT, NE]), ALU.mult)
                dve.drain()
                dve.tensor_tensor(oh[1], oh[1], wt[:, 1, :].unsqueeze(2).to_broadcast([P, NT, NE]), ALU.mult)
                dve.memset(vals[:, :, :, 2:4], 1.0)
                dve.drain()
                dve.tensor_tensor(vals[:, :, :, 1], oh[0], oh[1], ALU.add)
                dve.tensor_scalar(rtmp, chosen, 1000.0, -1000.0, ALU.mult, ALU.add)
                dve.wait_ge(s["rank_done"], l + 1)
                dve.tensor_tensor(rank, bank[5][:, 0:2 * NE].rearrange("p (t n) -> p t n", t=NT), chosen, ALU.mult)
                dve.tensor_reduce(cmax, bank[5][:, 2 * NE:3 * NE], AX.X, ALU.max)
                dve.drain()
                dve.tensor_tensor(rank, rank, rtmp, ALU.add)
                dve.tensor_copy(flag[:, :], cmax)
                dve.drain()
                dve.nop().then_inc(s["route_ready"], 1)

            def select(S, n, b, e, r, lag):
                before(dve, S["gather_done"], n, lag)
                for t in range(NT):
                    last = dve.tensor_scalar(sel[b][:, t, :], iota, float(CAP * r), rank[:, t, bass.ds(e, 1)],
                                             ALU.add, ALU.is_equal)
                last.then_inc(S["sel_ready"], 1)

            def hidden(S, n, b):
                dve.wait_ge(S["silu_ready"], n + 1)
                dve.tensor_tensor(hid[b], hid[b], bank[0][:, 256:512], ALU.mult).then_inc(S["hid_ready"], 1)

            def gathered(S, n, b, l, lag, scat, scat_n):
                dve.wait_ge(S["gather_done"], n + 1)
                before(dve, S["gu_done"], n, lag)
                dve.tensor_tensor(xT[b], bank[2][:, :].rearrange("p (k j) -> p k j", k=KD),
                                  gains[:, 2 * l + 1, :].unsqueeze(2).to_broadcast([P, KD, CAP]), ALU.mult
                                  ).then_inc(S["xT_ready"], 1)
                before(dve, S["y_ready"], n, lag)
                if scat_n is not None:
                    dve.wait_ge(scat, scat_n)
                dve.tensor_copy(rowv[b], bank[4][:, 0:4])
                dve.drain()
                dve.tensor_scalar(row_at[:, 2 * b:2 * b + 1], rowv[b][:, 0:1], 2.0, None, ALU.mult)
                dve.tensor_scalar(row_at[:, 2 * b + 1:2 * b + 2], rowv[b][:, 2:3], -FAR, cst[:, C_FAR:C_FAR + 1],
                                  ALU.mult, ALU.add)
                dve.drain()
                dve.nop().then_inc(S["dest_ready"], 1)

            def experts(l):
                S = ES[l]

                def prepare(n, b, i):
                    gathered(S, n, b, l, LAG, scattered[l][b], None if isinstance(i, int) and i == 0 else i * 16)

                def step(n, u, i, more=True):
                    v = (u + 1) % LAG
                    j = i + 1 if u == LAG - 1 else i
                    if more:
                        select(S, n + 1, v, n + 1, 0, LAG)
                    hidden(S, n, u)
                    if more:
                        prepare(n + 1, v, j)

                select(S, 0, 0, 0, 0, LAG)
                prepare(0, 0, 0)
                passes(dve, step, step, lambda n, u, i: step(n, u, i, n < NE - 1))

                O = OS[l]

                def body(m, e, r):
                    select(O, m, 0, e, r, 1)
                    gathered(O, m, 0, l, 1, over_scattered[l], None if isinstance(m, int) and m == 0 else m * 16)
                    hidden(O, m, 0)
                dve.wait_ge(ES[l]["down_done"], NE)
                for b in range(LAG):
                    dve.wait_ge(scattered[l][b], 16 * ((NE - b + LAG - 1) // LAG))
                overflow(dve, body)

            def combined(l):
                dve.wait_ge(combine_ld[l], 16)
                for t in range(NT):
                    dve.tensor_tensor(h[:, t, :], h[:, t, :], combine[:, t, 0, :], ALU.add)
                dve.drain()
                for t in range(NT):
                    dve.tensor_tensor(h[:, t, :], h[:, t, :], combine[:, t, 1, :], ALU.add).then_inc(h_ready, 1)
                dve.drain()

            names = ("step", "xr", "th", "k", "r", "t0", "w16", "cr", "ci", "lr", "li", "n0", "n1", "n2")
            V = {n: sml[:, j, :] for j, n in enumerate(names)}
            alpha = tmp_t[:, 0:320].rearrange("p (i a) -> p i a", i=PAIRS)
            beta = tmp_t[:, 320:640].rearrange("p (i a) -> p i a", i=PAIRS)
            whole = tmp_t[:, 640:960].rearrange("p (i a) -> p i a", i=PAIRS)
            a_re, a_im = ssm_p[:, 0, :], ssm_p[:, 1, :]
            norm(0)
            dve.wait_ge(ld_ssm, 48)
            dve.wait_ge(ld_const, 16 * 6)
            dve.wait_ge(expd, 1)
            dve.tensor_tensor(V["xr"], a_re, V["step"], ALU.mult).then_inc(lam_ready, 1)
            dve.tensor_tensor(V["th"], a_im, V["step"], ALU.mult)
            dve.drain()

            def rint(o, i):
                dve.tensor_scalar(o, i, RINT, -RINT, ALU.add, ALU.add)
                dve.drain()

            dve.tensor_scalar(V["k"], V["th"], 1.0 / (2.0 * math.pi), None, ALU.mult)
            dve.drain()
            rint(V["k"], V["k"])
            dve.scalar_tensor_tensor(out=V["th"], in0=V["k"], scalar=-TWO_PI_HI, in1=V["th"], op0=ALU.mult, op1=ALU.add)
            dve.drain()
            dve.scalar_tensor_tensor(out=V["th"], in0=V["k"], scalar=-TWO_PI_LO, in1=V["th"], op0=ALU.mult, op1=ALU.add)
            dve.drain()
            dve.tensor_scalar(V["th"], V["th"], 1.0 / (2.0 * math.pi), None, ALU.mult)
            dve.drain()
            dve.tensor_scalar(V["w16"], V["th"], 16.0, None, ALU.mult)
            dve.drain()
            rint(V["t0"], V["w16"])
            dve.tensor_tensor(V["w16"], V["w16"], V["t0"], ALU.subtract)
            dve.drain()
            i16 = cst[:, C_I16:C_I16 + 16].unsqueeze(1).to_broadcast([P, PAIRS, 16])
            for dst, w in ((alpha, V["w16"]), (beta, V["th"])):
                dve.tensor_tensor(dst, i16, w.unsqueeze(2).to_broadcast([P, PAIRS, 16]), ALU.mult)
                dve.drain()
                rint(whole, dst)
                dve.tensor_tensor(dst, dst, whole, ALU.subtract)
                dve.drain()
            dve.tensor_tensor(sin_t.rearrange("p i (a b) -> p i a b", a=16),
                              alpha.unsqueeze(3).to_broadcast([P, PAIRS, 16, 16]),
                              beta.unsqueeze(2).to_broadcast([P, PAIRS, 16, 16]), ALU.add)
            dve.drain()
            rint(tmp_t.rearrange("p (i t) -> p i t", i=PAIRS), sin_t)
            dve.tensor_tensor(sin_t, sin_t, tmp_t.rearrange("p (i t) -> p i t", i=PAIRS), ALU.subtract
                              ).then_inc(angle_ready, 1)
            norm_turned(0)
            dve.wait_ge(table_ready, 2)
            dve.tensor_tensor(V["lr"], V["r"], cos_t[:, :, 1], ALU.mult)
            dve.tensor_tensor(V["li"], V["r"], sin_t[:, :, 1], ALU.mult)
            dve.tensor_tensor(V["n0"], a_re, a_re, ALU.mult)
            dve.tensor_tensor(V["n1"], a_im, a_im, ALU.mult)
            dve.drain()
            dve.tensor_scalar(V["lr"], V["lr"], -1.0, None, ALU.add)
            dve.tensor_tensor(V["n0"], V["n0"], V["n1"], ALU.add)
            dve.drain()
            dve.reciprocal(V["n2"], V["n0"])
            dve.tensor_tensor(V["cr"], V["lr"], a_re, ALU.mult)
            dve.tensor_tensor(V["n1"], V["li"], a_im, ALU.mult)
            dve.tensor_tensor(V["ci"], V["li"], a_re, ALU.mult)
            dve.tensor_tensor(V["t0"], V["lr"], a_im, ALU.mult)
            dve.drain()
            dve.tensor_tensor(V["cr"], V["cr"], V["n1"], ALU.add)
            dve.tensor_tensor(V["ci"], V["ci"], V["t0"], ALU.subtract)
            dve.drain()
            dve.tensor_tensor(V["cr"], V["cr"], V["n2"], ALU.mult)
            dve.tensor_tensor(V["ci"], V["ci"], V["n2"], ALU.mult)
            dve.drain()
            cr = V["cr"].unsqueeze(2).to_broadcast([P, PAIRS, 32])
            ci = V["ci"].unsqueeze(2).to_broadcast([P, PAIRS, 32])
            pr = [tmp_t[:, 1024 + 640 * j:1664 + 640 * j].rearrange("p (i j) -> p i j", i=PAIRS) for j in range(4)]
            dve.tensor_tensor(pr[0], ssm_c[:, 0], cr, ALU.mult)
            dve.tensor_tensor(pr[1], ssm_c[:, 1], ci, ALU.mult)
            dve.tensor_tensor(pr[2], ssm_c[:, 0], ci, ALU.mult)
            dve.tensor_tensor(pr[3], ssm_c[:, 1], cr, ALU.mult)
            dve.drain()
            dve.tensor_tensor(ssm_c[:, 0], pr[0], pr[1], ALU.subtract)
            dve.tensor_tensor(ssm_cb, pr[1], pr[0], ALU.subtract)
            dve.scalar_tensor_tensor(out=ssm_c[:, 1], in0=pr[2], scalar=-1.0, in1=pr[3], op0=ALU.mult,
                                     op1=ALU.subtract)
            dve.drain()
            dve.nop().then_inc(c_ready, 1)

            for i in range(PAIRS):
                bu = bank[5 + i % 2][:, :].rearrange("p (c t) -> p c t", c=2)
                dve.wait_ge(bu_done, i + 1)
                dve.tensor_tensor(m1, bu, cos_t[:, i, :].unsqueeze(1).to_broadcast([P, 2, SEQ]), ALU.mult)
                dve.tensor_tensor(m2, bu, sin_t[:, i, :].unsqueeze(1).to_broadcast([P, 2, SEQ]), ALU.mult
                                  ).then_inc(bu_used, 1)
                dve.drain()
                dve.tensor_tensor(vv[:, 0, :], m1[:, 0, :], m2[:, 1, :], ALU.add)
                dve.tensor_tensor(vv[:, 1, :], m1[:, 1, :], m2[:, 0, :], ALU.subtract)
                dve.drain()
                if i >= 2:
                    dve.wait_ge(q_ready, i - 1)
                for c in range(2):
                    last = dve.tensor_tensor_scan(zz[i % 2][:, c, :], V["r"][:, i:i + 1].to_broadcast([P, SEQ]),
                                                  vv[:, c, :], 0.0, ALU.mult, ALU.add)
                last.then_inc(z_ready, 1)
                if i % 4 == 3:
                    c = i // 4
                    for cc in ([c - 1] if c else []) + ([c] if i == PAIRS - 1 else []):
                        dve.wait_ge(y_done, 4 * cc + 4)
                        if cc >= 2:
                            dve.wait_ge(gelu_ready, cc - 1)
                        dve.scalar_tensor_tensor(out=ypre[:, cc % 2, :], in0=uT[:, cc, :],
                                                 scalar=d_bglu[:, 0, cc:cc + 1],
                                                 in1=bank[(7, 4)[cc % 2]][:, 0:SEQ],
                                                 op0=ALU.mult, op1=ALU.add).then_inc(ypre_ready, 1)

            qk = qkv[:, :, 0:2, :].rearrange("p t w c -> p t (w c)")
            NH2 = 2 * HEADS
            ss = att_s[:, 0:24].rearrange("p (t n) -> p t n", t=NT)
            rs = att_s[:, 24:48].rearrange("p (t n) -> p t n", t=NT)
            dve.wait_ge(qkv_copied, 6)
            dve.wait_ge(q_ready, PAIRS)
            dve.wait_ge(ld_att, 32)
            dve.tensor_tensor(sq, qk, qk, ALU.mult)
            dve.drain()
            for t in range(NT):
                dve.tensor_reduce(ss[:, t, :], sq[:, t, :].rearrange("p (n e) -> p n e", e=HD), AX.X, ALU.add)
            dve.drain()
            dve.tensor_scalar(ss, ss, 1.0 / HD, EPS, ALU.mult, ALU.add).then_inc(qk_mean, 1)
            dve.wait_ge(qk_root, 1)
            dve.reciprocal(rs, rs)
            dve.drain()
            dve.tensor_scalar(rs[:, :, 0:HEADS], rs[:, :, 0:HEADS], HD ** -0.5, None, ALU.mult)
            dve.drain()
            for t in range(NT):
                v3 = qk[:, t, :].rearrange("p (n e) -> p n e", e=HD)
                dve.tensor_tensor(v3, v3, rs[:, t, :].unsqueeze(2).to_broadcast([P, NH2, HD]), ALU.mult)
            dve.drain()
            for t in range(NT):
                for w in range(2):
                    v3 = qkv[:, t, w, :].rearrange("p (n e) -> p n e", e=HD)
                    last = dve.tensor_tensor(v3, v3, qk_gain[:, w, :].unsqueeze(1).to_broadcast([P, HEADS, HD]), ALU.mult)
            last.then_inc(qk_ready, 1)
            for j in range(3):
                dve.wait_ge(qkT_done, j + 1)
                for (c0, c1) in (((0, 4),), ((0, 2), (2, 4)), ((0, 4),))[j]:
                    t, ch = (4 * j + c0) // 6, (4 * j + c0) % 6
                    last = dve.tensor_copy(qkT[:, ch:ch + c1 - c0, t * P:(t + 1) * P],
                                           bank[j][:, c0 * P:c1 * P].rearrange("p (c q) -> p c q", c=c1 - c0))
                last.then_inc(qkT_copied, 1)
            mx = att_s[:, 48:60].rearrange("p (t n) -> p t n", t=NT)
            lsum = att_s[:, 60:72].rearrange("p (t n) -> p t n", t=NT)
            dve.wait_ge(score_done, 1)
            for hh in range(HEADS):
                dve.tensor_tensor(prob[:, hh, :], bank[hh][:, 0:P + SEQ], att_bias[:, hh, :], ALU.add)
            dve.drain()
            cols = ((0, P), (P, P + SEQ))
            for t, (a, b) in enumerate(cols):
                dve.tensor_reduce(mx[:, t, :], prob[:, :, a:b], AX.X, ALU.max)
            dve.drain()
            for t, (a, b) in enumerate(cols):
                dve.tensor_tensor(prob[:, :, a:b], prob[:, :, a:b],
                                  mx[:, t, :].unsqueeze(2).to_broadcast([P, HEADS, b - a]), ALU.subtract
                                  ).then_inc(shifted, 1)
            dve.wait_ge(exp_done, 1)
            for t, (a, b) in enumerate(cols):
                dve.tensor_reduce(lsum[:, t, :], prob[:, :, a:b], AX.X, ALU.add)
            dve.drain()
            dve.reciprocal(lsum, lsum)
            dve.drain()
            for t, (a, b) in enumerate(cols):
                last = dve.tensor_tensor(prob[:, :, a:b], prob[:, :, a:b],
                                         lsum[:, t, :].unsqueeze(2).to_broadcast([P, HEADS, b - a]), ALU.mult)
            last.then_inc(prob_ready, 1)
            for m in range(CHW):
                dve.wait_ge(gate_ready, m + 1)
                dve.tensor_tensor(mixT[:, m, :], yT[:, m, :], glu[:, m, :], ALU.mult).then_inc(ssm_ready, 1)
            for hh in range(HEADS):
                dve.wait_ge(pT_done, hh + 1)
                dve.tensor_copy(probT[:, hh, :], bank[hh][:, 0:P + SEQ]).then_inc(pT_copied, 1)
            dve.wait_ge(pv_done, 1)
            dve.tensor_copy(mixT[:, 5:7, :], bank[6][:, :].rearrange("p (c t) -> p c t", c=2)).then_inc(att_ready, 1)
            dve.tensor_copy(mixT[:, 7, :], bank[7][:, 0:SEQ]).then_inc(att_ready, 1)
            residual(out0_done)
            norm(1)
            norm_turned(1)
            route(0)
            experts(0)
            combined(0)

            norm(2)
            norm_turned(2)
            dve.memset(zc, 0.0)
            dve.drain()
            for m in range(KD):
                b = m % 2
                dve.wait_ge(z_copied, m + 1)
                dve.tensor_tensor(zc[:, b, 2:], bank[4 + b][:, 0:SEQ], z_sb[:, b, :], ALU.mult)
                dve.drain()
                dve.tensor_scalar(cv[:, b, :], zc[:, b, 2:], conv_taps[:, m, 2:3], None, ALU.mult)
                dve.drain()
                for tap in (1, 0):
                    dve.scalar_tensor_tensor(out=cv[:, b, :], in0=zc[:, b, tap:tap + SEQ],
                                             scalar=conv_taps[:, m, tap:tap + 1], in1=cv[:, b, :],
                                             op0=ALU.mult, op1=ALU.add)
                    dve.drain()
                dve.wait_ge(b_done, m + 1)
                dve.tensor_tensor(mixT[:, m, :], cv[:, b, :], bank[6 + b][:, 0:SEQ], ALU.mult).then_inc(g_ready, 1)
            residual(out1_done)
            norm(3)
            norm_turned(3)
            route(1)
            experts(1)
            combined(1)

        @block.scalar
        def _(act):
            act.dma_start(cst[:, :], A["cst"]).then_inc(ld_const, 16)
            act.dma_start(gains[:, :, :], A["gains"]).then_inc(ld_const, 16)
            act.dma_start(stage[:, 6144:6204], A["ssm_p"]).then_inc(ld_ssm, 16)
            act.dma_start(stage[:, 2304:3584], A["ssm_b"]).then_inc(ld_ssm, 16)
            act.dma_start(stage[:, 3584:4864], A["ssm_c"]).then_inc(ld_ssm, 16)
            act.dma_start(w_router[:, :, :, :], A["w_router"]).then_inc(ld_const, 16)
            act.dma_start(b_router[:, :, :], A["b_router"]).then_inc(ld_const, 16)
            act.dma_start(d_bglu[:, :, :], A["d_bglu"]).then_inc(ld_const, 16)
            act.dma_start(conv_taps[:, :, :], A["conv_taps"]).then_inc(ld_const, 16)
            act.dma_start(qk_gain, A["qk_gain"]).then_inc(ld_att, 16)
            act.dma_start(att_bias, A["att_bias"]).then_inc(ld_att, 16)

            def norm(i):
                if i == 0:
                    act.wait_ge(ld_x, 16)
                else:
                    act.wait_ge(h_ready, 2 * i)
                for t in range(NT):
                    act.activation(hn[:, t, :], h[:, t, :], ACT.Square, accum_out=norm_s[:, 0, t:t + 1])
                act.drain()
                act.nop().then_inc(squares, 1)
                act.wait_ge(mean, i + 1)
                act.activation(norm_s[:, 2, :], norm_s[:, 1, :], ACT.Sqrt).then_inc(root, 1)

            def route(l):
                s = RS
                act.wait_ge(s["gshift"], l + 1)
                act.activation(ge, ge, ACT.Exp).then_inc(s["gexp"], 1)
                act.wait_ge(s["eshift"], l + 1)
                act.activation(ex, ex, ACT.Exp).then_inc(s["eexp"], 1)

            def silu(S, n, b, lag):
                act.wait_ge(S["gu_done"], n + 1)
                before(act, S["turn_done"], n, lag)
                act.activation(hid[b], bank[0][:, 0:256], ACT.Silu).then_inc(S["silu_ready"], 1)

            def turned(S, n, b, lag):
                act.wait_ge(S["turn_done"], n + 1)
                before(act, S["down_done"], n, lag)
                act.activation(hidT[b].rearrange("p b j -> p (b j)"), bank[3][:, 0:256], ACT.Copy
                               ).then_inc(S["hidT_ready"], 1)

            def weigh(S, n, b, scat, scat_n):
                act.wait_ge(S["down_done"], n + 1)
                act.wait_ge(S["dest_ready"], n + 1)
                if scat_n is not None:
                    act.wait_ge(scat, scat_n)
                act.activation(yrow[b], bank[1][:, :], ACT.Copy, scale=rowv[b][:, 1:2]).then_inc(S["y_ready"], 1)

            def experts(l):
                S = ES[l]

                def step(n, u, i):
                    silu(S, n, u, LAG)
                    turned(S, n, u, LAG)
                    weigh(S, n, u, scattered[l][u], None if isinstance(i, int) and i == 0 else i * 16)
                passes(act, step, step, step)
                O = OS[l]

                def body(m, e, r):
                    silu(O, m, 0, 1)
                    turned(O, m, 0, 1)
                    weigh(O, m, 0, over_scattered[l], None if isinstance(m, int) and m == 0 else m * 16)
                overflow(act, body)

            act.wait_ge(ld_ssm, 48)
            act.activation(sml[:, 0, :], ssm_p[:, 2, :], ACT.Exp).then_inc(expd, 1)
            norm(0)
            act.wait_ge(lam_ready, 1)
            act.activation(sml[:, 4, :], sml[:, 1, :], ACT.Exp)
            act.wait_ge(angle_ready, 1)
            act.activation(cos_t, sin_t, ACT.Abs)
            act.drain()
            act.activation(cos_t, cos_t, ACT.Sin, scale=-TURN, bias=cst[:, C_HPI:C_HPI + 1]).then_inc(table_ready, 1)
            act.activation(sin_t, sin_t, ACT.Sin, scale=TURN)
            act.drain()
            act.nop().then_inc(table_ready, 1)
            for j in range(3):
                act.wait_ge(u_done, j + 1)
                n = 2 if j < 2 else 1
                act.activation(uT[:, 2 * j:2 * j + n, :].rearrange("p c t -> p (c t)"), bank[4 + j][:, 0:256 * n],
                               ACT.Copy).then_inc(u_copied, 1)
            act.wait_ge(c_ready, 1)
            for j in range(6):
                w, t = j // 2, j % 2
                act.wait_ge(qkv_done, j + 1)
                act.activation(qkv[:, t, w, :], bank[j % 4][:, 0:ATT_W], ACT.Copy).then_inc(qkv_copied, 1)
            for c in range(CHW):
                act.wait_ge(ypre_ready, c + 1)
                act.activation(yT[:, c, :], ypre[:, c % 2, :], ACT.Gelu_apprx_tanh).then_inc(gelu_ready, 1)
            act.wait_ge(qk_mean, 1)
            act.activation(att_s[:, 24:48], att_s[:, 0:24], ACT.Sqrt).then_inc(qk_root, 1)
            act.wait_ge(shifted, 2)
            act.activation(prob, prob, ACT.Exp).then_inc(exp_done, 1)
            for m in range(CHW):
                act.wait_ge(glu_done, m + 1)
                act.activation(glu[:, m, :], bank[6 + m % 2][:, 0:SEQ], ACT.Sigmoid, bias=d_bglu[:, 1, m:m + 1]
                               ).then_inc(gate_ready, 1)
            norm(1)
            route(0)
            experts(0)
            norm(2)
            for m in range(KD):
                act.wait_ge(cz_done, m + 1)
                if m >= 2:
                    act.wait_ge(g_ready, m - 1)
                act.activation(z_sb[:, m % 2, :], bank[4 + m % 2][:, SEQ:2 * SEQ], ACT.Copy).then_inc(z_copied, 1)
            norm(3)
            route(1)
            experts(1)

        @block.gpsimd
        def _(pool):
            pool.wait_ge(table_ready, 2)
            for i in range(PAIRS):
                b = i % 2
                pool.wait_ge(z_ready, i + 1)
                if i >= 2:
                    pool.wait_ge(y_done, i - 1)
                for c in range(2):
                    pool.tensor_tensor(qc[b][:, c, :], zz[b][:, c, :], cos_t[:, i, :], ALU.mult)
                    last = pool.tensor_tensor(qs[b][:, c, :], zz[b][:, c, :], sin_t[:, i, :], ALU.mult)
                last.then_inc(q_ready, 1)

            def scatter(l, S, n, b, done):
                pool.wait_ge(S["y_ready"], n + 1)
                pool.tensor_tensor(dest[:, b:b + 1], row_at[:, 2 * b:2 * b + 1], row_at[:, 2 * b + 1:2 * b + 2],
                                   ALU.add)
                pool.drain()
                pool.indirect_dma_start(rows_dram[l], bass.IndirectOffsetOnAxis(ap=dest[:, b:b + 1], axis=0),
                                        yrow[b], None, bounds_check=4 * SEQ - 1, oob_is_err=False).then_inc(done, 16)

            for l in range(LAYERS):
                step = lambda n, u, i, l=l: scatter(l, ES[l], n, u, scattered[l][u])
                passes(pool, step, step, step)
                for b in range(LAG):
                    pool.wait_ge(scattered[l][b], 16 * ((NE - b + LAG - 1) // LAG))
                pool.wait_ge(RS["route_ready"], l + 1)
                count = pool.value_load(flag[0:1, 0:1], min_val=0, max_val=SEQ)
                with pool.If(count > CAP):
                    for r in range(ROUNDS - 1):
                        scatter(l, OS[l], r, 0, over_scattered[l])
                    with pool.Fori(1, NE) as e:
                        for r in range(ROUNDS - 1):
                            scatter(l, OS[l], e * (ROUNDS - 1) + r, 0, over_scattered[l])
                    pool.wait_ge(over_scattered[l], 16 * NE * (ROUNDS - 1))
                pool.dma_start(combine, rows_dram[l].rearrange("(t p s b) d -> p t s (b d)", t=NT, s=2, b=2)
                               ).then_inc(combine_ld[l], 16)


def constants(np):
    c = np.zeros((P, C_N), np.float32)
    r = np.arange(P)
    c[:, C_ID:C_ID + P] = np.eye(P)
    c[:, C_LT:C_LT + P] = r[:, None] < r[None, :]
    c[:, C_ONE:C_ONE + P] = 1.0
    c[:, C_IOTA:C_IOTA + P] = r % CAP
    c[:, C_E32:C_E32 + NE] = np.arange(NE)
    c[:, C_G32:C_G32 + NE] = np.arange(NE) // EPG
    c[:, C_TOK2:C_TOK2 + NT] = 2 * (r[:, None] + P * np.arange(NT)[None, :])
    c[:, C_FAR] = FAR + r // CAP
    c[:, C_I16:C_I16 + 16] = np.arange(16)
    c[:, C_HPI] = TURN / 4
    i, j = np.arange(SEQ)[:, None], np.arange(SEQ)[None, :]
    diff = i - j
    n = ((diff <= 128).astype(int) + (diff % 4 == 0) + (diff % 16 == 0)) * (diff >= 0)
    bias = np.zeros((P, HEADS, P + SEQ), np.float32)
    for hh in range(HEADS):
        slope = 2.0 ** (-8.0 * (hh + 1) / HEADS)
        full = np.where(n > 0, -slope * diff + np.log(np.maximum(n, 1)), NEG).astype(np.float32)
        bias[:, hh, 0:P] = full[0:P, 0:P]
        bias[:, hh, P:] = full[P:, :]
    return c, bias


def layout(np, I):
    pairs = lambda a: np.ascontiguousarray(a[0].reshape(PAIRS, P).T)
    step = np.repeat(np.asarray(I["ssm_log_step"])[0], 64).reshape(PAIRS, P).T
    ssm_p = np.stack([pairs(np.asarray(I["ssm_a_re"])), pairs(np.asarray(I["ssm_a_im"])), step], 1)
    ssm_b = np.zeros((4, 2, 16, 2, CHW, 2, 64), np.float32)
    ssm_c = np.zeros((2, 64, 2, PAIRS, 2, 16), np.float32)
    for z, (bn, cn) in enumerate((("ssm_b_re", "ssm_c_re"), ("ssm_b_im", "ssm_c_im"))):
        b = np.asarray(I[bn])[0].reshape(CHW, 4, 2, 64, 16)
        c = np.asarray(I[cn])[0].reshape(PAIRS, 2, 16, 64)
        for g in range(2):
            ssm_b[:, g, :, z, :, g, :] = b[:, :, g].transpose(1, 3, 0, 2)
            ssm_c[g, :, z, :, g, :] = c[:, g].transpose(2, 0, 1)
    gains = np.stack([np.asarray(I[n])[l].reshape(P, KD) for l in range(LAYERS) for n in ("norm_mix", "norm_ffn")], 1)
    w_router = np.stack([np.concatenate([np.asarray(I["w_router_group"])[l].reshape(P, KD, GROUPS),
                                         np.asarray(I["w_router_expert"])[l].reshape(P, KD, NE)], 2)
                         for l in range(LAYERS)], 1)
    b_router = np.concatenate([np.asarray(I["b_router_group"]), np.asarray(I["b_router_expert"])], 1)
    col = lambda a: np.asarray(a)[0].reshape(CHW, P).T
    cst, bias = constants(np)
    return {
        "ssm_p": ssm_p.reshape(P, 60), "ssm_b": ssm_b.reshape(P, 1280), "ssm_c": ssm_c.reshape(P, 1280),
        "gains": gains, "w_router": w_router, "b_router": np.tile(b_router[None], (P, 1, 1)),
        "d_bglu": np.stack([col(I["ssm_d"]), col(I["b_glu"])], 1),
        "conv_taps": np.asarray(I["conv_w"])[0].reshape(3, KD, P).transpose(2, 1, 0),
        "qk_gain": np.tile(np.concatenate([np.asarray(I["q_norm"]), np.asarray(I["k_norm"])], 0)[None], (P, 1, 1)),
        "cst": cst, "att_bias": bias,
    }


_BIG = ["x", "w_in_even", "w_glu", "w_out_even", "w_in_conv", "w_out_conv",
        "w_expert_gate", "w_expert_up", "w_expert_down"]


def kernel(**inputs):
    import numpy as np
    import concourse.bacc as bacc
    from concourse.bass_utils import run_bass_kernel_spmd

    nc = bacc.Bacc("TRN2", target_bir_lowering=False, num_devices=1)
    given = {n: np.ascontiguousarray(inputs[n]) for n in _BIG}
    given.update((n, np.ascontiguousarray(a)) for n, a in layout(np, inputs).items())
    arrays = {f"in_{n}": a for n, a in given.items()}
    A = {n: nc.dram_tensor(f"in_{n}", a.shape, F32, kind="ExternalInput").ap() for n, a in given.items()}
    out = nc.dram_tensor("out_0", (1, SEQ, D), F32, kind="ExternalOutput").ap()
    build(nc, A, out)
    r = run_bass_kernel_spmd(nc, [arrays], core_ids=[0])
    return r.results[0]["out_0"]
```

```python
from contextlib import ExitStack
import math

import concourse.bass as bass
from concourse import mybir

F32 = mybir.dt.float32
I32 = mybir.dt.int32
U32 = mybir.dt.uint32
ACT = mybir.ActivationFunctionType
ALU = mybir.AluOpType
AX = mybir.AxisListType

P = 128
SEQ = 256
D = 1024
NT = SEQ // P
KD = D // P
LAYERS = 2
SSM_W, PAIRS, CHW = 640, 20, 5
DUOS = PAIRS // 2
HEADS, HD, ATT_W = 6, 64, 384
QCH = ATT_W // P
EPS = 1e-6
GROUPS, EPG, NE, DE = 4, 8, 32, 512
CAP = 64
ROUNDS = SEQ // CAP
LAG = 3
SLOTS, SLOT = 9, 4096
FAR = 1.0e5
NEG = -1.0e30
RINT = 12582912.0
TWO_PI_HI = 6.28125
TWO_PI_LO = 2.0 * math.pi - 6.28125
TURN = 6.283185

C_ID, C_LT, C_ONE, C_IOTA = 0, 128, 256, 384
C_E32, C_G32, C_TOK2, C_FAR, C_I16, C_HPI = 512, 544, 576, 578, 579, 595
C_N = 596


def build(nc, A, out):
    with ExitStack() as ctx:
        def sb(name, shape, dt=F32):
            return ctx.enter_context(nc.sbuf_tensor(name, shape, dt))

        def sem(name):
            return ctx.enter_context(nc.semaphore(name))

        ring = sb("ring", [P, SLOTS, SLOT])
        keep = sb("keep", [P, 4 * NT * D])
        h = keep[:, 0:2048].rearrange("p (t d) -> p t d", t=NT)
        hn = keep[:, 2048:4096].rearrange("p (t d) -> p t d", t=NT)
        hT = keep[:, 4096:6144].rearrange("p (k t) -> p k t", k=KD)
        mixT = keep[:, 6144:8192].rearrange("p (k t) -> p k t", k=KD)
        hn_k = keep[:, 2048:4096].rearrange("p (t q k) -> p t k q", t=NT, k=KD)
        combine = keep[:, 4096:8192].rearrange("p (t s d) -> p t s d", t=NT, s=2)
        cst = sb("cst", [P, C_N])
        ident = cst[:, C_ID:C_ID + P]
        earlier = cst[:, C_LT:C_LT + P]
        ones = cst[:, C_ONE:C_ONE + P]
        iota = cst[:, C_IOTA:C_IOTA + P]
        gains = sb("gains", [P, 4, KD])
        w_router = sb("w_router", [P, LAYERS, KD, GROUPS + NE])
        b_router = sb("b_router", [P, LAYERS, GROUPS + NE])
        conv_taps = sb("conv_taps", [P, KD, 3])
        d_bglu = sb("d_bglu", [P, 2, CHW])
        qk_gain = sb("qk_gain", [P, 2])
        norm_s = sb("norm_s", [P, 4, NT])
        flag = sb("flag", [P, 1], I32)
        stage = sb("stage", [P, 6700])

        prob = stage[:, 0:2304].rearrange("p (h k) -> p h k", h=HEADS)
        ssm_b = stage[:, 2304:3584].rearrange("p (c a s) -> p c a s", c=2, a=CHW)
        glu = stage[:, 2304:3584].rearrange("p (c t) -> p c t", c=CHW)
        ssm_c = stage[:, 3584:4864].rearrange("p (c i j) -> p c i j", c=2, i=PAIRS)
        uT = stage[:, 4864:6144].rearrange("p (c t) -> p c t", c=CHW)
        yT = uT
        ssm_p = stage[:, 6144:6204].rearrange("p (v i) -> p v i", v=3)
        sml = stage[:, 6204:6684].rearrange("p (v i) -> p v i", v=24)
        c_tmp = [keep[:, 2048 + 640 * j:2688 + 640 * j].rearrange("p (i j) -> p i j", i=PAIRS) for j in range(3)]
        sq = keep[:, 2048:3584].rearrange("p (t c) -> p t c", t=NT)
        probT = keep[:, 2048:4352].rearrange("p (h k) -> p h k", h=HEADS)
        qkT = keep[:, 6144:7680].rearrange("p (c t) -> p c t", c=2 * QCH)
        scr = ring[:, 4:9, :].rearrange("p s n -> p (s n)")
        duo = lambda a: scr[:, a:a + 1024].rearrange("p (i c t) -> p i c t", i=2, c=2)
        cos_t = scr[:, 0:5120].rearrange("p (i t) -> p i t", i=PAIRS)
        sin_t = scr[:, 5120:10240].rearrange("p (i t) -> p i t", i=PAIRS)
        zz = [duo(10240 + 1024 * b) for b in range(2)]
        m2 = duo(12288)
        alpha, beta, whole = [scr[:, 12288 + 320 * j:12608 + 320 * j].rearrange("p (i a) -> p i a", i=PAIRS)
                              for j in range(3)]
        qc = [duo(13312 + 1024 * b) for b in range(2)]
        qs = [duo(15360 + 1024 * b) for b in range(2)]
        ypre = scr[:, 17408:17920].rearrange("p (b t) -> p b t", b=2)
        att_s = scr[:, 17920:18176]
        qkv = scr[:, 18176:20480].rearrange("p (t w c) -> p t w c", t=NT, w=3)
        ssm_cb = ring[:, 3, 3072:3712].rearrange("p (i j) -> p i j", i=PAIRS)
        z_sb = stage[:, 0:512].rearrange("p (b t) -> p b t", b=2)
        zc = stage[:, 512:1028].rearrange("p (b t) -> p b t", b=2)
        cv = stage[:, 1028:1540].rearrange("p (b t) -> p b t", b=2)
        sel = [stage[:, 256 * b:256 * b + 256].rearrange("p (t j) -> p t j", t=NT) for b in range(LAG)]
        xT = [stage[:, 768 + 512 * b:1280 + 512 * b].rearrange("p (k j) -> p k j", k=KD) for b in range(LAG)]
        hid = [stage[:, 2304 + 256 * b:2560 + 256 * b] for b in range(LAG)]
        hidT = [stage[:, 3072 + 256 * b:3328 + 256 * b].rearrange("p (b j) -> p b j", b=2) for b in range(LAG)]
        yrow = [stage[:, 3840 + 512 * b:4352 + 512 * b] for b in range(LAG)]
        vals = stage[:, 5376:5632].rearrange("p (t e v) -> p t e v", t=NT, v=4)
        rank = stage[:, 5632:5696].rearrange("p (t e) -> p t e", t=NT)
        rowv = [stage[:, 5696 + 4 * b:5700 + 4 * b] for b in range(LAG)]
        dest = sb("dest", [P, LAG], I32)
        row_at = sb("row_at", [P, 2 * LAG], I32)
        rt = keep[:, 6144:8192]
        lg = rt[:, 0:72].rearrange("p (t n) -> p t n", t=NT)
        gl8 = rt[:, 72:88].rearrange("p (t n) -> p t n", t=NT)
        gm8 = rt[:, 88:104].rearrange("p (t n) -> p t n", t=NT)
        gi8 = rt[:, 104:120].bitcast(U32).rearrange("p (t n) -> p t n", t=NT)
        gif = rt[:, 120:122].rearrange("p (t n) -> p t n", t=NT)
        ge = rt[:, 122:130].rearrange("p (t n) -> p t n", t=NT)
        gw = rt[:, 130:132]
        tm8 = rt[:, 132:148].rearrange("p (t n) -> p t n", t=NT)
        ti8 = rt[:, 148:164].bitcast(U32).rearrange("p (t n) -> p t n", t=NT)
        tif = rt[:, 164:168].rearrange("p (t n) -> p t n", t=NT)
        ex = rt[:, 168:170]
        den = rt[:, 170:172]
        wt = rt[:, 172:176].rearrange("p (s t) -> p s t", s=2)
        cmax = rt[:, 176:177]
        mask = rt[:, 192:256].rearrange("p (t n) -> p t n", t=NT)
        el = rt[:, 256:320].rearrange("p (t n) -> p t n", t=NT)
        oh = [rt[:, 320 + 64 * s:384 + 64 * s].rearrange("p (t n) -> p t n", t=NT) for s in range(2)]
        chosen = rt[:, 448:512].rearrange("p (t n) -> p t n", t=NT)
        rtmp = rt[:, 512:576].rearrange("p (t n) -> p t n", t=NT)

        psum = ctx.enter_context(nc.psum_tensor("psum", [P, 8, 512], F32))
        bank = [psum[:, i, :] for i in range(8)]
        rows_dram = [nc.dram_tensor(f"rows{l}", [SEQ * 2 * 2, D // 2], F32, kind="Internal").ap()
                     for l in range(LAYERS)]

        ld_p, ld_b, ld_c = sem("ld_p"), sem("ld_b"), sem("ld_c")
        ld_x = [sem(f"ld_x{t}") for t in range(NT)]
        ld_const, ld_att, ld_route = sem("ld_const"), sem("ld_att"), sem("ld_route")
        ld_mix0 = [sem(f"ld_mix0_{j}") for j in range(7)]
        ld_mix1 = ld_mix0[:6] + [sem(f"ld_mix1_{j}") for j in range(2)]
        h_ready = sem("h_ready")
        squares, mean, root, hn_ready, tp_done, hT_ready = (
            sem("squares"), sem("mean"), sem("root"), sem("hn_ready"), sem("tp_done"), sem("hT_ready"))
        u_done, u_copied = sem("u_done"), sem("u_copied")
        qkv_done, qkv_copied = sem("qkv_done"), sem("qkv_copied")
        expd, lam_ready, r_ready, turn_ready, pole_ready = (sem("expd"), sem("lam_ready"), sem("r_ready"),
                                                            sem("turn_ready"), sem("pole_ready"))
        ab_ready, pool_added, angle_ready, table_ready = (sem("ab_ready"), sem("pool_added"), sem("angle_ready"),
                                                          sem("table_ready"))
        c_ready = sem("c_ready")
        bu_done, bu_used, z_ready, q_ready, y_done = (sem("bu_done"), sem("bu_used"), sem("z_ready"),
                                                      sem("q_ready"), sem("y_done"))
        ypre_ready, gelu_ready = sem("ypre_ready"), sem("gelu_ready")
        qk_mean, qk_root, qk_ready = sem("qk_mean"), sem("qk_root"), sem("qk_ready")
        qkT_done, qkT_copied = sem("qkT_done"), sem("qkT_copied")
        score_done, score_copied, max_ready, exp_done, prob_ready = (
            sem("score_done"), sem("score_copied"), sem("max_ready"), sem("exp_done"), sem("prob_ready"))
        pT_done, pT_copied, pv_done, att_ready = sem("pT_done"), sem("pT_copied"), sem("pv_done"), sem("att_ready")
        glu_done, gate_ready, ssm_ready = sem("glu_done"), sem("gate_ready"), sem("ssm_ready")
        out0_done = sem("out0_done")
        cz_done, b_done, z_copied, g_ready, out1_done = (sem("cz_done"), sem("b_done"), sem("z_copied"),
                                                         sem("g_ready"), sem("out1_done"))
        names = ("logits", "gshift", "gexp", "eshift", "eexp", "chosen_ready", "rank_done", "route_ready")
        RS = dict((n, sem(n)) for n in names)

        def expert_sems(tag):
            s = dict((n, sem(f"{n}_{tag}")) for n in
                     ("sel_ready", "gather_done", "xT_ready", "dest_ready", "dest_made", "gu_done", "silu_ready", "hid_ready",
                      "turn_done", "hidT_ready", "down_done", "y_ready"))
            return s

        ES = [expert_sems(f"m{l}") for l in range(LAYERS)]
        OS = [expert_sems(f"o{l}") for l in range(LAYERS)]
        ld_gu = [[sem(f"ld_gu{l}_{u}") for u in range(LAG)] for l in range(LAYERS)]
        ld_down = [[sem(f"ld_down{l}_{u}") for u in range(LAG)] for l in range(LAYERS)]
        ld_over = [sem(f"ld_over{l}") for l in range(LAYERS)]
        scattered = [[sem(f"scattered{l}_{b}") for b in range(LAG)] for l in range(LAYERS)]
        over_scattered = [sem(f"over_scattered{l}") for l in range(LAYERS)]
        combine_asked = sem("combine_asked")
        combine_ld = [[sem(f"combine_ld{l}_{t}") for t in range(NT)] for l in range(LAYERS)]
        stored = sem("stored")

        FIRST_SLOT = (3, 0)
        OVER = 6

        def slots(l, u):
            s = FIRST_SLOT[l] + 3 * u
            return s % SLOTS, (s + 1) % SLOTS, (s + 2) % SLOTS

        def before(eng, s, n, lag, per=1):
            if isinstance(n, int) and n < lag:
                return
            eng.wait_ge(s, (n - (lag - 1)) * per)

        def passes(engine, first, steady, last):
            whole = NE // LAG
            for u in range(LAG):
                first(u, u, 0)
            with engine.Fori(1, whole) as i:
                for u in range(LAG):
                    steady(i * LAG + u, u, i)
            for n in range(whole * LAG, NE):
                last(n, n % LAG, whole)

        def overflow(engine, body):
            count = engine.value_load(flag[0:1, 0:1], min_val=0, max_val=SEQ)
            with engine.If(count > CAP):
                for r in range(1, ROUNDS):
                    body(r - 1, 0, r)
                with engine.Fori(1, NE) as e:
                    for r in range(1, ROUNDS):
                        body(e * (ROUNDS - 1) + (r - 1), e, r)

        w_in0 = A["w_in_even"][0].rearrange("(p k) n -> p k n", k=KD)
        TILES0 = ((0, 512), (512, 1024), (1024, 1408), (1408, 1792))
        w_conv = A["w_in_conv"][0].rearrange("(p k) n -> p k n", k=KD)
        w_gate = [A["w_expert_gate"][l].rearrange("e (p k) f -> p e (k f)", k=KD) for l in range(LAYERS)]
        w_up = [A["w_expert_up"][l].rearrange("e (p k) f -> p e (k f)", k=KD) for l in range(LAYERS)]
        w_down = [A["w_expert_down"][l].rearrange("e (h p b) d -> p e h (b d)", h=2, b=2) for l in range(LAYERS)]

        def slot2(s):
            return ring[:, s, :].rearrange("p (h n) -> p h n", h=2)

        def turn_bank(i, j):
            return (j + 2) % 4 if i == 1 else j

        def angle_sum(eng, c):
            i = slice(4 * c, 4 * c + 4)
            return eng.tensor_tensor(sin_t[:, i, :].rearrange("p i (a b) -> p i a b", a=16),
                                     alpha[:, i, :].unsqueeze(3).to_broadcast([P, 4, 16, 16]),
                                     beta[:, i, :].unsqueeze(2).to_broadcast([P, 4, 16, 16]), ALU.add)

        block = ctx.enter_context(nc.Block())

        @block.sync
        def _(sp):
            def projection(j):
                a, b = TILES0[j]
                sp.dma_start(ring[:, j, 0:KD * (b - a)].rearrange("p (k n) -> p k n", k=KD),
                             w_in0[:, :, a:b]).then_inc(ld_mix0[j], 16)

            sp.dma_start(stage[:, 6144:6204], A["ssm_p"]).then_inc(ld_p, 16)
            for t in range(NT):
                sp.dma_start(h[:, t, :], A["x"][0][t * P:(t + 1) * P, :]).then_inc(ld_x[t], 16)
            sp.dma_start(cst[:, :], A["cst"]).then_inc(ld_const, 16)
            sp.dma_start(gains[:, :, :], A["gains"]).then_inc(ld_const, 16)
            projection(0)
            sp.dma_start(stage[:, 2304:3584], A["ssm_b"]).then_inc(ld_b, 16)
            projection(1)
            sp.dma_start(stage[:, 3584:4864], A["ssm_c"]).then_inc(ld_c, 16)
            sp.dma_start(d_bglu[:, :, :], A["d_bglu"]).then_inc(ld_c, 16)
            projection(2)
            projection(3)
            sp.dma_start(qk_gain[:, :], A["qk_gain"]).then_inc(ld_att, 16)
            sp.dma_start(prob, A["att_bias"]).then_inc(ld_att, 16)
            sp.dma_start(w_router[:, :, :, :], A["w_router"]).then_inc(ld_route, 16)
            sp.dma_start(b_router[:, :, :], A["b_router"]).then_inc(ld_route, 16)
            sp.dma_start(conv_taps[:, :, :], A["conv_taps"]).then_inc(ld_route, 16)
            sp.wait_ge(u_done, 4)
            sp.dma_start(ring[:, 0, 0:CHW * SSM_W].rearrange("p (c n) -> p c n", c=CHW),
                         A["w_glu"][0].rearrange("(c p) n -> p c n", p=P)).then_inc(ld_mix0[4], 16)
            sp.wait_ge(qkv_done, 4)
            for j in range(2):
                sp.dma_start(ring[:, 1 + j, :].rearrange("p (c n) -> p c n", c=4),
                             A["w_out_even"][0].rearrange("(c p) n -> p c n", p=P)[:, 4 * j:4 * j + 4, :]
                             ).then_inc(ld_mix0[5 + j], 16)

            def load_g(l, e, g, landed):
                sp.dma_start(ring[:, g, :], w_gate[l][:, bass.ds(e, 1), :]).then_inc(landed, 16)

            def load_u(l, e, up, landed):
                sp.dma_start(ring[:, up, :], w_up[l][:, bass.ds(e, 1), :]).then_inc(landed, 16)

            def load_dn(l, e, d, landed):
                sp.dma_start(slot2(d), w_down[l][:, bass.ds(e, 1), :, :]).then_inc(landed, 16)

            def conv_tile(j):
                which, half = (1, 2, 0)[j % 3], j // 3
                sp.dma_start(ring[:, 1 + j, :].rearrange("p (k n) -> p k n", k=KD),
                             w_conv[:, :, which * D + half * 512:which * D + half * 512 + 512]
                             ).then_inc(ld_mix1[j], 16)

            for l in range(LAYERS):
                if l == 1:
                    sp.wait_ge(combine_asked, 1)
                    sp.wait_ge(ES[0]["down_done"], NE)
                    for j in range(3, 6):
                        conv_tile(j)
                    for j in range(2):
                        sp.dma_start(ring[:, 7 + j, :].rearrange("p (c n) -> p c n", c=4),
                                     A["w_out_conv"][0].rearrange("(c p) n -> p c n", p=P)[:, 4 * j:4 * j + 4, :]
                                     ).then_inc(ld_mix1[6 + j], 16)

                def first(n, u, i, l=l):
                    g, up, d = slots(l, u)
                    if l == 0 and u == 0:
                        sp.wait_ge(qkv_done, 6)
                        sp.wait_ge(y_done, DUOS)
                    load_g(l, n, g, ld_gu[l][u])
                    if l == 1 and u == 0:
                        sp.wait_ge(b_done, 4)
                    if l == 1 and u == 1:
                        sp.wait_ge(b_done, 8)
                    if l == 1 and u == 2:
                        sp.wait_ge(out1_done, 2)
                    if l == 0 and u == 2:
                        sp.wait_ge(out0_done, 2)
                    load_u(l, n, up, ld_gu[l][u])
                    if l == 0 and u == 1:
                        sp.wait_ge(gelu_ready, CHW)
                        sp.wait_ge(pv_done, 1)
                    load_dn(l, n, d, ld_down[l][u])
                    if l == 0 and u == 1:
                        sp.wait_ge(glu_done, CHW)

                def steady(n, u, i, l=l):
                    g, up, d = slots(l, u)
                    before(sp, ES[l]["gu_done"], n, LAG)
                    load_g(l, n, g, ld_gu[l][u])
                    load_u(l, n, up, ld_gu[l][u])
                    before(sp, ES[l]["down_done"], n, LAG)
                    load_dn(l, n, d, ld_down[l][u])

                passes(sp, first, steady, steady)

                if l == 0:
                    sp.wait_ge(ES[0]["gu_done"], NE - 2)
                    conv_tile(0)
                    sp.wait_ge(ES[0]["down_done"], NE - 2)
                    conv_tile(1)
                    sp.wait_ge(ES[0]["gu_done"], NE - 1)
                    conv_tile(2)
                sp.wait_ge(RS["route_ready"], l + 1)
                sp.wait_ge(ES[l]["down_done"], NE)

                def body(m, e, l=l):
                    before(sp, OS[l]["down_done"], m, 1)
                    load_g(l, e, OVER, ld_over[l])
                    load_u(l, e, OVER + 1, ld_over[l])
                    load_dn(l, e, OVER + 2, ld_over[l])

                count = sp.value_load(flag[0:1, 0:1], min_val=0, max_val=SEQ)
                with sp.If(count > CAP):
                    body(0, 0)
                    with sp.Fori(1, NE) as e:
                        body(e * (ROUNDS - 1), e)
                    sp.wait_ge(OS[l]["down_done"], NE * (ROUNDS - 1))
            for t in range(NT):
                sp.wait_ge(h_ready, 7 + t)
                sp.dma_start(out[0][t * P:(t + 1) * P, :], h[:, t, :]).then_inc(stored, 16)
            sp.wait_ge(stored, 16 * NT)

        @block.tensor
        def _(pe):
            def norm_turn(i):
                for j in range(4):
                    t, kh = j // 2, j % 2
                    if kh == 0:
                        pe.wait_ge(hn_ready, NT * i + t + 1)
                    for k in range(4):
                        last = pe.transpose(bank[turn_bank(i, j)][:, k * P:(k + 1) * P], hn_k[:, t, 4 * kh + k, :], ident)
                    last.then_inc(tp_done, 1)

            def route(l):
                s = RS
                for t in range(NT):
                    pe.wait_ge(hT_ready, 4 * (2 * l + 1) + 2 * t + 2)
                    for k in range(KD):
                        last = pe.matmul(bank[4][:, 36 * t:36 * t + 36], hT[:, k, t * P:(t + 1) * P],
                                         w_router[:, l, k, :], start=(k == 0), stop=(k == KD - 1))
                last.then_inc(s["logits"], 1)
                pe.wait_ge(s["chosen_ready"], l + 1)
                pe.matmul(bank[5][:, 0:NE], earlier, chosen[:, 0, :], start=True, stop=True)
                pe.matmul(bank[5][:, NE:2 * NE], ones, chosen[:, 0, :], start=True, stop=False)
                pe.matmul(bank[5][:, NE:2 * NE], earlier, chosen[:, 1, :], start=False, stop=True)
                pe.matmul(bank[5][:, 2 * NE:3 * NE], ones, chosen[:, 0, :], start=True, stop=False)
                pe.matmul(bank[5][:, 2 * NE:3 * NE], ones, chosen[:, 1, :], start=False, stop=True
                          ).then_inc(s["rank_done"], 1)

            def gather(S, n, b, e):
                pe.wait_ge(S["sel_ready"], n + 1)
                before(pe, S["dest_ready"], n, 1)
                for k in range(KD):
                    for t in range(NT):
                        pe.matmul(bank[2][:, k * CAP:(k + 1) * CAP], hn_k[:, t, k, :], sel[b][:, t, 0:CAP],
                                  start=(t == 0), stop=(t == NT - 1))
                for t in range(NT):
                    last = pe.matmul(bank[4][:, 0:4], sel[b][:, t, :], vals[:, t, bass.ds(e, 1), :],
                                     start=(t == 0), stop=(t == NT - 1))
                last.then_inc(S["gather_done"], 1)

            def gate_up(S, n, b, g):
                pe.wait_ge(S["xT_ready"], n + 1)
                before(pe, S["hid_ready"], n, 1)
                both = ring[:, g:g + 2, :].rearrange("p s (k n) -> p k s n", k=KD)
                for k in range(KD):
                    for half in range(2):
                        last = pe.matmul(bank[0][half * CAP:(half + 1) * CAP, :], xT[b][:, k, :],
                                         both[:, k, :, half * 256:half * 256 + 256],
                                         start=(k == 0), stop=(k == KD - 1))
                last.then_inc(S["gu_done"], 1)

            def turn(S, n, b):
                pe.wait_ge(S["hid_ready"], n + 1)
                before(pe, S["hidT_ready"], n, 1)
                for j in range(2):
                    last = pe.transpose(bank[3][:, j * P:(j + 1) * P],
                                        hid[b].rearrange("p (q b) -> p b q", b=2)[:, j, :], ident)
                last.then_inc(S["turn_done"], 1)

            def down(S, n, b, d):
                pe.wait_ge(S["hidT_ready"], n + 1)
                before(pe, S["y_ready"], n, 1)
                for c in range(4):
                    for half in range(2):
                        last = pe.matmul(bank[1][half * CAP:(half + 1) * CAP, :],
                                         hidT[b][:, c % 2, (c // 2) * CAP:(c // 2 + 1) * CAP],
                                         slot2(d)[:, c // 2, (c % 2) * D + half * 512:(c % 2) * D + half * 512 + 512],
                                         start=(c == 0), stop=(c == 3))
                last.then_inc(S["down_done"], 1)

            def experts(l):
                S = ES[l]
                pe.wait_ge(RS["route_ready"], l + 1)

                def step(n, u, i, more=True):
                    g, up, d = slots(l, u)
                    pe.wait_ge(ld_gu[l][u], (i + 1) * 32)
                    gate_up(S, n, u, g)
                    if more:
                        gather(S, n + 1, (u + 1) % LAG, n + 1)
                    turn(S, n, u)
                    pe.wait_ge(ld_down[l][u], (i + 1) * 16)
                    down(S, n, u, d)

                gather(S, 0, 0, 0)
                passes(pe, step, step, lambda n, u, i: step(n, u, i, n < NE - 1))

                O = OS[l]

                def body(m, e, r):
                    pe.wait_ge(ld_over[l], (e + 1) * 48)
                    gather(O, m, 0, e)
                    gate_up(O, m, 0, OVER)
                    turn(O, m, 0)
                    down(O, m, 0, OVER + 2)
                overflow(pe, body)

            pe.wait_ge(ld_const, 32)
            norm_turn(0)
            pe.wait_ge(hT_ready, 4)

            def project_u(m):
                j, c = (0, m) if m < 4 else (1, 0)
                w = ring[:, j, :].rearrange("p (k n) -> p k n", k=KD)
                pe.wait_ge(ld_mix0[j], 16)
                if m >= 2:
                    pe.wait_ge(u_copied, m - 1)
                for k in range(KD):
                    last = pe.matmul(bank[m % 2][:, 0:SEQ], w[:, k, c * P:(c + 1) * P], hT[:, k, :],
                                     start=(k == 0), stop=(k == KD - 1))
                last.then_inc(u_done, 1)

            def project_qkv(j):
                w3, t = j // 2, j % 2
                src = ((1, 128, 512), (2, 0, 384), (3, 0, 384))[w3]
                n = 512 if w3 == 0 else 384
                w = ring[:, src[0], 0:KD * n].rearrange("p (k n) -> p k n", k=KD)
                pe.wait_ge(ld_mix0[src[0]], 16)
                if j < 2:
                    pe.wait_ge(u_copied, 4 + j)
                else:
                    pe.wait_ge(qkv_copied, j - 1)
                for k in range(KD):
                    last = pe.matmul(bank[(1 + j) % 2][:, 0:ATT_W], hT[:, k, t * P:(t + 1) * P],
                                     w[:, k, src[1]:src[2]], start=(k == 0), stop=(k == KD - 1))
                last.then_inc(qkv_done, 1)

            def turn_qk():
                pe.wait_ge(qk_ready, 1)
                for j in range(3):
                    if j < 2:
                        pe.wait_ge(qkv_copied, 5 + j)
                    else:
                        pe.wait_ge(qkT_copied, 2)
                    for half in range(2):
                        ch = 2 * j + half
                        for t in range(NT):
                            last = pe.transpose(bank[(1 + j) % 2][:, (2 * half + t) * P:(2 * half + t + 1) * P],
                                                qkv[:, t, ch // 3, (ch % 3) * P:(ch % 3 + 1) * P], ident)
                    last.then_inc(qkT_done, 1)

            def scores(hh):
                r = 64 * (hh % 2)
                q, k = qkT[r:r + 64, hh // 2, :], qkT[r:r + 64, 3 + hh // 2, :]
                if hh == 0:
                    pe.wait_ge(qkT_copied, 6)
                if hh >= 2:
                    pe.wait_ge(score_copied, hh - 1)
                pe.matmul(bank[hh % 2][:, 0:P], q[:, 0:P], k[:, 0:P], start=True, stop=True)
                pe.matmul(bank[hh % 2][:, P:P + SEQ], q[:, P:SEQ], k, start=True, stop=True).then_inc(score_done, 1)

            def drive(d):
                if d == 0:
                    pe.wait_ge(ld_b, 16)
                if d % 2 == 0:
                    pe.wait_ge(u_copied, d // 2 + 1)
                if d >= 2:
                    pe.wait_ge(bu_used, d - 1)
                for c in range(2):
                    for i in (2 * d, 2 * d + 1):
                        r = 32 * (i % 4)
                        last = pe.matmul(bank[4 + i % 4][:, c * SEQ:(c + 1) * SEQ], ssm_b[r:r + 32, c, i // 4, :],
                                         uT[r:r + 32, i // 4, :], start=True, stop=True)
                last.then_inc(bu_done, 1)

            def readout(d):
                c, b = d // 2, d % 2
                if d == 0:
                    pe.wait_ge(c_ready, 1)
                pe.wait_ge(q_ready, d + 1)
                if c >= 2 and b == 0:
                    pe.wait_ge(ypre_ready, c - 1)
                terms = ((ssm_c[:, 0], qc[b], 0), (ssm_cb, qs[b], 1), (ssm_c[:, 1], qs[b], 0), (ssm_c[:, 1], qc[b], 1))
                for n, (w, q, part) in enumerate(terms):
                    for x, i in enumerate((2 * d, 2 * d + 1)):
                        r = 32 * (i % 4)
                        last = pe.matmul(bank[2 + c % 2][r:r + 32, 0:SEQ], w[:, i, :], q[:, x, part, :],
                                         start=(n == 0), stop=(n == 3))
                last.then_inc(y_done, 1)

            project_u(0)
            drive(0)
            drive(1)
            for d in range(DUOS):
                if d == 0:
                    project_u(1)
                elif d == 1:
                    project_u(2)
                    project_u(3)
                elif d == 2:
                    project_u(4)
                elif d < 9:
                    project_qkv(d - 3)
                else:
                    turn_qk()
                    for hh in range(HEADS):
                        scores(hh)
                if d + 2 < DUOS:
                    drive(d + 2)
                readout(d)

            GLU_BANK = (4, 5, 6, 7, 3)
            pe.wait_ge(ld_mix0[4], 16)
            pe.wait_ge(bu_used, DUOS)
            pe.wait_ge(ypre_ready, CHW - 1)
            wg = ring[:, 0, 0:CHW * SSM_W].rearrange("p (c n) -> p c n", c=CHW)
            for c in range(CHW):
                pe.wait_ge(gelu_ready, c + 1)
                for m in range(CHW):
                    last = pe.matmul(bank[GLU_BANK[m]][:, 0:SEQ], wg[:, c, m * P:(m + 1) * P], yT[:, c, :],
                                     start=(c == 0), stop=(c == CHW - 1))
                    if c == CHW - 1:
                        last.then_inc(glu_done, 1)
            pe.wait_ge(prob_ready, 1)
            pe.wait_ge(ypre_ready, CHW)
            for hh in range(HEADS):
                if hh >= 3:
                    pe.wait_ge(pT_copied, hh - 2)
                for j in range(3):
                    last = pe.transpose(bank[hh % 3][:, j * P:(j + 1) * P], prob[:, hh, j * P:(j + 1) * P], ident)
                last.then_inc(pT_done, 1)
            pe.wait_ge(pT_copied, HEADS)
            for hh in range(HEADS):
                r, c = 64 * (hh % 2), hh // 2
                o = bank[c][r:r + 64, 0:SEQ]
                pe.matmul(o, qkv[:, 0, 2, hh * HD:(hh + 1) * HD], probT[:, hh, 0:SEQ], start=True, stop=False)
                last = pe.matmul(o[:, P:SEQ], qkv[:, 1, 2, hh * HD:(hh + 1) * HD], probT[:, hh, SEQ:SEQ + P],
                                 start=False, stop=True)
            last.then_inc(pv_done, 1)
            for part, chunks in enumerate(((5, 6, 7), range(CHW))):
                for t in range(NT):
                    for c in chunks:
                        if part == 0 and t == 0 and c == 5:
                            pe.wait_ge(ld_mix0[6], 16)
                            pe.wait_ge(att_ready, 1)
                            pe.wait_ge(gate_ready, CHW)
                        if part == 1 and t == 0:
                            if c == 0:
                                pe.wait_ge(ld_mix0[5], 16)
                            pe.wait_ge(ssm_ready, c + 1)
                        w = ring[:, 1 + c // 4, :].rearrange("p (c n) -> p c n", c=4)
                        for n in range(2):
                            last = pe.matmul(bank[2 - 2 * t + n][:, :], mixT[:, c, t * P:(t + 1) * P],
                                             w[:, c % 4, n * 512:(n + 1) * 512], start=(c == 5), stop=(c == 4))
                    if part == 1:
                        last.then_inc(out0_done, 1)
            norm_turn(1)
            pe.wait_ge(ld_route, 48)
            route(0)
            experts(0)

            norm_turn(2)
            pe.wait_ge(hT_ready, 12)
            for m in range(KD):
                half, c = m // 4, m % 4
                for part in range(3):
                    pe.wait_ge(ld_mix1[3 * half + part], 32)
                    if part != 1 and m >= 2:
                        pe.wait_ge(g_ready, m - 1)
                    o = bank[4 + m % 2][:, part * 256:part * 256 + 256] if part < 2 else bank[6 + m % 2][:, 0:256]
                    w = ring[:, 1 + 3 * half + part, :].rearrange("p (k n) -> p k n", k=KD)
                    for k in range(KD):
                        last = pe.matmul(o, w[:, k, c * P:(c + 1) * P], hT[:, k, :], start=(k == 0), stop=(k == KD - 1))
                    if part > 0:
                        last.then_inc(cz_done if part == 1 else b_done, 1)
            for t in range(NT):
                for c in range(KD):
                    if t == 0:
                        if c % 4 == 0:
                            pe.wait_ge(ld_mix1[6 + c // 4], 16)
                        pe.wait_ge(g_ready, c + 1)
                    w = ring[:, 7 + c // 4, :].rearrange("p (c n) -> p c n", c=4)
                    for n in range(2):
                        last = pe.matmul(bank[2 * t + n][:, :], mixT[:, c, t * P:(t + 1) * P],
                                         w[:, c % 4, n * 512:(n + 1) * 512], start=(c == 0), stop=(c == KD - 1))
                last.then_inc(out1_done, 1)
            norm_turn(3)
            route(1)
            experts(1)

        @block.vector
        def _(dve):
            def norm_rows(i, t):
                dve.wait_ge(squares, NT * i + t + 1)
                dve.tensor_scalar(norm_s[:, 1, t:t + 1], norm_s[:, 0, t:t + 1], 1.0 / D, EPS, ALU.mult, ALU.add
                                  ).then_inc(mean, 1)
                dve.wait_ge(root, NT * i + t + 1)
                dve.reciprocal(norm_s[:, 3, t:t + 1], norm_s[:, 2, t:t + 1])
                dve.drain()
                dve.tensor_scalar(hn[:, t, :], h[:, t, :], norm_s[:, 3, t:t + 1], None, ALU.mult).then_inc(hn_ready, 1)

            def norm_turned(i):
                for j in range(4):
                    t, kh = j // 2, j % 2
                    dve.wait_ge(tp_done, 4 * i + j + 1)
                    dve.tensor_tensor(hT[:, 4 * kh:4 * kh + 4, t * P:(t + 1) * P],
                                      bank[turn_bank(i, j)][:, :].rearrange("p (k q) -> p k q", k=4),
                                      gains[:, i, 4 * kh:4 * kh + 4].unsqueeze(2).to_broadcast([P, 4, P]),
                                      ALU.mult).then_inc(hT_ready, 1)

            def residual(i, done, banks):
                for t in range(NT):
                    dve.wait_ge(done, t + 1)
                    for n in range(2):
                        last = dve.tensor_tensor(h[:, t, n * 512:(n + 1) * 512], h[:, t, n * 512:(n + 1) * 512],
                                                 bank[banks[t] + n][:, :], ALU.add)
                    last.then_inc(h_ready, 1)
                    dve.drain()
                    norm_rows(i, t)

            def route(l):
                s = RS
                dve.memset(gl8, NEG)
                dve.wait_ge(s["logits"], l + 1)
                dve.tensor_tensor(lg, bank[4][:, 0:72].rearrange("p (t n) -> p t n", t=NT),
                                  b_router[:, l, :].unsqueeze(1).to_broadcast([P, NT, GROUPS + NE]), ALU.add)
                dve.drain()
                dve.tensor_copy(gl8[:, :, 0:GROUPS], lg[:, :, 0:GROUPS])
                dve.drain()
                for t in range(NT):
                    dve.max(gm8[:, t, :], gl8[:, t, :])
                dve.drain()
                for t in range(NT):
                    dve.max_index(gi8[:, t, :], gm8[:, t, :], gl8[:, t, :])
                dve.tensor_tensor(ge, gl8[:, :, 0:GROUPS], gm8[:, :, 0:1].to_broadcast([P, NT, GROUPS]),
                                  ALU.subtract).then_inc(s["gshift"], 1)
                dve.drain()
                dve.tensor_copy(gif, gi8[:, :, 0:1])
                dve.drain()
                dve.tensor_tensor(mask, cst[:, C_G32:C_G32 + NE].unsqueeze(1).to_broadcast([P, NT, NE]),
                                  gif.to_broadcast([P, NT, NE]), ALU.is_equal)
                dve.drain()
                dve.tensor_tensor(el, lg[:, :, GROUPS:], mask, ALU.mult)
                dve.tensor_scalar(rtmp, mask, -NEG, NEG, ALU.mult, ALU.add)
                dve.drain()
                dve.tensor_tensor(el, el, rtmp, ALU.add)
                dve.drain()
                for t in range(NT):
                    dve.max(tm8[:, t, :], el[:, t, :])
                dve.drain()
                for t in range(NT):
                    dve.max_index(ti8[:, t, :], tm8[:, t, :], el[:, t, :])
                dve.tensor_tensor(ex.unsqueeze(2), tm8[:, :, 1:2], tm8[:, :, 0:1], ALU.subtract
                                  ).then_inc(s["eshift"], 1)
                dve.drain()
                dve.tensor_copy(tif, ti8[:, :, 0:2])
                dve.drain()
                for k in range(2):
                    dve.tensor_tensor(oh[k], cst[:, C_E32:C_E32 + NE].unsqueeze(1).to_broadcast([P, NT, NE]),
                                      tif[:, :, k:k + 1].to_broadcast([P, NT, NE]), ALU.is_equal)
                dve.drain()
                dve.tensor_tensor(chosen, oh[0], oh[1], ALU.add).then_inc(s["chosen_ready"], 1)
                dve.wait_ge(s["gexp"], l + 1)
                dve.wait_ge(s["eexp"], l + 1)
                dve.tensor_reduce(gw, ge, AX.X, ALU.add)
                dve.tensor_scalar(den, ex, 1.0, None, ALU.add)
                dve.drain()
                dve.tensor_tensor(den, den, gw, ALU.mult)
                dve.drain()
                dve.reciprocal(wt[:, 0, :], den)
                dve.drain()
                dve.tensor_tensor(wt[:, 1, :], wt[:, 0, :], ex, ALU.mult)
                dve.drain()
                dve.tensor_tensor(vals[:, :, :, 0], oh[1],
                                  cst[:, C_TOK2:C_TOK2 + NT].unsqueeze(2).to_broadcast([P, NT, NE]), ALU.add)
                dve.tensor_tensor(oh[0], oh[0], wt[:, 0, :].unsqueeze(2).to_broadcast([P, NT, NE]), ALU.mult)
                dve.drain()
                dve.tensor_tensor(oh[1], oh[1], wt[:, 1, :].unsqueeze(2).to_broadcast([P, NT, NE]), ALU.mult)
                dve.memset(vals[:, :, :, 2:4], 1.0)
                dve.drain()
                dve.tensor_tensor(vals[:, :, :, 1], oh[0], oh[1], ALU.add)
                dve.tensor_scalar(rtmp, chosen, 1000.0, -1000.0, ALU.mult, ALU.add)
                dve.wait_ge(s["rank_done"], l + 1)
                dve.tensor_tensor(rank, bank[5][:, 0:2 * NE].rearrange("p (t n) -> p t n", t=NT), chosen, ALU.mult)
                dve.tensor_reduce(cmax, bank[5][:, 2 * NE:3 * NE], AX.X, ALU.max)
                dve.drain()
                dve.tensor_tensor(rank, rank, rtmp, ALU.add)
                dve.tensor_copy(flag[:, :], cmax)
                dve.drain()
                dve.nop().then_inc(s["route_ready"], 1)

            def select(S, n, b, e, r, lag):
                before(dve, S["gather_done"], n, lag)
                for t in range(NT):
                    last = dve.tensor_scalar(sel[b][:, t, :], iota, float(CAP * r), rank[:, t, bass.ds(e, 1)],
                                             ALU.add, ALU.is_equal)
                last.then_inc(S["sel_ready"], 1)

            def hidden(S, n, b):
                dve.wait_ge(S["silu_ready"], n + 1)
                dve.tensor_tensor(hid[b], hid[b], bank[0][:, 256:512], ALU.mult).then_inc(S["hid_ready"], 1)

            def gathered(S, n, b, l, lag):
                dve.wait_ge(S["gather_done"], n + 1)
                before(dve, S["gu_done"], n, lag)
                dve.tensor_tensor(xT[b], bank[2][:, :].rearrange("p (k j) -> p k j", k=KD),
                                  gains[:, 2 * l + 1, :].unsqueeze(2).to_broadcast([P, KD, CAP]), ALU.mult
                                  ).then_inc(S["xT_ready"], 1)
                before(dve, S["y_ready"], n, lag)
                before(dve, S["dest_made"], n, lag)
                dve.tensor_copy(rowv[b], bank[4][:, 0:4])
                dve.drain()
                dve.tensor_scalar(row_at[:, 2 * b:2 * b + 1], rowv[b][:, 0:1], 2.0, None, ALU.mult)
                dve.tensor_scalar(row_at[:, 2 * b + 1:2 * b + 2], rowv[b][:, 2:3], -FAR, cst[:, C_FAR:C_FAR + 1],
                                  ALU.mult, ALU.add)
                dve.drain()
                dve.nop().then_inc(S["dest_ready"], 1)

            def experts(l):
                S = ES[l]

                def step(n, u, i, more=True):
                    v = (u + 1) % LAG
                    if more:
                        select(S, n + 1, v, n + 1, 0, LAG)
                    hidden(S, n, u)
                    if more:
                        gathered(S, n + 1, v, l, LAG)

                select(S, 0, 0, 0, 0, LAG)
                gathered(S, 0, 0, l, LAG)
                passes(dve, step, step, lambda n, u, i: step(n, u, i, n < NE - 1))

                O = OS[l]

                def body(m, e, r):
                    select(O, m, 0, e, r, 1)
                    gathered(O, m, 0, l, 1)
                    hidden(O, m, 0)
                dve.wait_ge(ES[l]["down_done"], NE)
                for b in range(LAG):
                    dve.wait_ge(scattered[l][b], 16 * ((NE - b + LAG - 1) // LAG))
                overflow(dve, body)

            def combined(l):
                for t in range(NT):
                    dve.wait_ge(combine_ld[l][t], 16)
                    dve.tensor_tensor(h[:, t, :], h[:, t, :], combine[:, t, 0, :], ALU.add)
                    dve.drain()
                    dve.tensor_tensor(h[:, t, :], h[:, t, :], combine[:, t, 1, :], ALU.add).then_inc(h_ready, 1)
                    dve.drain()
                    if l == 0 and t == 1:
                        norm_rows(2, 0)
                        norm_rows(2, 1)

            names = ("step", "xr", "th", "k", "r", "t0", "w16", "cr", "ci", "lr", "li", "n0", "n1", "n2", "cs", "sn")
            V = {n: sml[:, j, :] for j, n in enumerate(names)}
            a_re, a_im = ssm_p[:, 0, :], ssm_p[:, 1, :]
            dve.wait_ge(ld_p, 16)
            dve.wait_ge(expd, 1)
            dve.tensor_tensor(V["xr"], a_re, V["step"], ALU.mult).then_inc(lam_ready, 1)
            dve.tensor_tensor(V["th"], a_im, V["step"], ALU.mult)
            dve.drain()

            def rint(o, i):
                dve.tensor_scalar(o, i, RINT, -RINT, ALU.add, ALU.add)
                dve.drain()

            dve.tensor_scalar(V["k"], V["th"], 1.0 / (2.0 * math.pi), None, ALU.mult)
            dve.drain()
            rint(V["k"], V["k"])
            dve.scalar_tensor_tensor(out=V["th"], in0=V["k"], scalar=-TWO_PI_HI, in1=V["th"], op0=ALU.mult, op1=ALU.add)
            dve.drain()
            dve.scalar_tensor_tensor(out=V["th"], in0=V["k"], scalar=-TWO_PI_LO, in1=V["th"], op0=ALU.mult, op1=ALU.add)
            dve.drain()
            dve.tensor_scalar(V["th"], V["th"], 1.0 / (2.0 * math.pi), None, ALU.mult).then_inc(turn_ready, 1)
            dve.drain()
            dve.tensor_scalar(V["w16"], V["th"], 16.0, None, ALU.mult)
            dve.drain()
            rint(V["t0"], V["w16"])
            dve.tensor_tensor(V["w16"], V["w16"], V["t0"], ALU.subtract)
            dve.drain()
            norm_rows(0, 0)
            norm_rows(0, 1)
            dve.wait_ge(ld_const, 32)
            i16 = cst[:, C_I16:C_I16 + 16].unsqueeze(1).to_broadcast([P, PAIRS, 16])
            for dst, w in ((alpha, V["w16"]), (beta, V["th"])):
                dve.tensor_tensor(dst, i16, w.unsqueeze(2).to_broadcast([P, PAIRS, 16]), ALU.mult)
                dve.drain()
                rint(whole, dst)
                dve.tensor_tensor(dst, dst, whole, ALU.subtract)
                dve.drain()
            dve.scalar_tensor_tensor(out=alpha, in0=alpha, scalar=0.0, in1=alpha, op0=ALU.is_lt, op1=ALU.add)
            dve.drain()
            dve.nop().then_inc(ab_ready, 1)

            def add_turns(c):
                angle_sum(dve, c)
                dve.drain()

            def angle(c):
                if c >= 2:
                    dve.wait_ge(pool_added, c - 1)
                a = sin_t[:, 4 * c:4 * c + 4, :]
                dve.scalar_tensor_tensor(out=a, in0=a, scalar=0.5, in1=a, op0=ALU.is_ge, op1=ALU.subtract
                                         ).then_inc(angle_ready, 1)

            add_turns(0)
            angle(0)
            norm_turned(0)
            add_turns(1)
            for c in range(1, CHW):
                angle(c)

            def fold_c():
                dve.wait_ge(pole_ready, 1)
                dve.tensor_tensor(V["lr"], V["r"], V["cs"], ALU.mult)
                dve.tensor_tensor(V["li"], V["r"], V["sn"], ALU.mult)
                dve.tensor_tensor(V["n0"], a_re, a_re, ALU.mult)
                dve.tensor_tensor(V["n1"], a_im, a_im, ALU.mult)
                dve.drain()
                dve.tensor_scalar(V["lr"], V["lr"], -1.0, None, ALU.add)
                dve.tensor_tensor(V["n0"], V["n0"], V["n1"], ALU.add)
                dve.drain()
                dve.reciprocal(V["n2"], V["n0"])
                dve.tensor_tensor(V["cr"], V["lr"], a_re, ALU.mult)
                dve.tensor_tensor(V["n1"], V["li"], a_im, ALU.mult)
                dve.tensor_tensor(V["ci"], V["li"], a_re, ALU.mult)
                dve.tensor_tensor(V["t0"], V["lr"], a_im, ALU.mult)
                dve.drain()
                dve.tensor_tensor(V["cr"], V["cr"], V["n1"], ALU.add)
                dve.tensor_tensor(V["ci"], V["ci"], V["t0"], ALU.subtract)
                dve.drain()
                dve.tensor_tensor(V["cr"], V["cr"], V["n2"], ALU.mult)
                dve.tensor_tensor(V["ci"], V["ci"], V["n2"], ALU.mult)
                dve.drain()
                cr = V["cr"].unsqueeze(2).to_broadcast([P, PAIRS, 32])
                ci = V["ci"].unsqueeze(2).to_broadcast([P, PAIRS, 32])
                dve.wait_ge(ld_c, 32)
                dve.tensor_tensor(c_tmp[0], ssm_c[:, 0], cr, ALU.mult)
                dve.tensor_tensor(c_tmp[1], ssm_c[:, 1], ci, ALU.mult)
                dve.tensor_tensor(c_tmp[2], ssm_c[:, 0], ci, ALU.mult)
                dve.drain()
                dve.tensor_tensor(ssm_c[:, 0], c_tmp[0], c_tmp[1], ALU.subtract)
                dve.tensor_tensor(ssm_cb, c_tmp[1], c_tmp[0], ALU.subtract)
                dve.drain()
                dve.tensor_tensor(c_tmp[0], ssm_c[:, 1], cr, ALU.mult)
                dve.drain()
                dve.scalar_tensor_tensor(out=ssm_c[:, 1], in0=c_tmp[2], scalar=-1.0, in1=c_tmp[0], op0=ALU.mult,
                                         op1=ALU.subtract)
                dve.drain()
                dve.nop().then_inc(c_ready, 1)

            def skip_added(c):
                dve.wait_ge(y_done, 2 * c + 2)
                if c >= 2:
                    dve.wait_ge(gelu_ready, c - 1)
                dve.scalar_tensor_tensor(out=ypre[:, c % 2, :], in0=uT[:, c, :], scalar=d_bglu[:, 0, c:c + 1],
                                         in1=bank[2 + c % 2][:, 0:SEQ], op0=ALU.mult, op1=ALU.add
                                         ).then_inc(ypre_ready, 1)

            qk = qkv[:, :, 0:2, :].rearrange("p t w c -> p t (w c)")
            NH2 = 2 * HEADS
            ss = att_s[:, 0:24].rearrange("p (t n) -> p t n", t=NT)
            rs = att_s[:, 24:48].rearrange("p (t n) -> p t n", t=NT)
            nmax = att_s[:, 48:60].rearrange("p (t n) -> p t n", t=NT)
            lsum = att_s[:, 60:72].rearrange("p (t n) -> p t n", t=NT)

            def qk_squares():
                dve.wait_ge(qkv_copied, 4)
                dve.tensor_tensor(sq, qk, qk, ALU.mult)
                dve.drain()
                for t in range(NT):
                    dve.tensor_reduce(ss[:, t, :], sq[:, t, :].rearrange("p (n e) -> p n e", e=HD), AX.X, ALU.add)
                dve.drain()
                dve.tensor_scalar(ss, ss, 1.0 / HD, EPS, ALU.mult, ALU.add).then_inc(qk_mean, 1)

            def qk_normed():
                dve.wait_ge(qk_root, 1)
                dve.reciprocal(rs, rs)
                dve.drain()
                dve.tensor_scalar(rs[:, :, 0:HEADS], rs[:, :, 0:HEADS], HD ** -0.5, None, ALU.mult)
                dve.drain()
                for t in range(NT):
                    v3 = qk[:, t, :].rearrange("p (n e) -> p n e", e=HD)
                    last = dve.tensor_tensor(v3, v3, rs[:, t, :].unsqueeze(2).to_broadcast([P, NH2, HD]), ALU.mult)
                last.then_inc(qk_ready, 1)

            for d in range(DUOS):
                b = d % 2
                bu = psum[:, 4 + 2 * b:6 + 2 * b, :].rearrange("p i (c t) -> p i c t", c=2)
                rot = [x[:, 2 * d:2 * d + 2, :].unsqueeze(2).to_broadcast([P, 2, 2, SEQ]) for x in (cos_t, sin_t)]
                dve.wait_ge(table_ready, 2 * (d // 2) + 2)
                dve.wait_ge(bu_done, d + 1)
                if d >= 2:
                    dve.wait_ge(q_ready, d - 1)
                dve.tensor_tensor(zz[b], bu, rot[0], ALU.mult)
                dve.tensor_tensor(m2, bu, rot[1], ALU.mult).then_inc(bu_used, 1)
                dve.drain()
                dve.tensor_tensor(zz[b][:, :, 0, :], zz[b][:, :, 0, :], m2[:, :, 1, :], ALU.add)
                dve.tensor_tensor(zz[b][:, :, 1, :], zz[b][:, :, 1, :], m2[:, :, 0, :], ALU.subtract)
                dve.drain()
                if d == 0:
                    dve.wait_ge(r_ready, 1)
                for x in range(2):
                    i = 2 * d + x
                    for c in range(2):
                        last = dve.tensor_tensor_scan(zz[b][:, x, c, :], V["r"][:, i:i + 1].to_broadcast([P, SEQ]),
                                                      zz[b][:, x, c, :], 0.0, ALU.mult, ALU.add)
                last.then_inc(z_ready, 1)
                if d == 0:
                    fold_c()
                if d >= 2 and d % 2 == 0:
                    skip_added(d // 2 - 1)
                if d == 7:
                    qk_squares()
                if d == 8:
                    qk_normed()

            dve.wait_ge(ld_att, 32)
            for hh in range(HEADS):
                dve.wait_ge(score_done, hh + 1)
                dve.tensor_tensor(prob[:, hh, :], bank[hh % 2][:, 0:P + SEQ], prob[:, hh, :], ALU.add
                                  ).then_inc(score_copied, 1)
            dve.drain()
            cols = ((0, P), (P, P + SEQ))
            for t, (a, b) in enumerate(cols):
                dve.tensor_reduce(nmax[:, t, :], prob[:, :, a:b], AX.X, ALU.max)
            dve.drain()
            dve.tensor_scalar(nmax, nmax, -1.0, None, ALU.mult).then_inc(max_ready, 1)
            skip_added(CHW - 1)
            dve.wait_ge(exp_done, 2 * HEADS)
            dve.reciprocal(lsum, lsum)
            dve.drain()
            for t, (a, b) in enumerate(cols):
                last = dve.tensor_tensor(prob[:, :, a:b], prob[:, :, a:b],
                                         lsum[:, t, :].unsqueeze(2).to_broadcast([P, HEADS, b - a]), ALU.mult)
            last.then_inc(prob_ready, 1)
            for hh in range(HEADS):
                dve.wait_ge(pT_done, hh + 1)
                dve.tensor_copy(probT[:, hh, :], bank[hh % 3][:, 0:P + SEQ]).then_inc(pT_copied, 1)
            for m in range(CHW):
                dve.wait_ge(gate_ready, m + 1)
                dve.tensor_tensor(mixT[:, m, :], yT[:, m, :], glu[:, m, :], ALU.mult).then_inc(ssm_ready, 1)
            dve.wait_ge(pv_done, 1)
            dve.tensor_copy(mixT[:, 5:8, :], psum[:, 0:3, 0:SEQ]).then_inc(att_ready, 1)
            residual(1, out0_done, (2, 0))
            norm_turned(1)
            dve.wait_ge(ld_route, 48)
            route(0)
            experts(0)
            combined(0)

            norm_turned(2)
            dve.memset(zc, 0.0)
            dve.drain()
            for m in range(KD):
                b = m % 2
                dve.wait_ge(z_copied, m + 1)
                dve.tensor_tensor(zc[:, b, 2:], bank[4 + b][:, 0:SEQ], z_sb[:, b, :], ALU.mult)
                dve.drain()
                dve.tensor_scalar(cv[:, b, :], zc[:, b, 2:], conv_taps[:, m, 2:3], None, ALU.mult)
                dve.drain()
                for tap in (1, 0):
                    dve.scalar_tensor_tensor(out=cv[:, b, :], in0=zc[:, b, tap:tap + SEQ],
                                             scalar=conv_taps[:, m, tap:tap + 1], in1=cv[:, b, :],
                                             op0=ALU.mult, op1=ALU.add)
                    dve.drain()
                dve.wait_ge(b_done, m + 1)
                dve.tensor_tensor(mixT[:, m, :], cv[:, b, :], bank[6 + b][:, 0:SEQ], ALU.mult).then_inc(g_ready, 1)
            residual(3, out1_done, (0, 2))
            norm_turned(3)
            route(1)
            experts(1)
            combined(1)

        @block.scalar
        def _(act):
            def norm_tile(i, t):
                if i == 0:
                    act.wait_ge(ld_x[t], 16)
                else:
                    act.wait_ge(h_ready, NT * i + t - 1)
                act.activation(hn[:, t, :], h[:, t, :], ACT.Square, accum_out=norm_s[:, 0, t:t + 1])
                act.drain()
                act.nop().then_inc(squares, 1)
                act.wait_ge(mean, NT * i + t + 1)
                act.activation(norm_s[:, 2, t:t + 1], norm_s[:, 1, t:t + 1], ACT.Sqrt).then_inc(root, 1)

            def norm(i):
                for t in range(NT):
                    norm_tile(i, t)

            def route(l):
                s = RS
                act.wait_ge(s["gshift"], l + 1)
                act.activation(ge, ge, ACT.Exp).then_inc(s["gexp"], 1)
                act.wait_ge(s["eshift"], l + 1)
                act.activation(ex, ex, ACT.Exp).then_inc(s["eexp"], 1)

            def silu(S, n, b, lag):
                act.wait_ge(S["gu_done"], n + 1)
                before(act, S["turn_done"], n, lag)
                act.activation(hid[b], bank[0][:, 0:256], ACT.Silu).then_inc(S["silu_ready"], 1)

            def turned(S, n, b, lag):
                act.wait_ge(S["turn_done"], n + 1)
                before(act, S["down_done"], n, lag)
                act.activation(hidT[b].rearrange("p b j -> p (b j)"), bank[3][:, 0:256], ACT.Copy
                               ).then_inc(S["hidT_ready"], 1)

            def weigh(S, n, b, scat, scat_n):
                act.wait_ge(S["down_done"], n + 1)
                act.wait_ge(S["dest_ready"], n + 1)
                if scat_n is not None:
                    act.wait_ge(scat, scat_n)
                act.activation(yrow[b], bank[1][:, :], ACT.Copy, scale=rowv[b][:, 1:2]).then_inc(S["y_ready"], 1)

            def experts(l):
                S = ES[l]

                def step(n, u, i):
                    silu(S, n, u, LAG)
                    turned(S, n, u, LAG)
                    weigh(S, n, u, scattered[l][u], None if isinstance(i, int) and i == 0 else i * 16)
                passes(act, step, step, step)
                O = OS[l]

                def body(m, e, r):
                    silu(O, m, 0, 1)
                    turned(O, m, 0, 1)
                    weigh(O, m, 0, over_scattered[l], None if isinstance(m, int) and m == 0 else m * 16)
                overflow(act, body)

            act.wait_ge(ld_p, 16)
            act.activation(sml[:, 0, :], ssm_p[:, 2, :], ACT.Exp).then_inc(expd, 1)
            act.wait_ge(lam_ready, 1)
            act.activation(sml[:, 4, :], sml[:, 1, :], ACT.Exp).then_inc(r_ready, 1)
            norm(0)
            half_pi = cst[:, C_HPI:C_HPI + 1]
            act.wait_ge(ld_const, 32)
            act.wait_ge(turn_ready, 1)
            act.activation(sml[:, 14, :], sml[:, 2, :], ACT.Abs)
            act.activation(sml[:, 15, :], sml[:, 2, :], ACT.Sin, scale=TURN)
            act.drain()
            act.activation(sml[:, 14, :], sml[:, 14, :], ACT.Sin, scale=-TURN, bias=half_pi).then_inc(pole_ready, 1)

            def tables(c):
                cs, sn = cos_t[:, 4 * c:4 * c + 4, :], sin_t[:, 4 * c:4 * c + 4, :]
                act.wait_ge(angle_ready, c + 1)
                act.activation(cs, sn, ACT.Abs)
                act.drain()
                act.activation(cs, cs, ACT.Sin, scale=-TURN, bias=half_pi).then_inc(table_ready, 1)
                act.activation(sn, sn, ACT.Sin, scale=-TURN).then_inc(table_ready, 1)

            def u_copy(m):
                act.wait_ge(u_done, m + 1)
                act.activation(uT[:, m, :], bank[m % 2][:, 0:SEQ], ACT.Copy).then_inc(u_copied, 1)

            def qkv_copy(j):
                act.wait_ge(qkv_done, j + 1)
                act.activation(qkv[:, j % 2, j // 2, :], bank[(1 + j) % 2][:, 0:ATT_W], ACT.Copy).then_inc(qkv_copied, 1)

            def gelu(c):
                act.wait_ge(ypre_ready, c + 1)
                act.activation(yT[:, c, :], ypre[:, c % 2, :], ACT.Gelu_apprx_tanh).then_inc(gelu_ready, 1)

            tables(0)
            u_copy(0)
            tables(1)
            u_copy(1)
            tables(2)
            u_copy(2)
            u_copy(3)
            tables(3)
            tables(4)
            u_copy(4)
            gelu(0)
            qkv_copy(0)
            qkv_copy(1)
            gelu(1)
            qkv_copy(2)
            qkv_copy(3)
            gelu(2)
            qkv_copy(4)
            act.wait_ge(qk_mean, 1)
            act.activation(att_s[:, 24:48], att_s[:, 0:24], ACT.Sqrt).then_inc(qk_root, 1)
            qkv_copy(5)
            gelu(3)
            act.wait_ge(ld_att, 32)
            for ch in range(2 * QCH):
                act.wait_ge(qkT_done, ch // 2 + 1)
                act.activation(qkT[:, ch, :], bank[(1 + ch // 2) % 2][:, (ch % 2) * SEQ:(ch % 2) * SEQ + SEQ],
                               ACT.Copy, scale=qk_gain[:, ch // QCH:ch // QCH + 1]).then_inc(qkT_copied, 1)
            act.wait_ge(max_ready, 1)
            for hh in range(HEADS):
                for t, (a, b) in enumerate(((0, P), (P, P + SEQ))):
                    n = t * HEADS + hh
                    act.activation(prob[:, hh, a:b], prob[:, hh, a:b], ACT.Exp, bias=att_s[:, 48 + n:49 + n],
                                   accum_out=att_s[:, 60 + n:61 + n]).then_inc(exp_done, 1)
            gelu(4)
            for m in range(CHW):
                act.wait_ge(glu_done, m + 1)
                act.activation(glu[:, m, :], bank[(4, 5, 6, 7, 3)[m]][:, 0:SEQ], ACT.Sigmoid, bias=d_bglu[:, 1, m:m + 1]
                               ).then_inc(gate_ready, 1)
            norm(1)
            route(0)
            experts(0)
            norm(2)
            for m in range(KD):
                act.wait_ge(cz_done, m + 1)
                if m >= 2:
                    act.wait_ge(g_ready, m - 1)
                act.activation(z_sb[:, m % 2, :], bank[4 + m % 2][:, SEQ:2 * SEQ], ACT.Copy).then_inc(z_copied, 1)
            norm(3)
            route(1)
            experts(1)

        @block.gpsimd
        def _(pool):
            pool.wait_ge(ab_ready, 1)
            for c in range(2, CHW):
                angle_sum(pool, c).then_inc(pool_added, 1)
            for d in range(DUOS):
                b = d % 2
                rot = [x[:, 2 * d:2 * d + 2, :].unsqueeze(2).to_broadcast([P, 2, 2, SEQ]) for x in (cos_t, sin_t)]
                pool.wait_ge(z_ready, d + 1)
                if d >= 2:
                    pool.wait_ge(y_done, d - 1)
                pool.tensor_tensor(qc[b], zz[b], rot[0], ALU.mult)
                pool.tensor_tensor(qs[b], zz[b], rot[1], ALU.mult).then_inc(q_ready, 1)

            def scatter(l, S, n, b, done):
                pool.wait_ge(S["y_ready"], n + 1)
                pool.tensor_tensor(dest[:, b:b + 1], row_at[:, 2 * b:2 * b + 1], row_at[:, 2 * b + 1:2 * b + 2],
                                   ALU.add).then_inc(S["dest_made"], 1)
                pool.drain()
                pool.indirect_dma_start(rows_dram[l], bass.IndirectOffsetOnAxis(ap=dest[:, b:b + 1], axis=0),
                                        yrow[b], None, bounds_check=4 * SEQ - 1, oob_is_err=False).then_inc(done, 16)

            for l in range(LAYERS):
                step = lambda n, u, i, l=l: scatter(l, ES[l], n, u, scattered[l][u])
                passes(pool, step, step, step)
                for b in range(LAG):
                    pool.wait_ge(scattered[l][b], 16 * ((NE - b + LAG - 1) // LAG))
                pool.wait_ge(RS["route_ready"], l + 1)
                count = pool.value_load(flag[0:1, 0:1], min_val=0, max_val=SEQ)
                with pool.If(count > CAP):
                    for r in range(ROUNDS - 1):
                        scatter(l, OS[l], r, 0, over_scattered[l])
                    with pool.Fori(1, NE) as e:
                        for r in range(ROUNDS - 1):
                            scatter(l, OS[l], e * (ROUNDS - 1) + r, 0, over_scattered[l])
                    pool.wait_ge(over_scattered[l], 16 * NE * (ROUNDS - 1))
                for t in range(NT):
                    pool.dma_start(combine[:, t], rows_dram[l].rearrange("(t p s b) d -> p t s (b d)", t=NT, s=2, b=2)
                                   [:, t]).then_inc(combine_ld[l][t], 16)
                if l == 0:
                    pool.nop().then_inc(combine_asked, 1)


def constants(np):
    c = np.zeros((P, C_N), np.float32)
    r = np.arange(P)
    c[:, C_ID:C_ID + P] = np.eye(P)
    c[:, C_LT:C_LT + P] = r[:, None] < r[None, :]
    c[:, C_ONE:C_ONE + P] = 1.0
    c[:, C_IOTA:C_IOTA + P] = r % CAP
    c[:, C_E32:C_E32 + NE] = np.arange(NE)
    c[:, C_G32:C_G32 + NE] = np.arange(NE) // EPG
    c[:, C_TOK2:C_TOK2 + NT] = 2 * (r[:, None] + P * np.arange(NT)[None, :])
    c[:, C_FAR] = FAR + r // CAP
    c[:, C_I16:C_I16 + 16] = np.arange(16)
    c[:, C_HPI] = TURN / 4
    i, j = np.arange(SEQ)[:, None], np.arange(SEQ)[None, :]
    diff = i - j
    n = ((diff <= 128).astype(int) + (diff % 4 == 0) + (diff % 16 == 0)) * (diff >= 0)
    bias = np.zeros((P, HEADS, P + SEQ), np.float32)
    for hh in range(HEADS):
        slope = 2.0 ** (-8.0 * (hh + 1) / HEADS)
        full = np.where(n > 0, -slope * diff + np.log(np.maximum(n, 1)), NEG).astype(np.float32)
        bias[:, hh, 0:P] = full[0:P, 0:P]
        bias[:, hh, P:] = full[P:, :]
    return c, bias


def layout(np, I):
    pairs = lambda a: np.ascontiguousarray(a[0].reshape(PAIRS, P).T)
    step = np.repeat(np.asarray(I["ssm_log_step"])[0], 64).reshape(PAIRS, P).T
    ssm_p = np.stack([pairs(np.asarray(I["ssm_a_re"])), pairs(np.asarray(I["ssm_a_im"])), step], 1)
    ssm_b = np.zeros((4, 2, 16, 2, CHW, 2, 64), np.float32)
    ssm_c = np.zeros((2, 64, 2, PAIRS, 2, 16), np.float32)
    for z, (bn, cn) in enumerate((("ssm_b_re", "ssm_c_re"), ("ssm_b_im", "ssm_c_im"))):
        b = np.asarray(I[bn])[0].reshape(CHW, 4, 2, 64, 16)
        c = np.asarray(I[cn])[0].reshape(PAIRS, 2, 16, 64)
        for g in range(2):
            ssm_b[:, g, :, z, :, g, :] = b[:, :, g].transpose(1, 3, 0, 2)
            ssm_c[g, :, z, :, g, :] = c[:, g].transpose(2, 0, 1)
    gains = np.stack([np.asarray(I[n])[l].reshape(P, KD) for l in range(LAYERS) for n in ("norm_mix", "norm_ffn")], 1)
    w_router = np.stack([np.concatenate([np.asarray(I["w_router_group"])[l].reshape(P, KD, GROUPS),
                                         np.asarray(I["w_router_expert"])[l].reshape(P, KD, NE)], 2)
                         for l in range(LAYERS)], 1)
    b_router = np.concatenate([np.asarray(I["b_router_group"]), np.asarray(I["b_router_expert"])], 1)
    col = lambda a: np.asarray(a)[0].reshape(CHW, P).T
    cst, bias = constants(np)
    return {
        "ssm_p": ssm_p.reshape(P, 60), "ssm_b": ssm_b.reshape(P, 1280), "ssm_c": ssm_c.reshape(P, 1280),
        "gains": gains, "w_router": w_router, "b_router": np.tile(b_router[None], (P, 1, 1)),
        "d_bglu": np.stack([col(I["ssm_d"]), col(I["b_glu"])], 1),
        "conv_taps": np.asarray(I["conv_w"])[0].reshape(3, KD, P).transpose(2, 1, 0),
        "qk_gain": np.stack([np.tile(np.asarray(I[n])[0], P // HD) for n in ("q_norm", "k_norm")], 1),
        "cst": cst, "att_bias": bias,
    }


_BIG = ["x", "w_in_even", "w_glu", "w_out_even", "w_in_conv", "w_out_conv",
        "w_expert_gate", "w_expert_up", "w_expert_down"]


def kernel(**inputs):
    import numpy as np
    import concourse.bacc as bacc
    from concourse.bass_utils import run_bass_kernel_spmd

    nc = bacc.Bacc("TRN2", target_bir_lowering=False, num_devices=1)
    given = {n: np.ascontiguousarray(inputs[n]) for n in _BIG}
    given.update((n, np.ascontiguousarray(a)) for n, a in layout(np, inputs).items())
    arrays = {f"in_{n}": a for n, a in given.items()}
    A = {n: nc.dram_tensor(f"in_{n}", a.shape, F32, kind="ExternalInput").ap() for n, a in given.items()}
    out = nc.dram_tensor("out_0", (1, SEQ, D), F32, kind="ExternalOutput").ap()
    build(nc, A, out)
    r = run_bass_kernel_spmd(nc, [arrays], core_ids=[0])
    return r.results[0]["out_0"]
```

```python
from contextlib import ExitStack
import math

import concourse.bass as bass
from concourse import mybir

F32 = mybir.dt.float32
I32 = mybir.dt.int32
U32 = mybir.dt.uint32
ACT = mybir.ActivationFunctionType
ALU = mybir.AluOpType
AX = mybir.AxisListType

P = 128
SEQ = 256
D = 1024
NT = SEQ // P
KD = D // P
LAYERS = 2
SSM_W, PAIRS, CHW = 640, 20, 5
DUOS = PAIRS // 2
HEADS, HD, ATT_W = 6, 64, 384
QCH = ATT_W // P
EPS = 1e-6
GROUPS, EPG, NE, DE = 4, 8, 32, 512
CAP = 64
ROUNDS = SEQ // CAP
LAG = 3
TURN_N = 2 * LAG
SLOTS, SLOT = 9, 4096
NEG = -1.0e30
RINT = 12582912.0
TWO_PI_HI = 6.28125
TWO_PI_LO = 2.0 * math.pi - 6.28125
TURN = 6.283185

C_ID, C_LT, C_ONE, C_IOTA = 0, 128, 256, 384
C_E32, C_G32, C_TOK, C_I16, C_HPI = 640, 672, 704, 706, 722
C_N = 723


def build(nc, A, out):
    with ExitStack() as ctx:
        def sb(name, shape, dt=F32):
            return ctx.enter_context(nc.sbuf_tensor(name, shape, dt))

        def sem(name):
            return ctx.enter_context(nc.semaphore(name))

        ring = sb("ring", [P, SLOTS, SLOT])
        keep = sb("keep", [P, 4 * NT * D])
        h = keep[:, 0:2048].rearrange("p (t d) -> p t d", t=NT)
        hn = keep[:, 2048:4096].rearrange("p (t d) -> p t d", t=NT)
        hT = keep[:, 4096:6144].rearrange("p (k t) -> p k t", k=KD)
        mixT = keep[:, 6144:8192].rearrange("p (k t) -> p k t", k=KD)
        hn_k = keep[:, 2048:4096].rearrange("p (t q k) -> p t k q", t=NT, k=KD)
        cst = sb("cst", [P, C_N])
        ident = cst[:, C_ID:C_ID + P]
        earlier = cst[:, C_LT:C_LT + P]
        ones = cst[:, C_ONE:C_ONE + P]
        iota = cst[:, C_IOTA:C_IOTA + SEQ]
        gains = sb("gains", [P, 4, KD])
        w_router = sb("w_router", [P, LAYERS, KD, GROUPS + NE])
        b_router = sb("b_router", [P, LAYERS, GROUPS + NE])
        conv_taps = sb("conv_taps", [P, KD, 3])
        d_bglu = sb("d_bglu", [P, 2, CHW])
        qk_gain = sb("qk_gain", [P, 2])
        norm_s = sb("norm_s", [P, 4, NT])
        flag = sb("flag", [P, 1], I32)
        stage = sb("stage", [P, 6604])

        prob = stage[:, 0:2304].rearrange("p (h k) -> p h k", h=HEADS)
        ssm_b = stage[:, 2304:3584].rearrange("p (c a s) -> p c a s", c=2, a=CHW)
        glu = stage[:, 2304:3584].rearrange("p (c t) -> p c t", c=CHW)
        ssm_c = stage[:, 3584:4864].rearrange("p (c i j) -> p c i j", c=2, i=PAIRS)
        uT = stage[:, 4864:6144].rearrange("p (c t) -> p c t", c=CHW)
        yT = uT
        ssm_p = stage[:, 6144:6204].rearrange("p (v i) -> p v i", v=3)
        sml = stage[:, 6204:6604].rearrange("p (v i) -> p v i", v=20)
        c_tmp = [keep[:, 2048 + 640 * j:2688 + 640 * j].rearrange("p (i j) -> p i j", i=PAIRS) for j in range(3)]
        sq = keep[:, 2048:3584].rearrange("p (t c) -> p t c", t=NT)
        probT = keep[:, 2048:4352].rearrange("p (h k) -> p h k", h=HEADS)
        qkT = keep[:, 6144:7680].rearrange("p (c t) -> p c t", c=2 * QCH)
        scr = ring[:, 4:9, :].rearrange("p s n -> p (s n)")
        duo = lambda a: scr[:, a:a + 1024].rearrange("p (i c t) -> p i c t", i=2, c=2)
        cos_t = scr[:, 0:5120].rearrange("p (i t) -> p i t", i=PAIRS)
        sin_t = scr[:, 5120:10240].rearrange("p (i t) -> p i t", i=PAIRS)
        zz = [duo(10240 + 1024 * b) for b in range(2)]
        m2 = duo(12288)
        alpha, beta, whole = [scr[:, 12288 + 320 * j:12608 + 320 * j].rearrange("p (i a) -> p i a", i=PAIRS)
                              for j in range(3)]
        qc = [duo(13312 + 1024 * b) for b in range(2)]
        qs = [duo(15360 + 1024 * b) for b in range(2)]
        ypre = scr[:, 17408:17920].rearrange("p (b t) -> p b t", b=2)
        att_s = scr[:, 17920:18176]
        qkv = scr[:, 18176:20480].rearrange("p (t w c) -> p t w c", t=NT, w=3)
        zeros = scr[:, 18176:18688]
        ssm_cb = ring[:, 3, 3072:3712].rearrange("p (i j) -> p i j", i=PAIRS)
        z_sb = stage[:, 0:512].rearrange("p (b t) -> p b t", b=2)
        zc = stage[:, 512:1028].rearrange("p (b t) -> p b t", b=2)
        cv = stage[:, 1028:1540].rearrange("p (b t) -> p b t", b=2)
        sel = [stage[:, 256 * b:256 * b + 256].rearrange("p (t j) -> p t j", t=NT) for b in range(LAG)]
        xT = [stage[:, 768 + 512 * b:1280 + 512 * b].rearrange("p (k j) -> p k j", k=KD) for b in range(LAG)]
        hid = [stage[:, 2304 + 256 * b:2560 + 256 * b] for b in range(LAG)]
        turned = [stage[:, 3072 + 258 * b:3330 + 258 * b] for b in range(LAG)]
        hidT = [x[:, 0:256].rearrange("p (b j) -> p b j", b=2) for x in turned]
        rowv = [x[:, 256:258] for x in turned]
        xrow = [stage[:, 3846 + 512 * b:4358 + 512 * b] for b in range(LAG)]
        back = [stage[:, 5382 + 256 * b:5638 + 256 * b] for b in range(LAG)]
        vals = stage[:, 6150:6278].rearrange("p (t e v) -> p t e v", t=NT, v=2)
        rank = stage[:, 6278:6342].rearrange("p (t e) -> p t e", t=NT)
        y2 = [keep[:, 4096 + 1024 * b:5120 + 1024 * b] for b in range(LAG)]
        rt = keep[:, 6144:8192]
        lg = rt[:, 0:72].rearrange("p (t n) -> p t n", t=NT)
        gl8 = rt[:, 72:88].rearrange("p (t n) -> p t n", t=NT)
        gm8 = rt[:, 88:104].rearrange("p (t n) -> p t n", t=NT)
        gi8 = rt[:, 104:120].bitcast(U32).rearrange("p (t n) -> p t n", t=NT)
        gif = rt[:, 120:122].rearrange("p (t n) -> p t n", t=NT)
        ge = rt[:, 122:130].rearrange("p (t n) -> p t n", t=NT)
        gw = rt[:, 130:132]
        tm8 = rt[:, 132:148].rearrange("p (t n) -> p t n", t=NT)
        ti8 = rt[:, 148:164].bitcast(U32).rearrange("p (t n) -> p t n", t=NT)
        tif = rt[:, 164:168].rearrange("p (t n) -> p t n", t=NT)
        ex = rt[:, 168:170]
        den = rt[:, 170:172]
        wt = rt[:, 172:176].rearrange("p (s t) -> p s t", s=2)
        cmax = rt[:, 176:177]
        mask = rt[:, 192:256].rearrange("p (t n) -> p t n", t=NT)
        el = rt[:, 256:320].rearrange("p (t n) -> p t n", t=NT)
        oh = [rt[:, 320 + 64 * s:384 + 64 * s].rearrange("p (t n) -> p t n", t=NT) for s in range(2)]
        chosen = rt[:, 448:512].rearrange("p (t n) -> p t n", t=NT)
        rtmp = rt[:, 512:576].rearrange("p (t n) -> p t n", t=NT)

        psum = ctx.enter_context(nc.psum_tensor("psum", [P, 8, 512], F32))
        bank = [psum[:, i, :] for i in range(8)]

        ld_p, ld_b, ld_c = sem("ld_p"), sem("ld_b"), sem("ld_c")
        ld_x = [sem(f"ld_x{t}") for t in range(NT)]
        ld_const, ld_att, ld_route = sem("ld_const"), sem("ld_att"), sem("ld_route")
        ld_mix0 = [sem(f"ld_mix0_{j}") for j in range(7)]
        ld_mix1 = ld_mix0[:6] + [sem(f"ld_mix1_{j}") for j in range(2)]
        h_ready = sem("h_ready")
        squares, mean, root, hn_ready, tp_done, hT_ready = (
            sem("squares"), sem("mean"), sem("root"), sem("hn_ready"), sem("tp_done"), sem("hT_ready"))
        u_done, u_copied = sem("u_done"), sem("u_copied")
        qkv_done, qkv_copied = sem("qkv_done"), sem("qkv_copied")
        expd, lam_ready, r_ready, turn_ready, pole_ready = (sem("expd"), sem("lam_ready"), sem("r_ready"),
                                                            sem("turn_ready"), sem("pole_ready"))
        ab_ready, pool_added, angle_ready, table_ready = (sem("ab_ready"), sem("pool_added"), sem("angle_ready"),
                                                          sem("table_ready"))
        zeros_ready, factor_ready, c_ready = sem("zeros_ready"), sem("factor_ready"), sem("c_ready")
        bu_done, bu_used, z_ready, q_ready, y_done = (sem("bu_done"), sem("bu_used"), sem("z_ready"),
                                                      sem("q_ready"), sem("y_done"))
        ypre_ready, gelu_ready = sem("ypre_ready"), sem("gelu_ready")
        qk_mean, qk_root, qk_ready = sem("qk_mean"), sem("qk_root"), sem("qk_ready")
        qkT_done, qkT_copied = sem("qkT_done"), sem("qkT_copied")
        score_done, score_copied, max_ready, exp_done, prob_ready = (
            sem("score_done"), sem("score_copied"), sem("max_ready"), sem("exp_done"), sem("prob_ready"))
        pT_done, pT_copied, pv_done, att_ready = sem("pT_done"), sem("pT_copied"), sem("pv_done"), sem("att_ready")
        glu_done, gate_ready, ssm_ready = sem("glu_done"), sem("gate_ready"), sem("ssm_ready")
        out0_done = sem("out0_done")
        cz_done, b_done, z_copied, g_ready, out1_done = (sem("cz_done"), sem("b_done"), sem("z_copied"),
                                                         sem("g_ready"), sem("out1_done"))
        names = ("logits", "gshift", "gexp", "eshift", "eexp", "chosen_ready", "rank_done", "count_done", "route_ready")
        RS = dict((n, sem(n)) for n in names)

        def expert_sems(tag):
            s = dict((n, sem(f"{n}_{tag}")) for n in
                     ("sel_ready", "gather_done", "xrow_ready", "xt_done", "xT_ready", "gu_done", "silu_ready",
                      "hid_ready", "turn_done", "hidT_ready", "down_done", "y_ready", "back_ready", "acc_done"))
            return s

        ES = [expert_sems(f"m{l}") for l in range(LAYERS)]
        OS = [expert_sems(f"o{l}") for l in range(LAYERS)]
        ld_gu = [[sem(f"ld_gu{u}_{half}") for half in range(2)] for u in range(LAG)]
        gu_half = [sem(f"gu_half{l}") for l in range(LAYERS)]
        ld_down = [sem(f"ld_down{u}") for u in range(LAG)]
        ld_over = [sem(f"ld_over{l}") for l in range(LAYERS)]
        stored = sem("stored")

        FIRST_SLOT = (3, 0)
        OVER = 6
        OVER_B = 1
        PAIRS_DONE = NE // 2 - 1

        def slots(l, u):
            s = FIRST_SLOT[l] + 3 * u
            return s % SLOTS, (s + 1) % SLOTS, (s + 2) % SLOTS

        def before(eng, s, n, lag, per=1):
            if isinstance(n, int) and n < lag:
                return
            eng.wait_ge(s, (n - (lag - 1)) * per)

        def passes(engine, step, first=None):
            turns = NE // TURN_N
            for n in range(TURN_N):
                (first if first and n < LAG else step)(n, n, n // LAG, n // 2)
            with engine.Fori(1, turns) as j:
                for v in range(TURN_N):
                    step(j * TURN_N + v, v, j * 2 + v // LAG, j * LAG + v // 2)
            for n in range(turns * TURN_N, NE):
                step(n, n % TURN_N, n // LAG, n // 2)

        def more(n):
            return not (isinstance(n, int) and n == NE - 1)

        def overflow(engine, body):
            count = engine.value_load(flag[0:1, 0:1], min_val=0, max_val=SEQ)
            with engine.If(count > CAP):
                for r in range(1, ROUNDS):
                    body(r - 1, 0, r)
                with engine.Fori(1, NE) as e:
                    for r in range(1, ROUNDS):
                        body(e * (ROUNDS - 1) + (r - 1), e, r)

        w_in0 = A["w_in_even"][0].rearrange("(p k) n -> p k n", k=KD)
        TILES0 = ((0, 512), (512, 1024), (1024, 1408), (1408, 1792))
        w_conv = A["w_in_conv"][0].rearrange("(p k) n -> p k n", k=KD)
        w_gate = [A["w_expert_gate"][l].rearrange("e (p k) f -> p e (k f)", k=KD) for l in range(LAYERS)]
        w_up = [A["w_expert_up"][l].rearrange("e (p k) f -> p e (k f)", k=KD) for l in range(LAYERS)]
        w_down = [A["w_expert_down"][l].rearrange("e (h p b) d -> p e h (b d)", h=2, b=2) for l in range(LAYERS)]

        def slot2(s):
            return ring[:, s, :].rearrange("p (h n) -> p h n", h=2)

        def turn_bank(i, j):
            return (j + 2) % 4 if i == 1 else j

        def angle_sum(eng, c):
            i = slice(4 * c, 4 * c + 4)
            return eng.tensor_tensor(sin_t[:, i, :].rearrange("p i (a b) -> p i a b", a=16),
                                     alpha[:, i, :].unsqueeze(3).to_broadcast([P, 4, 16, 16]),
                                     beta[:, i, :].unsqueeze(2).to_broadcast([P, 4, 16, 16]), ALU.add)

        block = ctx.enter_context(nc.Block())

        @block.sync
        def _(sp):
            def projection(j):
                a, b = TILES0[j]
                sp.dma_start(ring[:, j, 0:KD * (b - a)].rearrange("p (k n) -> p k n", k=KD),
                             w_in0[:, :, a:b]).then_inc(ld_mix0[j], 16)

            sp.dma_start(stage[:, 6144:6204], A["ssm_p"]).then_inc(ld_p, 16)
            for t in range(NT):
                sp.dma_start(h[:, t, :], A["x"][0][t * P:(t + 1) * P, :]).then_inc(ld_x[t], 16)
            sp.dma_start(cst[:, :], A["cst"]).then_inc(ld_const, 16)
            sp.dma_start(gains[:, :, :], A["gains"]).then_inc(ld_const, 16)
            projection(0)
            sp.dma_start(stage[:, 2304:3584], A["ssm_b"]).then_inc(ld_b, 16)
            projection(1)
            sp.dma_start(stage[:, 3584:4864], A["ssm_c"]).then_inc(ld_c, 16)
            sp.dma_start(d_bglu[:, :, :], A["d_bglu"]).then_inc(ld_c, 16)
            projection(2)
            projection(3)
            sp.dma_start(qk_gain[:, :], A["qk_gain"]).then_inc(ld_att, 16)
            sp.dma_start(prob, A["att_bias"]).then_inc(ld_att, 16)
            sp.dma_start(w_router[:, :, :, :], A["w_router"]).then_inc(ld_route, 16)
            sp.dma_start(b_router[:, :, :], A["b_router"]).then_inc(ld_route, 16)
            sp.dma_start(conv_taps[:, :, :], A["conv_taps"]).then_inc(ld_route, 16)
            sp.wait_ge(u_done, 4)
            sp.dma_start(ring[:, 0, 0:CHW * SSM_W].rearrange("p (c n) -> p c n", c=CHW),
                         A["w_glu"][0].rearrange("(c p) n -> p c n", p=P)).then_inc(ld_mix0[4], 16)
            sp.wait_ge(qkv_done, 4)
            for j in range(2):
                sp.dma_start(ring[:, 1 + j, :].rearrange("p (c n) -> p c n", c=4),
                             A["w_out_even"][0].rearrange("(c p) n -> p c n", p=P)[:, 4 * j:4 * j + 4, :]
                             ).then_inc(ld_mix0[5 + j], 16)

            HALF = SLOT // 2

            def load_part(w, l, e, s, half, landed):
                a = half * HALF
                sp.dma_start(ring[:, s, a:a + HALF], w[l][:, bass.ds(e, 1), a:a + HALF]).then_inc(landed, 16)

            def load_whole(w, l, e, s, landed):
                for half in range(2):
                    load_part(w, l, e, s, half, landed[half])

            def load_dn(l, e, d, landed):
                sp.dma_start(slot2(d), w_down[l][:, bass.ds(e, 1), :, :]).then_inc(landed, 16)

            def conv_tile(j):
                which, half = (1, 2, 0)[j % 3], j // 3
                sp.dma_start(ring[:, 1 + j, :].rearrange("p (k n) -> p k n", k=KD),
                             w_conv[:, :, which * D + half * 512:which * D + half * 512 + 512]
                             ).then_inc(ld_mix1[j], 16)

            for l in range(LAYERS):
                if l == 1:
                    sp.wait_ge(ES[0]["down_done"], NE)
                    for j in range(3, 6):
                        conv_tile(j)
                    for j in range(2):
                        sp.dma_start(ring[:, 7 + j, :].rearrange("p (c n) -> p c n", c=4),
                                     A["w_out_conv"][0].rearrange("(c p) n -> p c n", p=P)[:, 4 * j:4 * j + 4, :]
                                     ).then_inc(ld_mix1[6 + j], 16)

                def first(n, u, i, m, l=l):
                    g, up, d = slots(l, u)
                    if l == 0 and u == 0:
                        sp.wait_ge(qkv_done, 6)
                        sp.wait_ge(y_done, DUOS)
                    load_whole(w_gate, l, n, g, ld_gu[u])
                    if l == 1 and u == 0:
                        sp.wait_ge(b_done, 4)
                    if l == 1 and u == 1:
                        sp.wait_ge(b_done, 8)
                    if l == 1 and u == 2:
                        sp.wait_ge(out1_done, 3)
                    if l == 0 and u == 2:
                        sp.wait_ge(out0_done, 3)
                    load_whole(w_up, l, n, up, ld_gu[u])
                    if l == 0 and u == 1:
                        sp.wait_ge(gelu_ready, CHW)
                        sp.wait_ge(pv_done, 1)
                    load_dn(l, n, d, ld_down[u])
                    if l == 0 and u == 1:
                        sp.wait_ge(glu_done, CHW)

                def steady(n, v, i, m, l=l):
                    u = v % LAG
                    g, up, d = slots(l, u)
                    for half, read in enumerate((gu_half[l], ES[l]["gu_done"])):
                        before(sp, read, n, LAG)
                        load_part(w_gate, l, n, g, half, ld_gu[u][half])
                        load_part(w_up, l, n, up, half, ld_gu[u][half])
                    before(sp, ES[l]["down_done"], n, LAG)
                    load_dn(l, n, d, ld_down[u])

                passes(sp, steady, first)

                if l == 0:
                    sp.wait_ge(ES[0]["gu_done"], NE - 2)
                    conv_tile(0)
                    sp.wait_ge(ES[0]["down_done"], NE - 2)
                    conv_tile(1)
                    sp.wait_ge(ES[0]["gu_done"], NE - 1)
                    conv_tile(2)
                sp.wait_ge(RS["route_ready"], l + 1)
                sp.wait_ge(ES[l]["down_done"], NE)

                def body(m, e, l=l):
                    before(sp, OS[l]["down_done"], m, 1)
                    load_whole(w_gate, l, e, OVER, [ld_over[l]] * 2)
                    load_whole(w_up, l, e, OVER + 1, [ld_over[l]] * 2)
                    load_dn(l, e, OVER + 2, ld_over[l])

                count = sp.value_load(flag[0:1, 0:1], min_val=0, max_val=SEQ)
                with sp.If(count > CAP):
                    body(0, 0)
                    with sp.Fori(1, NE) as e:
                        body(e * (ROUNDS - 1), e)
                    sp.wait_ge(OS[l]["down_done"], NE * (ROUNDS - 1))
            for t in range(NT):
                sp.wait_ge(h_ready, 7 + t)
                sp.dma_start(out[0][t * P:(t + 1) * P, :], h[:, t, :]).then_inc(stored, 16)
            sp.wait_ge(stored, 16 * NT)

        @block.tensor
        def _(pe):
            def norm_turn(i, t):
                pe.wait_ge(hn_ready, NT * i + t + 1)
                for kh in range(2):
                    for k in range(4):
                        last = pe.transpose(bank[turn_bank(i, 2 * t + kh)][:, k * P:(k + 1) * P],
                                            hn_k[:, t, 4 * kh + k, :], ident)
                    last.then_inc(tp_done, 1)

            def keep_warm(n, a, b):
                for _ in range(n):
                    pe.matmul(bank[7][:, :], a, b, start=True, stop=True)

            def logits(l, t):
                pe.wait_ge(hT_ready, 4 * (2 * l + 1) + 2 * t + 2)
                for k in range(KD):
                    last = pe.matmul(bank[4][:, 36 * t:36 * t + 36], hT[:, k, t * P:(t + 1) * P],
                                     w_router[:, l, k, :], start=(k == 0), stop=(k == KD - 1))
                last.then_inc(RS["logits"], 1)

            def route(l):
                keep_warm(4, ident, cst[:, 0:512])
                pe.wait_ge(RS["chosen_ready"], l + 1)
                pe.matmul(bank[5][:, 0:NE], earlier, chosen[:, 0, :], start=True, stop=True)
                pe.matmul(bank[5][:, NE:2 * NE], ones, chosen[:, 0, :], start=True, stop=False)
                pe.matmul(bank[5][:, NE:2 * NE], earlier, chosen[:, 1, :], start=False, stop=True
                          ).then_inc(RS["rank_done"], 1)
                pe.matmul(bank[4][:, 2 * NE:3 * NE], ones, chosen[:, 0, :], start=True, stop=False)
                pe.matmul(bank[4][:, 2 * NE:3 * NE], ones, chosen[:, 1, :], start=False, stop=True
                          ).then_inc(RS["count_done"], 1)

            def gather(S, n, b, lag):
                pe.wait_ge(S["sel_ready"], n + 1)
                before(pe, S["hidT_ready"], n, lag)
                for t in range(NT):
                    for half in range(2):
                        last = pe.matmul(bank[1][half * CAP:(half + 1) * CAP, :].rearrange("p (k q) -> p k q", k=4),
                                         sel[b][:, t, 0:CAP], hn_k[:, t, 4 * half:4 * half + 4, :],
                                         start=(t == 0), stop=(t == NT - 1))
                last.then_inc(S["gather_done"], 1)

            def turn_rows(S, n, b):
                pe.wait_ge(S["xrow_ready"], n + 1)
                before(pe, S["xT_ready"], n, 1)
                for j in range(4):
                    last = pe.transpose(bank[2][:, j * P:(j + 1) * P], xrow[b][:, j * P:(j + 1) * P], ident)
                last.then_inc(S["xt_done"], 1)

            def add_back(b, t, rows, start, stop):
                for half in range(2):
                    last = pe.matmul(bank[4 + 2 * t + half][:, :], back[b][0:rows, t * P:(t + 1) * P],
                                     y2[b][0:rows, half * 512:(half + 1) * 512], start=start, stop=stop)
                return last

            def gate_up(S, n, b, g, landed=None, count=None, half_read=None):
                pe.wait_ge(S["xT_ready"], n + 1)
                before(pe, S["hid_ready"], n, 1)
                both = ring[:, g:g + 2, :].rearrange("p s (k n) -> p k s n", k=KD)
                for k in range(KD):
                    if landed and k % 4 == 0:
                        pe.wait_ge(landed[k // 4], count)
                    for half in range(2):
                        last = pe.matmul(bank[0][half * CAP:(half + 1) * CAP, :], xT[b][:, k, :],
                                         both[:, k, :, half * 256:half * 256 + 256],
                                         start=(k == 0), stop=(k == KD - 1))
                    if half_read and k == 3:
                        last.then_inc(half_read, 1)
                last.then_inc(S["gu_done"], 1)

            def turn(S, n, b, e, rows):
                pe.wait_ge(S["hid_ready"], n + 1)
                pe.wait_ge(S["xrow_ready"], rows)
                for j in range(2):
                    pe.transpose(bank[1][:, j * P:(j + 1) * P], hid[b].rearrange("p (q b) -> p b q", b=2)[:, j, :], ident)
                for t in range(NT):
                    last = pe.matmul(bank[1][:, 256:258], sel[b][:, t, :], vals[:, t, bass.ds(e, 1), :],
                                     start=(t == 0), stop=(t == NT - 1))
                last.then_inc(S["turn_done"], 1)

            def down(S, n, b, d):
                pe.wait_ge(S["hidT_ready"], n + 1)
                before(pe, S["y_ready"], n, 1)
                for c in range(4):
                    for half in range(2):
                        last = pe.matmul(bank[3][half * CAP:(half + 1) * CAP, :],
                                         hidT[b][:, c % 2, (c // 2) * CAP:(c // 2 + 1) * CAP],
                                         slot2(d)[:, c // 2, (c % 2) * D + half * 512:(c % 2) * D + half * 512 + 512],
                                         start=(c == 0), stop=(c == 3))
                last.then_inc(S["down_done"], 1)

            def experts(l):
                S = ES[l]

                def step(n, v, i, m):
                    u, w = v % LAG, (v + 1) % LAG
                    g, up, d = slots(l, u)
                    turns = i + 1 + l * ((NE - u + LAG - 1) // LAG)
                    gate_up(S, n, u, g, ld_gu[u], turns * 32, gu_half[l])
                    if more(n):
                        gather(S, n + 1, w, 2)
                    if not (isinstance(n, int) and n < 2):
                        if v % 2 == 0:
                            pe.wait_ge(S["y_ready"], n)
                            pe.wait_ge(S["back_ready"], n)
                        last = add_back((v // 2 - 1) % LAG, v % 2, P, isinstance(n, int) and n < 4, False)
                        if v % 2:
                            last.then_inc(S["acc_done"], 1)
                    turn(S, n, u, n, n + 2 if more(n) else n + 1)
                    if more(n):
                        turn_rows(S, n + 1, w)
                    pe.wait_ge(ld_down[u], turns * 16)
                    down(S, n, u, d)

                gather(S, 0, 0, 2)
                turn_rows(S, 0, 0)
                passes(pe, step)
                pe.wait_ge(S["y_ready"], NE)
                pe.wait_ge(S["back_ready"], NE)
                pe.wait_ge(RS["route_ready"], l + 1)

                O = OS[l]

                def body(m, e, r):
                    pe.wait_ge(ld_over[l], (e + 1) * 80)
                    gather(O, m, 0, 1)
                    turn_rows(O, m, 0)
                    gate_up(O, m, 0, OVER)
                    turn(O, m, 0, e, m + 1)
                    down(O, m, 0, OVER + 2)
                    pe.wait_ge(O["y_ready"], m + 1)
                    pe.wait_ge(O["back_ready"], m + 1)
                    for t in range(NT):
                        last = add_back(OVER_B, t, CAP, False, False)
                    last.then_inc(O["acc_done"], 1)
                overflow(pe, body)
                for t in range(NT):
                    add_back((NE // 2 - 1) % LAG, t, P, False, True).then_inc(S["acc_done"], 1)

            pe.wait_ge(zeros_ready, 1)
            keep_warm(5, zeros[:, 0:P], zeros)
            pe.wait_ge(ld_const, 32)
            for t in range(NT):
                norm_turn(0, t)
            keep_warm(2, zeros[:, 0:P], zeros)
            pe.wait_ge(hT_ready, 4)

            def project_u(m):
                j, c = (0, m) if m < 4 else (1, 0)
                w = ring[:, j, :].rearrange("p (k n) -> p k n", k=KD)
                pe.wait_ge(ld_mix0[j], 16)
                if m >= 2:
                    pe.wait_ge(u_copied, m - 1)
                for k in range(KD):
                    last = pe.matmul(bank[m % 2][:, 0:SEQ], w[:, k, c * P:(c + 1) * P], hT[:, k, :],
                                     start=(k == 0), stop=(k == KD - 1))
                last.then_inc(u_done, 1)

            def project_qkv(j):
                w3, t = j // 2, j % 2
                src = ((1, 128, 512), (2, 0, 384), (3, 0, 384))[w3]
                n = 512 if w3 == 0 else 384
                w = ring[:, src[0], 0:KD * n].rearrange("p (k n) -> p k n", k=KD)
                pe.wait_ge(ld_mix0[src[0]], 16)
                if j < 2:
                    pe.wait_ge(u_copied, 4 + j)
                else:
                    pe.wait_ge(qkv_copied, j - 1)
                for k in range(KD):
                    last = pe.matmul(bank[(1 + j) % 2][:, 0:ATT_W], hT[:, k, t * P:(t + 1) * P],
                                     w[:, k, src[1]:src[2]], start=(k == 0), stop=(k == KD - 1))
                last.then_inc(qkv_done, 1)

            def turn_qk():
                pe.wait_ge(qk_ready, 1)
                for j in range(3):
                    if j < 2:
                        pe.wait_ge(qkv_copied, 5 + j)
                    else:
                        pe.wait_ge(qkT_copied, 2)
                    for half in range(2):
                        ch = 2 * j + half
                        for t in range(NT):
                            last = pe.transpose(bank[(1 + j) % 2][:, (2 * half + t) * P:(2 * half + t + 1) * P],
                                                qkv[:, t, ch // 3, (ch % 3) * P:(ch % 3 + 1) * P], ident)
                    last.then_inc(qkT_done, 1)

            def scores(hh):
                r = 64 * (hh % 2)
                q, k = qkT[r:r + 64, hh // 2, :], qkT[r:r + 64, 3 + hh // 2, :]
                if hh == 0:
                    pe.wait_ge(qkT_copied, 6)
                if hh >= 2:
                    pe.wait_ge(score_copied, hh - 1)
                pe.matmul(bank[hh % 2][:, 0:P], q[:, 0:P], k[:, 0:P], start=True, stop=True)
                pe.matmul(bank[hh % 2][:, P:P + SEQ], q[:, P:SEQ], k, start=True, stop=True).then_inc(score_done, 1)

            def drive(d):
                if d == 0:
                    pe.wait_ge(ld_b, 16)
                if d % 2 == 0:
                    pe.wait_ge(u_copied, d // 2 + 1)
                if d >= 2:
                    pe.wait_ge(bu_used, d - 1)
                for c in range(2):
                    for i in (2 * d, 2 * d + 1):
                        r = 32 * (i % 4)
                        last = pe.matmul(bank[4 + i % 4][:, c * SEQ:(c + 1) * SEQ], ssm_b[r:r + 32, c, i // 4, :],
                                         uT[r:r + 32, i // 4, :], start=True, stop=True)
                last.then_inc(bu_done, 1)

            def readout(d):
                c, b = d // 2, d % 2
                if d == 0:
                    pe.wait_ge(c_ready, 1)
                pe.wait_ge(q_ready, d + 1)
                if c >= 2 and b == 0:
                    pe.wait_ge(ypre_ready, c - 1)
                terms = ((ssm_c[:, 0], qc[b], 0), (ssm_cb, qs[b], 1), (ssm_c[:, 1], qs[b], 0), (ssm_c[:, 1], qc[b], 1))
                for n, (w, q, part) in enumerate(terms):
                    for x, i in enumerate((2 * d, 2 * d + 1)):
                        r = 32 * (i % 4)
                        last = pe.matmul(bank[2 + c % 2][r:r + 32, 0:SEQ], w[:, i, :], q[:, x, part, :],
                                         start=(n == 0), stop=(n == 3))
                last.then_inc(y_done, 1)

            project_u(0)
            project_u(1)
            drive(0)
            drive(1)
            for d in range(DUOS):
                if d == 0:
                    project_u(2)
                elif d == 1:
                    for m in range(3, CHW):
                        project_u(m)
                elif d < 8:
                    project_qkv(d - 2)
                elif d == 9:
                    turn_qk()
                    for hh in range(HEADS):
                        scores(hh)
                if d + 2 < DUOS:
                    drive(d + 2)
                if d >= 1:
                    readout(d - 1)
            readout(DUOS - 1)

            GLU_BANK = (4, 5, 6, 7, 3)
            pe.wait_ge(ld_mix0[4], 16)
            pe.wait_ge(bu_used, DUOS)
            pe.wait_ge(ypre_ready, CHW - 1)
            wg = ring[:, 0, 0:CHW * SSM_W].rearrange("p (c n) -> p c n", c=CHW)
            for c in range(CHW):
                pe.wait_ge(gelu_ready, c + 1)
                for m in range(CHW):
                    last = pe.matmul(bank[GLU_BANK[m]][:, 0:SEQ], wg[:, c, m * P:(m + 1) * P], yT[:, c, :],
                                     start=(c == 0), stop=(c == CHW - 1))
                    if c == CHW - 1:
                        last.then_inc(glu_done, 1)
            pe.wait_ge(prob_ready, 1)
            pe.wait_ge(ypre_ready, CHW)
            for hh in range(HEADS):
                if hh >= 3:
                    pe.wait_ge(pT_copied, hh - 2)
                for j in range(3):
                    last = pe.transpose(bank[hh % 3][:, j * P:(j + 1) * P], prob[:, hh, j * P:(j + 1) * P], ident)
                last.then_inc(pT_done, 1)
            pe.wait_ge(pT_copied, HEADS)
            for hh in range(HEADS):
                r, c = 64 * (hh % 2), hh // 2
                o = bank[c][r:r + 64, 0:SEQ]
                pe.matmul(o, qkv[:, 0, 2, hh * HD:(hh + 1) * HD], probT[:, hh, 0:SEQ], start=True, stop=False)
                last = pe.matmul(o[:, P:SEQ], qkv[:, 1, 2, hh * HD:(hh + 1) * HD], probT[:, hh, SEQ:SEQ + P],
                                 start=False, stop=True)
            last.then_inc(pv_done, 1)
            att_chunks, ssm_chunks = (5, 6, 7), tuple(range(CHW))
            for t, chunks in ((0, att_chunks), (1, att_chunks), (0, ssm_chunks)):
                for c in chunks:
                    if t == 0 and c == 5:
                        pe.wait_ge(ld_mix0[6], 16)
                        pe.wait_ge(att_ready, 1)
                        pe.wait_ge(gate_ready, CHW)
                    if c < CHW:
                        if c == 0:
                            pe.wait_ge(ld_mix0[5], 16)
                        pe.wait_ge(ssm_ready, c + 1)
                    w = ring[:, 1 + c // 4, :].rearrange("p (c n) -> p c n", c=4)
                    for n in range(2):
                        last = pe.matmul(bank[2 - 2 * t + n][:, :], mixT[:, c, t * P:(t + 1) * P],
                                         w[:, c % 4, n * 512:(n + 1) * 512], start=(c == 5), stop=(c == 4))
            last.then_inc(out0_done, 1)
            for n in range(2):
                for c in range(CHW):
                    w = ring[:, 1 + c // 4, :].rearrange("p (c n) -> p c n", c=4)
                    last = pe.matmul(bank[n][:, :], mixT[:, c, P:2 * P], w[:, c % 4, n * 512:(n + 1) * 512],
                                     start=False, stop=(c == 4))
                last.then_inc(out0_done, 1)
                if n == 0:
                    norm_turn(1, 0)
            pe.wait_ge(ld_route, 48)
            logits(0, 0)
            keep_warm(2, ident, cst[:, 0:512])
            norm_turn(1, 1)
            logits(0, 1)
            route(0)
            experts(0)

            for t in range(NT):
                norm_turn(2, t)
            pe.wait_ge(hT_ready, 12)
            for m in range(KD):
                half, c = m // 4, m % 4
                for part in range(3):
                    pe.wait_ge(ld_mix1[3 * half + part], 32)
                    if part != 1 and m >= 2:
                        pe.wait_ge(g_ready, m - 1)
                    o = bank[4 + m % 2][:, part * 256:part * 256 + 256] if part < 2 else bank[6 + m % 2][:, 0:256]
                    w = ring[:, 1 + 3 * half + part, :].rearrange("p (k n) -> p k n", k=KD)
                    for k in range(KD):
                        last = pe.matmul(o, w[:, k, c * P:(c + 1) * P], hT[:, k, :], start=(k == 0), stop=(k == KD - 1))
                    if part > 0:
                        last.then_inc(cz_done if part == 1 else b_done, 1)
            for c in range(KD):
                if c % 4 == 0:
                    pe.wait_ge(ld_mix1[6 + c // 4], 16)
                pe.wait_ge(g_ready, c + 1)
                w = ring[:, 7 + c // 4, :].rearrange("p (c n) -> p c n", c=4)
                for n in range(2):
                    last = pe.matmul(bank[n][:, :], mixT[:, c, 0:P],
                                     w[:, c % 4, n * 512:(n + 1) * 512], start=(c == 0), stop=(c == KD - 1))
            last.then_inc(out1_done, 1)
            for n in range(2):
                for c in range(KD):
                    w = ring[:, 7 + c // 4, :].rearrange("p (c n) -> p c n", c=4)
                    last = pe.matmul(bank[2 + n][:, :], mixT[:, c, P:2 * P],
                                     w[:, c % 4, n * 512:(n + 1) * 512], start=(c == 0), stop=(c == KD - 1))
                last.then_inc(out1_done, 1)
                if n == 0:
                    norm_turn(3, 0)
            logits(1, 0)
            keep_warm(2, ident, cst[:, 0:512])
            norm_turn(3, 1)
            logits(1, 1)
            route(1)
            experts(1)

        @block.vector
        def _(dve):
            def norm_rows(i, t):
                dve.wait_ge(squares, NT * i + t + 1)
                dve.tensor_scalar(norm_s[:, 1, t:t + 1], norm_s[:, 0, t:t + 1], 1.0 / D, EPS, ALU.mult, ALU.add
                                  ).then_inc(mean, 1)
                dve.wait_ge(root, NT * i + t + 1)
                dve.reciprocal(norm_s[:, 3, t:t + 1], norm_s[:, 2, t:t + 1])
                dve.drain()
                dve.tensor_scalar(hn[:, t, :], h[:, t, :], norm_s[:, 3, t:t + 1], None, ALU.mult).then_inc(hn_ready, 1)

            def norm_turned(i, t):
                for kh in range(2):
                    dve.wait_ge(tp_done, 4 * i + 2 * t + kh + 1)
                    dve.tensor_tensor(hT[:, 4 * kh:4 * kh + 4, t * P:(t + 1) * P],
                                      bank[turn_bank(i, 2 * t + kh)][:, :].rearrange("p (k q) -> p k q", k=4),
                                      gains[:, i, 4 * kh:4 * kh + 4].unsqueeze(2).to_broadcast([P, 4, P]),
                                      ALU.mult).then_inc(hT_ready, 1)

            def residual(i, done, banks):
                for t in range(NT):
                    for n in range(2):
                        if t == 1 or n == 0:
                            dve.wait_ge(done, t + n + 1)
                        last = dve.tensor_tensor(h[:, t, n * 512:(n + 1) * 512], h[:, t, n * 512:(n + 1) * 512],
                                                 bank[banks[t] + n][:, :], ALU.add)
                    last.then_inc(h_ready, 1)
                    dve.drain()
                    norm_rows(i, t)
                    norm_turned(i, t)

            def route(l):
                s = RS
                dve.memset(gl8, NEG)
                dve.wait_ge(s["logits"], NT * l + NT)
                dve.tensor_tensor(lg, bank[4][:, 0:72].rearrange("p (t n) -> p t n", t=NT),
                                  b_router[:, l, :].unsqueeze(1).to_broadcast([P, NT, GROUPS + NE]), ALU.add)
                dve.drain()
                dve.tensor_copy(gl8[:, :, 0:GROUPS], lg[:, :, 0:GROUPS])
                dve.drain()
                for t in range(NT):
                    dve.max(gm8[:, t, :], gl8[:, t, :])
                dve.drain()
                for t in range(NT):
                    dve.max_index(gi8[:, t, :], gm8[:, t, :], gl8[:, t, :])
                dve.tensor_tensor(ge, gl8[:, :, 0:GROUPS], gm8[:, :, 0:1].to_broadcast([P, NT, GROUPS]),
                                  ALU.subtract).then_inc(s["gshift"], 1)
                dve.drain()
                dve.tensor_copy(gif, gi8[:, :, 0:1])
                dve.drain()
                dve.tensor_tensor(mask, cst[:, C_G32:C_G32 + NE].unsqueeze(1).to_broadcast([P, NT, NE]),
                                  gif.to_broadcast([P, NT, NE]), ALU.is_equal)
                dve.drain()
                dve.tensor_tensor(el, lg[:, :, GROUPS:], mask, ALU.mult)
                dve.tensor_scalar(rtmp, mask, -NEG, NEG, ALU.mult, ALU.add)
                dve.drain()
                dve.tensor_tensor(el, el, rtmp, ALU.add)
                dve.drain()
                for t in range(NT):
                    dve.max(tm8[:, t, :], el[:, t, :])
                dve.drain()
                for t in range(NT):
                    dve.max_index(ti8[:, t, :], tm8[:, t, :], el[:, t, :])
                dve.tensor_tensor(ex.unsqueeze(2), tm8[:, :, 1:2], tm8[:, :, 0:1], ALU.subtract
                                  ).then_inc(s["eshift"], 1)
                dve.drain()
                dve.tensor_copy(tif, ti8[:, :, 0:2])
                dve.drain()
                for k in range(2):
                    dve.tensor_tensor(oh[k], cst[:, C_E32:C_E32 + NE].unsqueeze(1).to_broadcast([P, NT, NE]),
                                      tif[:, :, k:k + 1].to_broadcast([P, NT, NE]), ALU.is_equal)
                dve.drain()
                dve.tensor_tensor(chosen, oh[0], oh[1], ALU.add).then_inc(s["chosen_ready"], 1)
                dve.drain()
                dve.tensor_copy(vals[:, :, :, 0], cst[:, C_TOK:C_TOK + NT].unsqueeze(2).to_broadcast([P, NT, NE]))
                dve.tensor_scalar(rtmp, chosen, 1000.0, -1000.0, ALU.mult, ALU.add)
                dve.wait_ge(s["rank_done"], l + 1)
                dve.tensor_tensor(rank, bank[5][:, 0:2 * NE].rearrange("p (t n) -> p t n", t=NT), chosen, ALU.mult)
                dve.drain()
                dve.tensor_tensor(rank, rank, rtmp, ALU.add)
                dve.drain()
                select(ES[l], 0, 0, 0, 0, LAG)
                dve.wait_ge(s["gexp"], l + 1)
                dve.wait_ge(s["eexp"], l + 1)
                dve.tensor_reduce(gw, ge, AX.X, ALU.add)
                dve.tensor_scalar(den, ex, 1.0, None, ALU.add)
                dve.drain()
                dve.tensor_tensor(den, den, gw, ALU.mult)
                dve.drain()
                dve.reciprocal(wt[:, 0, :], den)
                dve.drain()
                dve.tensor_tensor(wt[:, 1, :], wt[:, 0, :], ex, ALU.mult)
                dve.drain()
                for k in range(2):
                    dve.tensor_tensor(oh[k], oh[k], wt[:, k, :].unsqueeze(2).to_broadcast([P, NT, NE]), ALU.mult)
                dve.drain()
                dve.tensor_tensor(vals[:, :, :, 1], oh[0], oh[1], ALU.add)
                dve.wait_ge(s["count_done"], l + 1)
                dve.tensor_reduce(cmax, bank[4][:, 2 * NE:3 * NE], AX.X, ALU.max)
                dve.drain()
                dve.tensor_copy(flag[:, :], cmax).then_inc(s["route_ready"], 1)

            def select(S, n, b, e, r, lag):
                before(dve, S["turn_done"], n, lag)
                for t in range(NT):
                    last = dve.tensor_scalar(sel[b][:, t, :].rearrange("p (c j) -> p c j", c=2),
                                             iota[:, 0:CAP].unsqueeze(1).to_broadcast([P, 2, CAP]), float(CAP * r), rank[:, t, bass.ds(e, 1)],
                                             ALU.add, ALU.is_equal)
                last.then_inc(S["sel_ready"], 1)

            def hidden(S, n, b):
                dve.wait_ge(S["silu_ready"], n + 1)
                dve.tensor_tensor(hid[b], hid[b], bank[0][:, 256:512], ALU.mult).then_inc(S["hid_ready"], 1)

            def gathered(S, n, b, l, lag):
                dve.wait_ge(S["xt_done"], n + 1)
                before(dve, S["gu_done"], n, lag)
                dve.tensor_tensor(xT[b].rearrange("p (h k) j -> p k h j", h=2),
                                  bank[2][:, :].rearrange("p (k h j) -> p k h j", k=4, h=2),
                                  gains[:, 2 * l + 1, :].rearrange("p (h k) -> p k h", h=2).unsqueeze(3)
                                  .to_broadcast([P, 4, 2, CAP]), ALU.mult).then_inc(S["xT_ready"], 1)

            def way_back(S, n, b, p, w, m, lag):
                dve.wait_ge(S["hidT_ready"], n + 1)
                before(dve, S["acc_done"], m, lag)
                dve.tensor_scalar(back[w][p:p + CAP, :], iota[p:p + CAP, :], rowv[b][p:p + CAP, 0:1],
                                  rowv[b][p:p + CAP, 1:2], ALU.is_equal, ALU.mult).then_inc(S["back_ready"], 1)

            def experts(l):
                S = ES[l]

                def step(n, v, i, m):
                    u, w = v % LAG, (v + 1) % LAG
                    if more(n):
                        select(S, n + 1, w, n + 1, 0, LAG)
                    hidden(S, n, u)
                    if more(n):
                        gathered(S, n + 1, w, l, LAG)
                    way_back(S, n, u, CAP * (v % 2), v // 2, m, LAG)

                gathered(S, 0, 0, l, LAG)
                passes(dve, step)

                O = OS[l]

                def body(m, e, r):
                    select(O, m, 0, e, r, 1)
                    gathered(O, m, 0, l, 1)
                    hidden(O, m, 0)
                    way_back(O, m, 0, 0, OVER_B, m, 1)
                dve.wait_ge(S["acc_done"], PAIRS_DONE)
                overflow(dve, body)

            def combined(l):
                for t in range(NT):
                    dve.wait_ge(ES[l]["acc_done"], PAIRS_DONE + t + 1)
                    dve.tensor_tensor(h[:, t, :].rearrange("p (n d) -> p n d", n=2),
                                      h[:, t, :].rearrange("p (n d) -> p n d", n=2),
                                      psum[:, 4 + 2 * t:6 + 2 * t, :], ALU.add).then_inc(h_ready, 1)
                    dve.drain()
                if l == 0:
                    for t in range(NT):
                        norm_rows(2, t)
                    for t in range(NT):
                        norm_turned(2, t)

            names = ("step", "xr", "th", "k", "r", "t0", "w16", "cr", "ci", "lr", "li", "n0", "n1", "n2", "cs", "sn")
            V = {n: sml[:, j, :] for j, n in enumerate(names)}
            a_re, a_im = ssm_p[:, 0, :], ssm_p[:, 1, :]
            dve.wait_ge(ld_p, 16)
            dve.wait_ge(expd, 1)
            dve.tensor_tensor(V["xr"], a_re, V["step"], ALU.mult).then_inc(lam_ready, 1)
            dve.tensor_tensor(V["th"], a_im, V["step"], ALU.mult)
            dve.drain()

            def rint(o, i):
                dve.tensor_scalar(o, i, RINT, -RINT, ALU.add, ALU.add)
                dve.drain()

            dve.tensor_scalar(V["k"], V["th"], 1.0 / (2.0 * math.pi), None, ALU.mult)
            dve.drain()
            rint(V["k"], V["k"])
            dve.scalar_tensor_tensor(out=V["th"], in0=V["k"], scalar=-TWO_PI_HI, in1=V["th"], op0=ALU.mult, op1=ALU.add)
            dve.drain()
            dve.scalar_tensor_tensor(out=V["th"], in0=V["k"], scalar=-TWO_PI_LO, in1=V["th"], op0=ALU.mult, op1=ALU.add)
            dve.drain()
            dve.tensor_scalar(V["th"], V["th"], 1.0 / (2.0 * math.pi), None, ALU.mult).then_inc(turn_ready, 1)
            dve.drain()
            dve.tensor_scalar(V["w16"], V["th"], 16.0, None, ALU.mult)
            dve.drain()
            rint(V["t0"], V["w16"])
            dve.tensor_tensor(V["w16"], V["w16"], V["t0"], ALU.subtract)
            dve.drain()
            norm_rows(0, 0)
            norm_rows(0, 1)
            dve.wait_ge(ld_const, 32)
            i16 = cst[:, C_I16:C_I16 + 16].unsqueeze(1).to_broadcast([P, PAIRS, 16])
            for dst, w in ((alpha, V["w16"]), (beta, V["th"])):
                dve.tensor_tensor(dst, i16, w.unsqueeze(2).to_broadcast([P, PAIRS, 16]), ALU.mult)
                dve.drain()
                rint(whole, dst)
                dve.tensor_tensor(dst, dst, whole, ALU.subtract)
                dve.drain()
                if dst is alpha:
                    dve.scalar_tensor_tensor(out=alpha, in0=alpha, scalar=0.0, in1=alpha, op0=ALU.is_lt, op1=ALU.add)
                    for t in range(NT):
                        norm_turned(0, t)
            dve.nop().then_inc(ab_ready, 1)

            def add_turns(c):
                angle_sum(dve, c)
                dve.drain()

            def angle(c):
                if c >= 2:
                    dve.wait_ge(pool_added, c - 1)
                a = sin_t[:, 4 * c:4 * c + 4, :]
                dve.scalar_tensor_tensor(out=a, in0=a, scalar=0.5, in1=a, op0=ALU.is_ge, op1=ALU.subtract
                                         ).then_inc(angle_ready, 1)

            add_turns(0)
            angle(0)
            add_turns(1)
            for c in range(1, CHW):
                angle(c)

            def factor():
                dve.wait_ge(pole_ready, 1)
                dve.tensor_tensor(V["lr"], V["r"], V["cs"], ALU.mult)
                dve.tensor_tensor(V["li"], V["r"], V["sn"], ALU.mult)
                dve.tensor_tensor(V["n0"], a_re, a_re, ALU.mult)
                dve.tensor_tensor(V["n1"], a_im, a_im, ALU.mult)
                dve.drain()
                dve.tensor_scalar(V["lr"], V["lr"], -1.0, None, ALU.add)
                dve.tensor_tensor(V["n0"], V["n0"], V["n1"], ALU.add)
                dve.drain()
                dve.reciprocal(V["n2"], V["n0"])
                dve.tensor_tensor(V["cr"], V["lr"], a_re, ALU.mult)
                dve.tensor_tensor(V["n1"], V["li"], a_im, ALU.mult)
                dve.tensor_tensor(V["ci"], V["li"], a_re, ALU.mult)
                dve.tensor_tensor(V["t0"], V["lr"], a_im, ALU.mult)
                dve.drain()
                dve.tensor_tensor(V["cr"], V["cr"], V["n1"], ALU.add)
                dve.tensor_tensor(V["ci"], V["ci"], V["t0"], ALU.subtract)
                dve.drain()
                dve.tensor_tensor(V["cr"], V["cr"], V["n2"], ALU.mult)
                dve.tensor_tensor(V["ci"], V["ci"], V["n2"], ALU.mult)
                dve.drain()
                dve.tensor_scalar(V["n0"], V["ci"], -1.0, None, ALU.mult)
                dve.drain()
                dve.nop().then_inc(factor_ready, 1)

            factor()

            def skip_added(c):
                dve.wait_ge(y_done, 2 * c + 2)
                if c >= 2:
                    dve.wait_ge(gelu_ready, c - 1)
                dve.scalar_tensor_tensor(out=ypre[:, c % 2, :], in0=uT[:, c, :], scalar=d_bglu[:, 0, c:c + 1],
                                         in1=bank[2 + c % 2][:, 0:SEQ], op0=ALU.mult, op1=ALU.add
                                         ).then_inc(ypre_ready, 1)

            qk = qkv[:, :, 0:2, :].rearrange("p t w c -> p t (w c)")
            NH2 = 2 * HEADS
            ss = att_s[:, 0:24].rearrange("p (t n) -> p t n", t=NT)
            rs = att_s[:, 24:48].rearrange("p (t n) -> p t n", t=NT)
            nmax = att_s[:, 48:60].rearrange("p (t n) -> p t n", t=NT)
            lsum = att_s[:, 60:72].rearrange("p (t n) -> p t n", t=NT)

            def qk_squares():
                dve.wait_ge(qkv_copied, 4)
                dve.tensor_tensor(sq, qk, qk, ALU.mult)
                dve.drain()
                for t in range(NT):
                    dve.tensor_reduce(ss[:, t, :], sq[:, t, :].rearrange("p (n e) -> p n e", e=HD), AX.X, ALU.add)
                dve.drain()
                dve.tensor_scalar(ss, ss, 1.0 / HD, EPS, ALU.mult, ALU.add).then_inc(qk_mean, 1)

            def qk_normed():
                dve.wait_ge(qk_root, 1)
                dve.reciprocal(rs, rs)
                dve.drain()
                dve.tensor_scalar(rs[:, :, 0:HEADS], rs[:, :, 0:HEADS], HD ** -0.5, None, ALU.mult)
                dve.drain()
                for t in range(NT):
                    v3 = qk[:, t, :].rearrange("p (n e) -> p n e", e=HD)
                    last = dve.tensor_tensor(v3, v3, rs[:, t, :].unsqueeze(2).to_broadcast([P, NH2, HD]), ALU.mult)
                last.then_inc(qk_ready, 1)

            for d in range(DUOS):
                b = d % 2
                bu = psum[:, 4 + 2 * b:6 + 2 * b, :].rearrange("p i (c t) -> p i c t", c=2)
                rot = [x[:, 2 * d:2 * d + 2, :].unsqueeze(2).to_broadcast([P, 2, 2, SEQ]) for x in (cos_t, sin_t)]
                dve.wait_ge(table_ready, 2 * (d // 2) + 2)
                dve.wait_ge(bu_done, d + 1)
                if d >= 2:
                    dve.wait_ge(q_ready, d - 1)
                dve.tensor_tensor(zz[b], bu, rot[0], ALU.mult)
                dve.tensor_tensor(m2, bu, rot[1], ALU.mult).then_inc(bu_used, 1)
                dve.drain()
                dve.tensor_tensor(zz[b][:, :, 0, :], zz[b][:, :, 0, :], m2[:, :, 1, :], ALU.add)
                dve.tensor_tensor(zz[b][:, :, 1, :], zz[b][:, :, 1, :], m2[:, :, 0, :], ALU.subtract)
                dve.drain()
                if d == 0:
                    dve.wait_ge(r_ready, 1)
                for x in range(2):
                    i = 2 * d + x
                    for c in range(2):
                        last = dve.tensor_tensor_scan(zz[b][:, x, c, :], V["r"][:, i:i + 1].to_broadcast([P, SEQ]),
                                                      zz[b][:, x, c, :], 0.0, ALU.mult, ALU.add)
                last.then_inc(z_ready, 1)
                if d == 6:
                    qk_squares()
                if d == 7:
                    qk_normed()
                if d >= 3 and d % 2 == 1:
                    skip_added((d - 3) // 2)

            dve.wait_ge(ld_att, 32)
            for hh in range(HEADS):
                dve.wait_ge(score_done, hh + 1)
                dve.tensor_tensor(prob[:, hh, :], bank[hh % 2][:, 0:P + SEQ], prob[:, hh, :], ALU.add
                                  ).then_inc(score_copied, 1)
            dve.drain()
            cols = ((0, P), (P, P + SEQ))
            for t, (a, b) in enumerate(cols):
                dve.tensor_reduce(nmax[:, t, :], prob[:, :, a:b], AX.X, ALU.max)
            dve.drain()
            dve.tensor_scalar(nmax, nmax, -1.0, None, ALU.mult).then_inc(max_ready, 1)
            skip_added(CHW - 1)
            dve.wait_ge(exp_done, 2 * HEADS)
            dve.reciprocal(lsum, lsum)
            dve.drain()
            for t, (a, b) in enumerate(cols):
                last = dve.tensor_tensor(prob[:, :, a:b], prob[:, :, a:b],
                                         lsum[:, t, :].unsqueeze(2).to_broadcast([P, HEADS, b - a]), ALU.mult)
            last.then_inc(prob_ready, 1)
            for hh in range(HEADS):
                dve.wait_ge(pT_done, hh + 1)
                dve.tensor_copy(probT[:, hh, :], bank[hh % 3][:, 0:P + SEQ]).then_inc(pT_copied, 1)
            for m in range(CHW):
                dve.wait_ge(gate_ready, m + 1)
                dve.tensor_tensor(mixT[:, m, :], yT[:, m, :], glu[:, m, :], ALU.mult).then_inc(ssm_ready, 1)
            dve.wait_ge(pv_done, 1)
            dve.tensor_copy(mixT[:, 5:8, :], psum[:, 0:3, 0:SEQ]).then_inc(att_ready, 1)
            residual(1, out0_done, (2, 0))
            dve.wait_ge(ld_route, 48)
            route(0)
            experts(0)
            combined(0)

            dve.memset(zc, 0.0)
            dve.drain()
            for m in range(KD):
                b = m % 2
                dve.wait_ge(z_copied, m + 1)
                dve.tensor_tensor(zc[:, b, 2:], bank[4 + b][:, 0:SEQ], z_sb[:, b, :], ALU.mult)
                dve.drain()
                dve.tensor_scalar(cv[:, b, :], zc[:, b, 2:], conv_taps[:, m, 2:3], None, ALU.mult)
                dve.drain()
                for tap in (1, 0):
                    dve.scalar_tensor_tensor(out=cv[:, b, :], in0=zc[:, b, tap:tap + SEQ],
                                             scalar=conv_taps[:, m, tap:tap + 1], in1=cv[:, b, :],
                                             op0=ALU.mult, op1=ALU.add)
                    dve.drain()
                dve.wait_ge(b_done, m + 1)
                dve.tensor_tensor(mixT[:, m, :], cv[:, b, :], bank[6 + b][:, 0:SEQ], ALU.mult).then_inc(g_ready, 1)
            residual(3, out1_done, (0, 2))
            route(1)
            experts(1)
            combined(1)

        @block.scalar
        def _(act):
            def norm_tile(i, t):
                if i == 0:
                    act.wait_ge(ld_x[t], 16)
                else:
                    act.wait_ge(h_ready, NT * i + t - 1)
                act.activation(hn[:, t, :], h[:, t, :], ACT.Square, accum_out=norm_s[:, 0, t:t + 1])
                act.drain()
                act.nop().then_inc(squares, 1)
                act.wait_ge(mean, NT * i + t + 1)
                act.activation(norm_s[:, 2, t:t + 1], norm_s[:, 1, t:t + 1], ACT.Sqrt).then_inc(root, 1)

            def norm(i):
                if i > 0:
                    act.activation(norm_s[:, 2, :], norm_s[:, 1, :], ACT.Sqrt)
                    act.drain()
                for t in range(NT):
                    norm_tile(i, t)

            def route(l):
                s = RS
                act.wait_ge(s["gshift"], l + 1)
                act.activation(ge, ge, ACT.Exp).then_inc(s["gexp"], 1)
                act.wait_ge(s["eshift"], l + 1)
                act.activation(ex, ex, ACT.Exp).then_inc(s["eexp"], 1)

            def rows(S, n, b, lag):
                act.wait_ge(S["gather_done"], n + 1)
                before(act, S["xt_done"], n, lag)
                act.activation(xrow[b], bank[1][:, :], ACT.Copy).then_inc(S["xrow_ready"], 1)

            def silu(S, n, b, lag):
                act.wait_ge(S["gu_done"], n + 1)
                before(act, S["turn_done"], n, lag)
                act.activation(hid[b], bank[0][:, 0:256], ACT.Silu).then_inc(S["silu_ready"], 1)

            def hidden_turned(S, n, b, lag):
                act.wait_ge(S["turn_done"], n + 1)
                before(act, S["down_done"], n, lag)
                before(act, S["back_ready"], n, lag)
                act.activation(turned[b], bank[1][:, 0:258], ACT.Copy).then_inc(S["hidT_ready"], 1)

            def outputs(S, n, p, w, m, lag):
                act.wait_ge(S["down_done"], n + 1)
                before(act, S["acc_done"], m, lag)
                for half in range(2):
                    last = act.activation(y2[w][p:p + CAP, half * 512:(half + 1) * 512],
                                          bank[3][half * CAP:(half + 1) * CAP, :], ACT.Copy)
                last.then_inc(S["y_ready"], 1)

            def experts(l):
                S = ES[l]

                def step(n, v, i, m):
                    u, w = v % LAG, (v + 1) % LAG
                    silu(S, n, u, LAG)
                    if more(n):
                        rows(S, n + 1, w, LAG)
                    hidden_turned(S, n, u, LAG)
                    outputs(S, n, CAP * (v % 2), v // 2, m, LAG)
                rows(S, 0, 0, LAG)
                passes(act, step)
                O = OS[l]

                def body(m, e, r):
                    rows(O, m, 0, 1)
                    silu(O, m, 0, 1)
                    hidden_turned(O, m, 0, 1)
                    outputs(O, m, 0, OVER_B, m, 1)
                act.wait_ge(S["acc_done"], PAIRS_DONE)
                overflow(act, body)

            act.wait_ge(ld_p, 16)
            act.activation(sml[:, 0, :], ssm_p[:, 2, :], ACT.Exp).then_inc(expd, 1)
            act.wait_ge(lam_ready, 1)
            act.activation(sml[:, 4, :], sml[:, 1, :], ACT.Exp).then_inc(r_ready, 1)
            norm(0)
            half_pi = cst[:, C_HPI:C_HPI + 1]
            act.wait_ge(ld_const, 32)
            act.wait_ge(turn_ready, 1)
            act.activation(sml[:, 14, :], sml[:, 2, :], ACT.Abs)
            act.activation(sml[:, 15, :], sml[:, 2, :], ACT.Sin, scale=TURN)
            act.drain()
            act.activation(sml[:, 14, :], sml[:, 14, :], ACT.Sin, scale=-TURN, bias=half_pi).then_inc(pole_ready, 1)

            def tables(c):
                cs, sn = cos_t[:, 4 * c:4 * c + 4, :], sin_t[:, 4 * c:4 * c + 4, :]
                act.wait_ge(angle_ready, c + 1)
                act.activation(cs, sn, ACT.Abs)
                act.drain()
                act.activation(cs, cs, ACT.Sin, scale=-TURN, bias=half_pi).then_inc(table_ready, 1)
                act.activation(sn, sn, ACT.Sin, scale=-TURN).then_inc(table_ready, 1)

            def u_copy(m):
                act.wait_ge(u_done, m + 1)
                act.activation(uT[:, m, :], bank[m % 2][:, 0:SEQ], ACT.Copy).then_inc(u_copied, 1)

            def qkv_copy(j):
                act.wait_ge(qkv_done, j + 1)
                act.activation(qkv[:, j % 2, j // 2, :], bank[(1 + j) % 2][:, 0:ATT_W], ACT.Copy).then_inc(qkv_copied, 1)

            def gelu(c):
                act.wait_ge(ypre_ready, c + 1)
                act.activation(yT[:, c, :], ypre[:, c % 2, :], ACT.Gelu_apprx_tanh).then_inc(gelu_ready, 1)

            u_copy(0)
            tables(0)
            u_copy(1)
            tables(1)
            u_copy(2)
            tables(2)
            u_copy(3)
            tables(3)
            u_copy(4)
            tables(4)
            gelu(0)
            qkv_copy(0)
            qkv_copy(1)
            gelu(1)
            qkv_copy(2)
            qkv_copy(3)
            act.wait_ge(qk_mean, 1)
            act.activation(att_s[:, 24:48], att_s[:, 0:24], ACT.Sqrt).then_inc(qk_root, 1)
            gelu(2)
            qkv_copy(4)
            qkv_copy(5)
            act.wait_ge(ld_att, 32)
            for ch in range(2 * QCH):
                act.wait_ge(qkT_done, ch // 2 + 1)
                act.activation(qkT[:, ch, :], bank[(1 + ch // 2) % 2][:, (ch % 2) * SEQ:(ch % 2) * SEQ + SEQ],
                               ACT.Copy, scale=qk_gain[:, ch // QCH:ch // QCH + 1]).then_inc(qkT_copied, 1)
            gelu(3)
            gelu(4)
            act.wait_ge(max_ready, 1)
            for hh in range(HEADS):
                for t, (a, b) in enumerate(((0, P), (P, P + SEQ))):
                    n = t * HEADS + hh
                    act.activation(prob[:, hh, a:b], prob[:, hh, a:b], ACT.Exp, bias=att_s[:, 48 + n:49 + n],
                                   accum_out=att_s[:, 60 + n:61 + n]).then_inc(exp_done, 1)
            for m in range(CHW):
                act.wait_ge(glu_done, m + 1)
                act.activation(glu[:, m, :], bank[(4, 5, 6, 7, 3)[m]][:, 0:SEQ], ACT.Sigmoid, bias=d_bglu[:, 1, m:m + 1]
                               ).then_inc(gate_ready, 1)
            norm(1)
            route(0)
            experts(0)
            norm(2)
            for m in range(KD):
                act.wait_ge(cz_done, m + 1)
                if m >= 2:
                    act.wait_ge(g_ready, m - 1)
                act.activation(z_sb[:, m % 2, :], bank[4 + m % 2][:, SEQ:2 * SEQ], ACT.Copy).then_inc(z_copied, 1)
            norm(3)
            route(1)
            experts(1)

        @block.gpsimd
        def _(pool):
            pool.memset(zeros, 0.0).then_inc(zeros_ready, 1)
            pool.wait_ge(ab_ready, 1)
            for c in range(2, CHW):
                angle_sum(pool, c).then_inc(pool_added, 1)
            pool.wait_ge(factor_ready, 1)
            pool.wait_ge(ld_c, 32)
            cr, ci, nci = [sml[:, j, :].unsqueeze(2).to_broadcast([P, PAIRS, 32]) for j in (7, 8, 11)]
            pool.tensor_tensor(c_tmp[0], ssm_c[:, 0], cr, ALU.mult)
            pool.tensor_tensor(c_tmp[1], ssm_c[:, 1], ci, ALU.mult)
            pool.tensor_tensor(c_tmp[2], ssm_c[:, 0], nci, ALU.mult)
            pool.drain()
            pool.tensor_tensor(ssm_c[:, 0], c_tmp[0], c_tmp[1], ALU.subtract)
            pool.tensor_tensor(ssm_cb, c_tmp[1], c_tmp[0], ALU.subtract)
            pool.drain()
            pool.tensor_tensor(c_tmp[0], ssm_c[:, 1], cr, ALU.mult)
            pool.drain()
            pool.tensor_tensor(ssm_c[:, 1], c_tmp[2], c_tmp[0], ALU.subtract).then_inc(c_ready, 1)
            for d in range(DUOS):
                b = d % 2
                rot = [x[:, 2 * d:2 * d + 2, :].unsqueeze(2).to_broadcast([P, 2, 2, SEQ]) for x in (cos_t, sin_t)]
                pool.wait_ge(z_ready, d + 1)
                if d >= 2:
                    pool.wait_ge(y_done, d - 1)
                pool.tensor_tensor(qc[b], zz[b], rot[0], ALU.mult)
                pool.tensor_tensor(qs[b], zz[b], rot[1], ALU.mult).then_inc(q_ready, 1)


def constants(np):
    c = np.zeros((P, C_N), np.float32)
    r = np.arange(P)
    c[:, C_ID:C_ID + P] = np.eye(P)
    c[:, C_LT:C_LT + P] = r[:, None] < r[None, :]
    c[:, C_ONE:C_ONE + P] = 1.0
    c[:, C_IOTA:C_IOTA + SEQ] = np.arange(SEQ)
    c[:, C_E32:C_E32 + NE] = np.arange(NE)
    c[:, C_G32:C_G32 + NE] = np.arange(NE) // EPG
    c[:, C_TOK:C_TOK + NT] = r[:, None] + P * np.arange(NT)[None, :]
    c[:, C_I16:C_I16 + 16] = np.arange(16)
    c[:, C_HPI] = TURN / 4
    i, j = np.arange(SEQ)[:, None], np.arange(SEQ)[None, :]
    diff = i - j
    n = ((diff <= 128).astype(int) + (diff % 4 == 0) + (diff % 16 == 0)) * (diff >= 0)
    bias = np.zeros((P, HEADS, P + SEQ), np.float32)
    for hh in range(HEADS):
        slope = 2.0 ** (-8.0 * (hh + 1) / HEADS)
        full = np.where(n > 0, -slope * diff + np.log(np.maximum(n, 1)), NEG).astype(np.float32)
        bias[:, hh, 0:P] = full[0:P, 0:P]
        bias[:, hh, P:] = full[P:, :]
    return c, bias


def layout(np, I):
    pairs = lambda a: np.ascontiguousarray(a[0].reshape(PAIRS, P).T)
    step = np.repeat(np.asarray(I["ssm_log_step"])[0], 64).reshape(PAIRS, P).T
    ssm_p = np.stack([pairs(np.asarray(I["ssm_a_re"])), pairs(np.asarray(I["ssm_a_im"])), step], 1)
    ssm_b = np.zeros((4, 2, 16, 2, CHW, 2, 64), np.float32)
    ssm_c = np.zeros((2, 64, 2, PAIRS, 2, 16), np.float32)
    for z, (bn, cn) in enumerate((("ssm_b_re", "ssm_c_re"), ("ssm_b_im", "ssm_c_im"))):
        b = np.asarray(I[bn])[0].reshape(CHW, 4, 2, 64, 16)
        c = np.asarray(I[cn])[0].reshape(PAIRS, 2, 16, 64)
        for g in range(2):
            ssm_b[:, g, :, z, :, g, :] = b[:, :, g].transpose(1, 3, 0, 2)
            ssm_c[g, :, z, :, g, :] = c[:, g].transpose(2, 0, 1)
    gains = np.stack([np.asarray(I[n])[l].reshape(P, KD) for l in range(LAYERS) for n in ("norm_mix", "norm_ffn")], 1)
    w_router = np.stack([np.concatenate([np.asarray(I["w_router_group"])[l].reshape(P, KD, GROUPS),
                                         np.asarray(I["w_router_expert"])[l].reshape(P, KD, NE)], 2)
                         for l in range(LAYERS)], 1)
    b_router = np.concatenate([np.asarray(I["b_router_group"]), np.asarray(I["b_router_expert"])], 1)
    col = lambda a: np.asarray(a)[0].reshape(CHW, P).T
    cst, bias = constants(np)
    return {
        "ssm_p": ssm_p.reshape(P, 60), "ssm_b": ssm_b.reshape(P, 1280), "ssm_c": ssm_c.reshape(P, 1280),
        "gains": gains, "w_router": w_router, "b_router": np.tile(b_router[None], (P, 1, 1)),
        "d_bglu": np.stack([col(I["ssm_d"]), col(I["b_glu"])], 1),
        "conv_taps": np.asarray(I["conv_w"])[0].reshape(3, KD, P).transpose(2, 1, 0),
        "qk_gain": np.stack([np.tile(np.asarray(I[n])[0], P // HD) for n in ("q_norm", "k_norm")], 1),
        "cst": cst, "att_bias": bias,
    }


_BIG = ["x", "w_in_even", "w_glu", "w_out_even", "w_in_conv", "w_out_conv",
        "w_expert_gate", "w_expert_up", "w_expert_down"]


def kernel(**inputs):
    import numpy as np
    import concourse.bacc as bacc
    from concourse.bass_utils import run_bass_kernel_spmd

    nc = bacc.Bacc("TRN2", target_bir_lowering=False, num_devices=1)
    given = {n: np.ascontiguousarray(inputs[n]) for n in _BIG}
    given.update((n, np.ascontiguousarray(a)) for n, a in layout(np, inputs).items())
    arrays = {f"in_{n}": a for n, a in given.items()}
    A = {n: nc.dram_tensor(f"in_{n}", a.shape, F32, kind="ExternalInput").ap() for n, a in given.items()}
    out = nc.dram_tensor("out_0", (1, SEQ, D), F32, kind="ExternalOutput").ap()
    build(nc, A, out)
    r = run_bass_kernel_spmd(nc, [arrays], core_ids=[0])
    return r.results[0]["out_0"]
```
